# Optimizing a Trainium2 kernel written in Bass

```python
import math
import jax, jax.numpy as jnp
from jax import lax
import numpy as np

D_MODEL = 1024
BATCH = 1
SEQ = 256
DEPTH = 2

GRID_W = 64
CTX_LEN = 256
N_MIXERS = 2
EPS = 1e-6

HY_SHORT_K = 3
HY_EMB_BANDS = 16
HY_EMB_DIM = 1 + 2 * HY_EMB_BANDS
HY_FILTER_HIDDEN = 64
HY_INNER_MLPS = 2
HY_DECAY_TARGET = 1e-2
HY_FAST_DECAY_PCT = 0.3
HY_SLOW_DECAY_PCT = 1.5

MLA_HEADS = D_MODEL // 128
MLA_NOPE = 128
MLA_ROPE = 64
MLA_QK = MLA_NOPE + MLA_ROPE
MLA_V = 128
MLA_Q_LORA = 384
MLA_KV_LORA = 256
ROPE_BASE = 10000.0
Q_BLOCK = 128
SOFTMAX_SCALE = MLA_QK ** -0.5

N_EXPERTS = 16
N_GROUPS = 4
EXPERTS_PER_GROUP = N_EXPERTS // N_GROUPS
TOPK_GROUPS = 1
TOP_K = 2
D_EXPERT = 512
D_SHARED = 512

kernel_name = "hybrid_hyena_mla_grouped_moe_dit"

F32 = jnp.float32

def rmsnorm(x, g):
    xf = x.astype(F32)
    y = xf * lax.rsqrt(jnp.mean(xf * xf, axis=-1, keepdims=True) + EPS)
    return (y * g.astype(F32)).astype(x.dtype)

def modulate(h, shift, scale):
    return h * (1.0 + scale) + shift

def short_conv3(u, w, b):
    up = jnp.pad(u, ((0, 0), (1, 1), (0, 0)))
    return up[:, :-2] * w[0] + up[:, 1:-1] * w[1] + up[:, 2:] * w[2] + b

def hyena_filter(L, w1, b1, w2, b2, w3, freq):
    t_norm = jnp.linspace(0.0, 1.0, L, dtype=F32)[:, None]
    pos = jnp.arange(L, dtype=F32)[:, None]
    bands = jnp.linspace(1e-4, HY_EMB_BANDS - 1, HY_EMB_BANDS, dtype=F32)[None, :]
    ang = 2.0 * math.pi * bands * pos / L
    z = jnp.concatenate([t_norm, jnp.cos(ang), -jnp.sin(ang)], axis=-1)
    fr = freq.astype(F32)
    h = jnp.sin(fr * (z @ w1.astype(F32) + b1.astype(F32)))
    for m in range(HY_INNER_MLPS):
        h = jnp.sin(fr * (h @ w2[m].astype(F32) + b2[m].astype(F32)))
    h = (h @ w3.astype(F32)).reshape(L, 2, D_MODEL)
    max_decay = math.log(HY_DECAY_TARGET) / HY_FAST_DECAY_PCT
    min_decay = math.log(HY_DECAY_TARGET) / HY_SLOW_DECAY_PCT
    deltas = jnp.linspace(min_decay, max_decay, D_MODEL, dtype=F32)
    decay = jnp.exp(-t_norm * jnp.abs(deltas))
    h = h * decay[:, None, :]
    h_fwd, h_bwd = h[:, 0], h[:, 1]
    k = jnp.concatenate([h_fwd, jnp.zeros((1, D_MODEL), F32), h_bwd[1:][::-1]], axis=0)
    return k / jnp.sum(jnp.abs(k), axis=0, keepdims=True)

def hyena_mixer(u, in_w, in_b, conv_w, conv_b, fw1, fb1, fw2, fb2, fw3, freq, f_bias, out_w, out_b):
    L = u.shape[1]
    z = short_conv3(u @ in_w + in_b, conv_w, conv_b)
    x0, x1, v = jnp.split(z, 3, axis=-1)
    k = hyena_filter(L, fw1, fb1, fw2, fb2, fw3, freq)
    vg = (v * x1).astype(F32)
    n = 2 * L
    y = jnp.fft.irfft(jnp.fft.rfft(vg, n=n, axis=1) * jnp.fft.rfft(k, n=n, axis=0)[None], n=n, axis=1)[:, :L]
    y = y + vg * f_bias.astype(F32)
    y = (x0.astype(F32) * y).astype(u.dtype)
    return y @ out_w + out_b

def axial_rope_angles(L):
    rows = L // GRID_W
    t_row = jnp.repeat(jnp.arange(rows, dtype=F32), GRID_W)
    t_col = jnp.tile(jnp.arange(GRID_W, dtype=F32), rows)
    half = MLA_ROPE // 2
    inv = ROPE_BASE ** (-jnp.arange(0, half, 2, dtype=F32) / half)
    return t_row[:, None] * inv, t_col[:, None] * inv

def rope_1d(x, ang):
    cos = jnp.cos(ang)[None, :, None, :].astype(x.dtype)
    sin = jnp.sin(ang)[None, :, None, :].astype(x.dtype)
    x1, x2 = jnp.split(x, 2, axis=-1)
    return jnp.concatenate([x1 * cos - x2 * sin, x2 * cos + x1 * sin], axis=-1)

def apply_axial_rope(t, angles):
    ang_row, ang_col = angles
    t_nope, t_rope = t[..., :MLA_NOPE], t[..., MLA_NOPE:]
    r_row, r_col = jnp.split(t_rope, 2, axis=-1)
    return jnp.concatenate([t_nope, rope_1d(r_row, ang_row), rope_1d(r_col, ang_col)], axis=-1)

def mla_queries(h, wq_down, q_norm_g, wq_up, q_head_g, angles):
    B, L, _ = h.shape
    q = (rmsnorm(h @ wq_down, q_norm_g) @ wq_up).reshape(B, L, MLA_HEADS, MLA_QK)
    q = rmsnorm(q, q_head_g)
    return q if angles is None else apply_axial_rope(q, angles)

def mla_keys_values(h, wkv_down, kv_norm_g, wkv_up, k_head_g, angles):
    B, L, _ = h.shape
    kv = h @ wkv_down
    c_kv, k_pe = kv[..., :MLA_KV_LORA], kv[..., MLA_KV_LORA:]
    kvu = (rmsnorm(c_kv, kv_norm_g) @ wkv_up).reshape(B, L, MLA_HEADS, MLA_NOPE + MLA_V)
    k_nope, v = kvu[..., :MLA_NOPE], kvu[..., MLA_NOPE:]
    k_pe = jnp.broadcast_to(k_pe[:, :, None, :], (B, L, MLA_HEADS, MLA_ROPE))
    k = rmsnorm(jnp.concatenate([k_nope, k_pe], axis=-1), k_head_g)
    k = k if angles is None else apply_axial_rope(k, angles)
    return k, v

def attend(q, k, v):
    s = jnp.einsum('bqhd,bkhd->bhqk', q, k, preferred_element_type=F32) * SOFTMAX_SCALE
    p = jax.nn.softmax(s, axis=-1).astype(v.dtype)
    return jnp.einsum('bhqk,bkhd->bqhd', p, v)

def mla_mixer(h, hc, wq_down, q_norm_g, wq_up, wkv_down, kv_norm_g, wkv_up, q_head_g, k_head_g, wo, need_ctx):
    B, L, _ = h.shape
    angles = axial_rope_angles(L)
    q = mla_queries(h, wq_down, q_norm_g, wq_up, q_head_g, angles)
    k, v = mla_keys_values(h, wkv_down, kv_norm_g, wkv_up, k_head_g, angles)
    kc, vc = mla_keys_values(hc, wkv_down, kv_norm_g, wkv_up, k_head_g, None)
    k_all = jnp.concatenate([k, kc], axis=1)
    v_all = jnp.concatenate([v, vc], axis=1)
    nb = L // Q_BLOCK
    qb = jnp.moveaxis(q.reshape(B, nb, Q_BLOCK, MLA_HEADS, MLA_QK), 1, 0)
    ob = lax.map(lambda qq: attend(qq, k_all, v_all), qb)
    y = jnp.moveaxis(ob, 0, 1).reshape(B, L, MLA_HEADS * MLA_V) @ wo
    if not need_ctx:
        return y, None
    qc = mla_queries(hc, wq_down, q_norm_g, wq_up, q_head_g, None)
    Bc, Lc, _ = hc.shape
    yc = attend(qc, kc, vc).reshape(Bc, Lc, MLA_HEADS * MLA_V) @ wo
    return y, yc

def swiglu(h, w1, w3, w2):
    return (jax.nn.silu(h @ w1) * (h @ w3)) @ w2

def grouped_moe(h, router_w, router_bias, w1, w3, w2, sw1, sw3, sw2):
    N = h.shape[0]
    s = jax.nn.sigmoid(jnp.dot(h, router_w, preferred_element_type=F32))
    sb = (s + router_bias.astype(F32)).reshape(N, N_GROUPS, EXPERTS_PER_GROUP)
    group_score = jnp.sum(lax.top_k(sb, TOP_K)[0], axis=-1)
    _, g_sel = lax.top_k(group_score, TOPK_GROUPS)
    g_mask = jnp.any(g_sel[:, :, None] == jnp.arange(N_GROUPS)[None, None, :], axis=1)
    sb = jnp.where(g_mask[:, :, None], sb, -jnp.inf).reshape(N, N_EXPERTS)
    _, e_sel = lax.top_k(sb, TOP_K)
    w = jnp.take_along_axis(s, e_sel, axis=-1)
    w = w / jnp.sum(w, axis=-1, keepdims=True)
    gates = jnp.sum(jax.nn.one_hot(e_sel, N_EXPERTS, dtype=F32) * w[..., None], axis=1).astype(h.dtype)
    out = swiglu(h, sw1, sw3, sw2)
    for e in range(N_EXPERTS):
        out = out + gates[:, e:e + 1] * swiglu(h, w1[e], w3[e], w2[e])
    return out

def setup_inputs(seed: int = 0) -> dict:
    key = jax.random.key(seed)
    ks = iter(jax.random.split(key, 48))

    def nrm(shape, scale):
        return scale * jax.random.normal(next(ks), shape, F32)

    def gain(shape):
        return 1.0 + 0.1 * jax.random.normal(next(ks), shape, F32)

    D = D_MODEL
    nh = (DEPTH + 1) // 2
    nm = DEPTH // 2
    H, HID = MLA_HEADS, HY_FILTER_HIDDEN
    return {
        "x": nrm((BATCH, SEQ, D), 1.0),
        "c": nrm((BATCH, D), 1.0),
        "ctx": nrm((BATCH, CTX_LEN, D), 1.0),
        "c_ctx": nrm((D,), 1.0),
        "ada_w": nrm((DEPTH, D, 6 * D), 0.5 * D ** -0.5),
        "ada_b": nrm((DEPTH, 6 * D), 0.02),
        "norm_mix_g": gain((DEPTH, D)),
        "norm_ffn_g": gain((DEPTH, D)),
        "hy_in_w": nrm((nh, D, 3 * D), D ** -0.5),
        "hy_in_b": nrm((nh, 3 * D), 0.02),
        "hy_conv_w": nrm((nh, HY_SHORT_K, 3 * D), HY_SHORT_K ** -0.5),
        "hy_conv_b": nrm((nh, 3 * D), 0.02),
        "hy_f_w1": nrm((nh, HY_EMB_DIM, HID), HY_EMB_DIM ** -0.5),
        "hy_f_b1": nrm((nh, HID), 0.1),
        "hy_f_w2": nrm((nh, HY_INNER_MLPS, HID, HID), HID ** -0.5),
        "hy_f_b2": nrm((nh, HY_INNER_MLPS, HID), 0.1),
        "hy_f_w3": nrm((nh, HID, 2 * D), HID ** -0.5),
        "hy_sin_freq": gain((nh, HID)),
        "hy_f_bias": nrm((nh, D), 0.1),
        "hy_out_w": nrm((nh, D, D), D ** -0.5),
        "hy_out_b": nrm((nh, D), 0.02),
        "mla_wq_down": nrm((nm, D, MLA_Q_LORA), D ** -0.5),
        "mla_q_norm_g": gain((nm, MLA_Q_LORA)),
        "mla_wq_up": nrm((nm, MLA_Q_LORA, H * MLA_QK), MLA_Q_LORA ** -0.5),
        "mla_wkv_down": nrm((nm, D, MLA_KV_LORA + MLA_ROPE), D ** -0.5),
        "mla_kv_norm_g": gain((nm, MLA_KV_LORA)),
        "mla_wkv_up": nrm((nm, MLA_KV_LORA, H * (MLA_NOPE + MLA_V)), MLA_KV_LORA ** -0.5),
        "mla_q_head_g": gain((nm, MLA_QK)),
        "mla_k_head_g": gain((nm, MLA_QK)),
        "mla_wo": nrm((nm, H * MLA_V, D), (H * MLA_V) ** -0.5),
        "router_w": nrm((D, N_EXPERTS), D ** -0.5),
        "router_bias": nrm((N_EXPERTS,), 0.01),
        "exp_w1": nrm((DEPTH, N_EXPERTS, D, D_EXPERT), D ** -0.5),
        "exp_w3": nrm((DEPTH, N_EXPERTS, D, D_EXPERT), D ** -0.5),
        "exp_w2": nrm((DEPTH, N_EXPERTS, D_EXPERT, D), D_EXPERT ** -0.5),
        "sh_w1": nrm((DEPTH, D, D_SHARED), D ** -0.5),
        "sh_w3": nrm((DEPTH, D, D_SHARED), D ** -0.5),
        "sh_w2": nrm((DEPTH, D_SHARED, D), D_SHARED ** -0.5),
    }

def reference(x, c, ctx, c_ctx, ada_w, ada_b, norm_mix_g, norm_ffn_g,
              hy_in_w, hy_in_b, hy_conv_w, hy_conv_b, hy_f_w1, hy_f_b1, hy_f_w2, hy_f_b2, hy_f_w3,
              hy_sin_freq, hy_f_bias, hy_out_w, hy_out_b,
              mla_wq_down, mla_q_norm_g, mla_wq_up, mla_wkv_down, mla_kv_norm_g, mla_wkv_up,
              mla_q_head_g, mla_k_head_g, mla_wo,
              router_w, router_bias, exp_w1, exp_w3, exp_w2, sh_w1, sh_w3, sh_w2):
    D = D_MODEL
    xc = ctx
    silu_c = jax.nn.silu(c)
    silu_cc = jax.nn.silu(c_ctx)
    for i in range(DEPTH):
        need_ctx = i < DEPTH - 1
        j = i // N_MIXERS
        mod = (silu_c @ ada_w[i] + ada_b[i])[:, None, :]
        mod_c = silu_cc @ ada_w[i] + ada_b[i]
        sh1, sc1, g1, sh2, sc2, g2 = jnp.split(mod, 6, axis=-1)
        sh1c, sc1c, g1c, sh2c, sc2c, g2c = jnp.split(mod_c, 6, axis=-1)
        h = modulate(rmsnorm(x, norm_mix_g[i]), sh1, sc1)
        hc = modulate(rmsnorm(xc, norm_mix_g[i]), sh1c, sc1c)
        if i % N_MIXERS == 0:
            hp = (hy_in_w[j], hy_in_b[j], hy_conv_w[j], hy_conv_b[j], hy_f_w1[j], hy_f_b1[j],
                  hy_f_w2[j], hy_f_b2[j], hy_f_w3[j], hy_sin_freq[j], hy_f_bias[j], hy_out_w[j], hy_out_b[j])
            y = hyena_mixer(h, *hp)
            yc = hyena_mixer(hc, *hp) if need_ctx else None
        else:
            y, yc = mla_mixer(h, hc, mla_wq_down[j], mla_q_norm_g[j], mla_wq_up[j], mla_wkv_down[j],
                              mla_kv_norm_g[j], mla_wkv_up[j], mla_q_head_g[j], mla_k_head_g[j], mla_wo[j],
                              need_ctx)
        x = x + g1 * y
        h2 = modulate(rmsnorm(x, norm_ffn_g[i]), sh2, sc2)
        ep = (router_w, router_bias, exp_w1[i], exp_w3[i], exp_w2[i], sh_w1[i], sh_w3[i], sh_w2[i])
        if need_ctx:
            xc = xc + g1c * yc
            h2c = modulate(rmsnorm(xc, norm_ffn_g[i]), sh2c, sc2c)
            n_lat = h2.shape[0] * h2.shape[1]
            f = grouped_moe(jnp.concatenate([h2.reshape(-1, D), h2c.reshape(-1, D)], axis=0), *ep)
            x = x + g2 * f[:n_lat].reshape(x.shape)
            xc = xc + g2c * f[n_lat:].reshape(xc.shape)
        else:
            x = x + g2 * grouped_moe(h2.reshape(-1, D), *ep).reshape(x.shape)
    return x


_drawn_inputs = setup_inputs


def setup_inputs(seed=0):
    import zlib

    import numpy as np

    out = dict(_drawn_inputs(seed))
    spreads = {}
    factors = {'hy_in_b': 4.927,
     'hy_conv_b': 4.358,
     'hy_f_b1': 3.0,
     'hy_sin_freq': 4.255,
     'hy_out_b': 3.83,
     'mla_q_norm_g': 8.0,
     'mla_kv_norm_g': 3.552,
     'mla_q_head_g': 3.857,
     'mla_k_head_g': 4.637}
    for name, (base, spread) in spreads.items():
        noise = np.random.default_rng([zlib.crc32(name.encode()), seed]).standard_normal(out[name].shape)
        drawn = base * np.exp(spread * noise) if base else spread * noise
        out[name] = __import__('jax').numpy.asarray(drawn.astype(out[name].dtype))
    for name, factor in factors.items():
        out[name] = (out[name] * factor).astype(out[name].dtype)
    return out
```

```python
from contextlib import ExitStack

import numpy as np
import concourse.bass as bass
from concourse import mybir

ACT = mybir.ActivationFunctionType
ALU = mybir.AluOpType
AX = mybir.AxisListType
F32 = mybir.dt.float32
I32 = mybir.dt.int32

P = 128
D = 1024
DC = D // P
SEQ = 256
TILES = 2 * SEQ // P
LAT_TILES = SEQ // P
DEPTH = 2
EPS = 1e-6
N_MOD = 6
SHIFT1, SCALE1, GATE1, SHIFT2, SCALE2, GATE2 = range(N_MOD)

HID = 64
EMB = 33
BANDS = 16
TWO_PI_HI = 6.28125
TWO_PI_LO = 2.0 * np.pi - TWO_PI_HI
ROUND = 1.5 * 2.0 ** 23

H = 8
NOPE, ROPE, QK, VD = 128, 64, 192, 128
Q_LORA, KV_LORA = 384, 256
SM_SCALE = QK ** -0.5

E, G, PER_G = 16, 4, 4
FF = 512
FC = FF // P
TOP_K = 2


def expert_tiles(tokens):
    return (tokens * TOP_K - E) // P + E


TOKEN_TILES = [TILES, LAT_TILES]
EXPERT_TILES = [expert_tiles(t * P) for t in TOKEN_TILES]
T_MAX = max(EXPERT_TILES)

SLOTS = 6
SLOT_W = 4096
BIG = 1.0e30

C_IDENT, C_UPPER, C_ONES, C_IOTA = 0, 128, 256, 384
C_GRID = 512
C_TILE = C_GRID + T_MAX + 1
C_DESC = C_TILE + T_MAX + 1
C_DESC4 = C_DESC + E
C_TOK = C_DESC4 + G
C_ROPE = C_TOK + TILES
C_END = C_ROPE + LAT_TILES * 64


def shape_constants():
    f = np.float32
    small = np.zeros((P, C_END), f)
    small[:, C_IDENT:C_IDENT + P] = np.eye(P)
    small[:, C_UPPER:C_UPPER + P] = np.triu(np.ones((P, P)), 1)
    small[:, C_ONES:C_ONES + P] = 1
    small[:, C_IOTA:C_IOTA + P] = np.arange(P)
    small[:, C_GRID:C_GRID + T_MAX + 1] = P * np.arange(T_MAX + 1)
    small[:, C_TILE:C_TILE + T_MAX + 1] = np.arange(T_MAX + 1)
    small[:, C_DESC:C_DESC + E] = E - np.arange(E)
    small[:, C_DESC4:C_DESC4 + G] = G - np.arange(G)
    small[:, C_TOK:C_TOK + TILES] = np.arange(P)[:, None] + P * np.arange(TILES)[None]
    grid_w, half = 64, ROPE // 2
    inv = (f(10000.0) ** (-np.arange(0, half, 2, dtype=f) / f(half))).astype(f)
    tok = np.arange(SEQ)
    ang = np.stack([(tok // grid_w).astype(f)[:, None] * inv, (tok % grid_w).astype(f)[:, None] * inv], 1)
    for t in range(LAT_TILES):
        a = ang[t * P:(t + 1) * P].reshape(P, 32)
        small[:, C_ROPE + 64 * t:C_ROPE + 64 * t + 32] = np.cos(a)
        small[:, C_ROPE + 64 * t + 32:C_ROPE + 64 * t + 64] = np.sin(a)
    w = np.pi * np.outer(np.arange(SEQ), 2 * np.arange(SEQ) + 1) / (2.0 * SEQ)
    fwd = np.concatenate([np.cos(w), -np.sin(w)], 1).reshape(2, P, 2 * SEQ).transpose(1, 0, 2)
    inv_t = np.concatenate([np.cos(w.T), -np.sin(w.T)], 0).reshape(4, P, SEQ).transpose(1, 0, 2) / SEQ
    dft = np.concatenate([fwd.reshape(P, -1), inv_t.reshape(P, -1)], 1).astype(f)
    t_norm = np.linspace(0.0, 1.0, SEQ, dtype=f)[:, None]
    bands = np.linspace(1e-4, BANDS - 1, BANDS, dtype=f)[None]
    a = (f(2.0 * np.pi) * bands * np.arange(SEQ, dtype=f)[:, None] / f(SEQ)).astype(f)
    pos = np.ascontiguousarray(np.concatenate([t_norm, np.cos(a), -np.sin(a)], 1).T.astype(f))
    lo, hi = np.log(1e-2) / 1.5, np.log(1e-2) / 0.3
    deltas = np.linspace(lo, hi, D, dtype=f)
    decay = np.exp(-t_norm * np.abs(deltas)).astype(f)
    return {"c_small": small, "c_dft": dft, "c_pos": pos, "c_decay": decay}


class Link:

    def __init__(self, eng, sem):
        self.eng, self.sem, self.n, self.off = eng, sem, 0, 0

    def __call__(self, ins):
        self.n += 1
        ins.then_inc(self.sem, 1)
        self.eng.wait_ge(self.sem, self.off + self.n)

    def enter(self, i, per):
        self.at, self.per, self.off = self.n, per, i * per

    def leave(self, iterations):
        assert self.n == self.at + self.per, (self.n - self.at, self.per)
        self.n, self.off = self.at + self.per * iterations, 0


def build(nc, a, out, dbg=None):
    with ExitStack() as ctx:
        def sb(name, words, dt=F32):
            return ctx.enter_context(nc.sbuf_tensor(name, [P, words], dt))

        def sem(name):
            return ctx.enter_context(nc.semaphore(name))

        def dram(name, shape):
            return nc.dram_tensor(name, shape, F32, kind="Internal").ap()

        mod_d = dram("mod_rows", [DEPTH, 2, N_MOD * D])
        h2_d = [dram(f"h2_{l}", [TOKEN_TILES[l] * P, D]) for l in range(DEPTH)]
        y_d = [dram(f"expert_out_{l}", [EXPERT_TILES[l] * P, D]) for l in range(DEPTH)]

        ring = sb("weight_ring", SLOTS * SLOT_W)
        Xt = sb("residual", TILES * D)
        blk = sb("blocks", 5 * 4096)
        dft_t = sb("dft", 2048)
        cst = sb("small_constants", C_END)
        misc = sb("short_rows", 608)
        small = sb("small_values", 560)
        ints = sb("int_values", 2 * T_MAX + 2 * TILES + 2, I32)
        psum = ctx.enter_context(nc.psum_tensor("psum", [P, 8, 512], F32))

        def slot(s, words=SLOT_W):
            return ring[:, s * SLOT_W:s * SLOT_W + words]

        def B(block, at, words):
            return blk[:, block * 4096 + at:block * 4096 + at + words]

        def C(at, words):
            return cst[:, at:at + words]

        small_at = [0]

        def sm(words):
            at = small_at[0]
            small_at[0] += words
            assert small_at[0] <= 560
            return small[:, at:at + words]

        X = Xt[:, :].rearrange("p (t d) -> p t d", d=D)
        ident = C(C_IDENT, P)
        dft_fwd = dft_t[:, 0:1024].rearrange("p (t f) -> p t f", t=2)
        dft_inv = dft_t[:, 1024:2048].rearrange("p (k t) -> p k t", k=4)

        cT = sm(16)
        scT = sm(16).rearrange("p (c s) -> p c s", s=2)
        ssq, var, std, rstd = sm(8), sm(8), sm(8), sm(8)
        hy_par = sm(120)
        pm = [sm(15), sm(15)]
        router_b = sm(E)
        sel_a, sel_b = sm(TILES * E), sm(TILES * E)
        gates = sm(2 * TILES)
        cnt16 = sm(E)
        scan = [sm(2 * E), sm(2 * E)]
        lat_g = sm(5)
        idx_i = ints[:, 0:T_MAX]
        eid_i = ints[:, T_MAX:2 * T_MAX]
        slot_i = ints[:, 2 * T_MAX:2 * T_MAX + 2 * TILES]
        idx_cur = ints[:, 2 * T_MAX + 2 * TILES:2 * T_MAX + 2 * TILES + 2]

        def bc(ap, axis, n):
            u = ap.unsqueeze(axis)
            shape = list(u.shape)
            shape[axis] = n
            return u.broadcast_to(shape)

        def bank(k, words=512, parts=P):
            return psum[0:parts, k, 0:words]

        def banks(k, n):
            return psum[:, k:k + n, :].rearrange("p b n -> p (b n)")

        w_loaded = [sem(f"w_loaded{s}") for s in range(SLOTS)]
        w_loaded_in = [sem(f"w_loaded_in{u}") for u in range(2)]
        w_used = [sem(f"w_used{s}") for s in range(SLOTS)]
        names = """phase link_dve link_act link_pool ld_const ld_cond ld_x ld_hy ld_filt ld_adab ld_rows ld_rows2 ld_lat
            silu_c hy_turned f_pre f_arg f_sin f_w3 f_h f_abs f_norm f_sd f_k f_kdone
            ada_done modT_ready mod_turned modr_ready mod_stored
            n_ssq n_var n_std n_h n_T n_hT n_st0 n_st1 g_rows
            ip_pm ip_z ip_u ip_c ip_vg ip_vt ip_ve
            cv_x cv_y cv_xfree cv_inv cv_yt op_y op_x
            l_down l_ssq l_var l_std l_lat l_T l_TT l_up l_hssq l_hvar l_hstd l_hn l_v l_hr l_HT l_hevac
            a_s a_m a_p a_pn a_pT a_PT a_o a_ot out_st""".split()
        S = {n: sem(n) for n in names}
        moe_names = "logits aff sel pos hot idxp idx eid h13 silu hid hT hidT y yev xT xTe xg0 xg1 cur yst ga0 ga1 comb ld rw go".split()
        M = [{n: sem(f"{n}_{l}") for n in moe_names} for l in range(DEPTH)]

        loads, landed = [0] * SLOTS, [0] * SLOTS
        W, LANDED = {}, {}

        def book(name, s, times=1, own_sem=False):
            W[name], LANDED[name] = (s, loads[s]), landed[s]
            loads[s] += times
            landed[s] += 0 if own_sem else times

        for u in range(6):
            book(f"ada0_{u}", u, 2)
        for u in range(2):
            book(f"hy_in_{u}", u, 4, True)
            book(f"ada1_{u}", 2 + u, 4)
        for k, s in enumerate((4, 5, 2, 3)):
            book(f"ada1_tail{k}", s)
        book("hy_out0", 0)
        book("hy_out1", 1)

        def book_moe(l):
            for w, s in ((1, 4), (3, 5), (2, 3)):
                book(f"sh{w}_{l}", s)
            for j in range(EXPERT_TILES[l]):
                for k, w in enumerate((1, 3, 2)):
                    book(f"e{w}_{l}_{j}", 3 * (j % 2) + k)

        book_moe(0)
        for name, s in (("wqd", 3), ("wkvd", 4), ("wkvu", 5), ("wqu0", 0), ("wqu1", 1), ("wo0", 2), ("wo1", 3)):
            book(name, s)
        book_moe(1)

        def wait_piece(pe, name, i=0):
            pe.wait_ge(w_loaded[W[name][0]], 16 * (LANDED[name] + 1) + 16 * i)

        def piece(name, words=SLOT_W):
            return slot(W[name][0], words)

        def freed(ins, name):
            ins.then_inc(w_used[W[name][0]], 1)

        LOOP_AT = 2
        LOOPED = [t - 3 for t in EXPERT_TILES]

        def norm_places(k):
            if k == 0:
                return B(1, 0, 4096), B(2, 0, 1024), B(2, 1024, 1024), B(3, 0, 2048)
            if k == 1:
                return B(4, 0, 4096), B(2, 0, 1024), B(2, 1024, 1024), B(2, 2048, 2048)
            return B(1, 0, 4096), B(2, 0, 1024), B(2, 1024, 1024), B(2, 2048, 2048)

        NORM_TILES = [4, 4, 4, 2]
        NORM_BASE = [0, 4, 8, 12]
        hT = B(0, 0, 4096).rearrange("p (c t) -> p c t", c=DC)

        adab = [misc[:, 128 * l:128 * (l + 1)] for l in range(DEPTH)]
        hy_rows, modT, mod_r = misc[:, 256:384], misc[:, 384:480], misc[:, 480:608]
        f_rn, f_bias = B(0, 0, D), B(0, D, D)
        f_pos, f_arg, f_n = (B(0, 2 * D + 256 * k, 256) for k in range(3))
        f_h = [B(0, 2 * D + 256 * (3 + k), 256) for k in range(3)]
        f_w1, f_par = B(0, 3584, HID), B(0, 3584 + 3 * HID, 4)
        f_w2 = [B(0, 3584 + HID * (1 + k), HID) for k in range(2)]
        f_hfb = B(1, 0, 4096).rearrange("p (t n) -> p t n", t=2)
        f_mag = B(2, 0, 4096).rearrange("p (t n) -> p t n", t=2)
        f_sd = B(2, 0, 4096).rearrange("p (k t n) -> p k t n", k=2, t=2)
        f_decay = B(3, 0, 2048).rearrange("p (t n) -> p t n", t=2)
        f_w3 = B(3, 2048, 2048)
        f_K = B(4, 0, 4096).rearrange("p (k n) -> p k n", k=4)
        N_FILT = 12
        x0T = B(1, 0, 4096).rearrange("p (m t) -> p m t", m=8)
        vgtok = B(2, 0, 4096).rearrange("p (t d) -> p t d", d=D)
        ip_u = B(3, 0, 1548).rearrange("p (o s t) -> p o s t", o=3, s=2)
        ip_t = B(3, 1548, 1536).rearrange("p (o s t) -> p o s t", o=3, s=2)
        ip_vgb = B(3, 3084, 512)
        cv_Y = B(0, 0, 4096).rearrange("p (k f n) -> p k f n", k=2, f=4)
        cv_t = B(3, 3072, 1024).rearrange("p (k n) -> p k n", k=2)
        op_rows = B(3, 0, 3072).rearrange("p (k n) -> p k n", k=3)
        op_t = B(0, 0, 1024).rearrange("p (k n) -> p k n", k=2)
        moe_S = B(1, 0, 4096).rearrange("p (t d) -> p t d", d=D)
        moe_xg = [B(2, b * D, D) for b in range(2)]
        moe_xT = [B(2, (2 + b) * D, D).rearrange("p (c n) -> p c n", c=DC) for b in range(2)]
        moe_hid = [B(3, b * FF, FF) for b in range(2)]
        moe_hidT = [B(3, (2 + b) * FF, FF).rearrange("p (c n) -> p c n", c=FC) for b in range(2)]
        moe_y = B(3, 2048, D)
        moe_rw = B(3, 3072, 128).rearrange("p (c e) -> p c e", c=DC)
        moe_aff = B(3, 3200, 64)
        moe_sel = B(3, 3264, 64).rearrange("p (t e) -> p t e", e=E)
        moe_g2 = B(4, 0, 2048).rearrange("p (s d) -> p s d", s=2)
        moe_hot = B(4, 2048, 1024).rearrange("p (q n) -> p q n", q=2 * TILES)
        moe_hit = B(4, 3072, 2 * TILES * (T_MAX + 1)).rearrange("p (q t) -> p q t", t=T_MAX + 1)
        moe_cmp = B(4, 3264, 384)
        moe_r = [B(4, 3648 + 64 * k, 64) for k in range(3)]
        moe_pair = B(4, 3840, 96).rearrange("p (g s) -> p g s", s=6)
        moe_g4 = [B(4, 3936 + 16 * k, 16) for k in range(3)]
        moe_slot = B(4, 3984, 4 * TILES)
        moe_gat = B(0, 0, 4096).rearrange("p (b k d) -> p b k d", b=2, k=2)
        a_V = B(1, 0, 4096).rearrange("p (t d) -> p t d", d=D)
        kTn = B(2, 0, 4096).rearrange("p (h t) -> p h t", h=H)
        kTr = B(3, 0, 2048).rearrange("p (h t) -> p h t", h=H // 2)
        qTn = B(3, 2048, 2048).rearrange("p (h t) -> p h t", h=H)
        qTr = B(4, 0, 1024).rearrange("p (h t) -> p h t", h=H // 2)
        mla_hn = B(4, 1024, H * NOPE).rearrange("p (h d) -> p h d", h=H)
        mla_hr = B(4, 2048, H * ROPE).rearrange("p (h d) -> p h d", h=H)
        mla_t, mla_sq = B(4, 2560, 1024), B(4, 3584, 384)
        mla_lat, mla_latT = dft_t[:, 0:384], dft_t[:, 384:768].rearrange("p (c n) -> p c n", c=3)
        mla_g, mla_pe = dft_t[:, 768:768 + 2 * QK], dft_t[:, 1152:1152 + ROPE]
        o_gate = dft_t[:, 768:1792]
        hssq, hvar, hstd, hrstd = (dft_t[:, 1792 + 8 * k:1800 + 8 * k] for k in range(4))
        a_nm, a_sum = dft_t[:, 1824:1828], dft_t[:, 1828:1832]
        OT = B(0, 0, 2048).rearrange("p (h t) -> p h t", h=H)
        a_PT = B(0, 2048, 2048).rearrange("p (b k t) -> p b k t", b=2, k=4)
        a_P = B(4, 1024, 2048).rearrange("p (u n) -> p u n", u=4)
        o_t = B(4, 3072, 1024).rearrange("p (k n) -> p k n", k=2)

        def mod_row(l, stream, k):
            return mod_d[l, stream:stream + 1, k * D:(k + 1) * D].partition_broadcast(P)

        def row(ap):
            return ap.rearrange("(o n) -> o n", o=1).partition_broadcast(P)

        block = ctx.enter_context(nc.Block())

        def end_phase(eng, k):
            eng.drain().then_inc(S["phase"], 1)
            eng.wait_ge(S["phase"], 4 * k)

        @block.sync
        def _(sp):
            def load(name, dst_words, src, i=0, shape=None):
                s, n = W[name]
                sp.wait_ge(w_used[s], n + 1 + i)
                dst = slot(s, dst_words)
                if shape:
                    dst = dst.rearrange(shape[0], **shape[1])
                sp.dma_start(dst, src).then_inc(w_loaded[s], 16)

            def ada(l, q):
                return a["ada_w"][l, :, bass.ds(q * 512, 512)].rearrange("(p c) n -> p c n", c=DC)

            k8 = ("p (c n) -> p c n", {"c": DC})
            sp.dma_start(cst[:, :], a["c_small"]).then_inc(S["ld_const"], 16)
            for s, v in enumerate((a["c"][0], a["c_ctx"])):
                sp.dma_start(cT[:, 8 * s:8 * s + 8], v.rearrange("(p c) -> p c", c=DC)).then_inc(S["ld_cond"], 16)
            with sp.Fori(0, 2) as i:
                for u in range(6):
                    load(f"ada0_{u}", 4096, ada(0, 6 * i + u), i, k8)
            with sp.Fori(0, 4) as i:
                for u in range(2):
                    s, n = W[f"hy_in_{u}"]
                    sp.wait_ge(w_used[s], n + 1 + i)
                    src = a["hy_in_w"][0].rearrange("(p c) (q m n) -> p c q m n", c=DC, q=3, n=P)
                    dst = slot(s, 3072).rearrange("p (q c n) -> p q c n", q=3, c=DC)
                    for q in range(3):
                        sp.dma_start(dst[:, q], src[:, :, q, bass.ds(2 * i + u, 1), :].rearrange("p c o n -> p c (o n)")
                                     ).then_inc(w_loaded_in[u], 16)
                    load(f"ada1_{u}", 4096, ada(1, 2 * i + u), i, k8)
            for k in range(4):
                load(f"ada1_tail{k}", 4096, ada(1, 8 + k), 0, k8)
            for n in range(2):
                load(f"hy_out{n}", 4096, a["hy_out_w"][0, :, n * 512:(n + 1) * 512]
                     .rearrange("(m p) n -> p m n", p=P), 0, k8)

            def experts(l):
                up = "(p c) n -> p c n"
                load(f"sh1_{l}", 4096, a["sh_w1"][l].rearrange(up, c=DC), 0, k8)
                load(f"sh3_{l}", 4096, a["sh_w3"][l].rearrange(up, c=DC), 0, k8)
                load(f"sh2_{l}", 4096, a["sh_w2"][l].rearrange(up, c=FC), 0, ("p (c n) -> p c n", {"c": FC}))
                sp.wait_ge(M[l]["eid"], 1)

                def tile_weights(name_j, j, i):
                    e = sp.value_load(eid_i[0:1, bass.ds(j, 1)], min_val=0, max_val=E - 1)
                    for w, c in ((1, DC), (3, DC), (2, FC)):
                        src = a[f"exp_w{w}"][l, bass.ds(e, 1), :, :].rearrange("o (p c) n -> p (o c) n", c=c)
                        load(f"e{w}_{l}_{name_j}", 4096, src, i, ("p (c n) -> p c n", {"c": c}))

                for j in range(LOOP_AT):
                    tile_weights(j, j, 0)
                with sp.Fori(0, LOOPED[l] // 2) as i:
                    for u in range(2):
                        tile_weights(LOOP_AT + u, 2 * i + LOOP_AT + u, i)
                tile_weights(EXPERT_TILES[l] - 1, EXPERT_TILES[l] - 1, 0)

            experts(0)
            load("wqd", 3072, a["mla_wq_down"][0].rearrange("(p c) n -> p c n", c=DC), 0, k8)
            load("wkvd", 2560, a["mla_wkv_down"][0].rearrange("(p c) n -> p c n", c=DC), 0, k8)
            load("wkvu", 4096, a["mla_wkv_up"][0].rearrange("(c p) n -> p c n", p=P), 0,
                 ("p (c n) -> p c n", {"c": 2}))
            for n in range(2):
                load(f"wqu{n}", 2304, a["mla_wq_up"][0, :, n * 768:(n + 1) * 768].rearrange("(c p) n -> p c n", p=P),
                     0, ("p (c n) -> p c n", {"c": 3}))
            for n in range(2):
                load(f"wo{n}", 4096, a["mla_wo"][0, :, n * 512:(n + 1) * 512].rearrange("(h p) n -> p h n", p=P), 0, k8)
            experts(1)

        @block.tensor
        def _(pe):
            mm = pe.matmul
            for s in range(SLOTS):
                pe.sem_inc(w_used[s], 1)

            pe.wait_ge(S["ld_const"], 16)
            pe.wait_ge(S["ld_hy"], 48)
            pe.transpose(bank(7, 120), hy_rows[0:120, :], ident[0:120, 0:120]).then_inc(S["hy_turned"], 1)
            pe.wait_ge(S["ld_filt"], 16 * N_FILT)
            mm(bank(0, SEQ, HID), f_w1[0:EMB, :], f_pos[0:EMB, :], start=True, stop=True).then_inc(S["f_pre"], 1)
            for k in range(2):
                pe.wait_ge(S["f_sin"], k + 1)
                mm(bank(1 + k, SEQ, HID), f_w2[k][0:HID, :], f_h[k][0:HID, :], start=True, stop=True
                   ).then_inc(S["f_pre"], 1)
            pe.wait_ge(S["f_sin"], 3)
            for j in range(8):
                t, n = j % 2, j // 2
                if j >= 4:
                    pe.wait_ge(S["f_h"], j - 3)
                mm(bank(j % 4), f_h[2][0:HID, t * P:(t + 1) * P], f_w3[0:HID, n * 512:(n + 1) * 512],
                   start=True, stop=True).then_inc(S["f_w3"], 1)
            pe.wait_ge(S["f_abs"], 1)
            for half in range(2):
                for k in range(4):
                    t, side = k % 2, k // 2
                    m = mm(bank(4 + half), C(C_ONES, P), f_mag[:, t, side * D + half * 512:side * D + half * 512 + 512],
                           start=(k == 0), stop=(k == 3))
            m.then_inc(S["f_norm"], 1)
            pe.wait_ge(S["f_sd"], 1)
            for j in range(8):
                comp, ft, half = j // 4, (j // 2) % 2, j % 2
                pe.wait_ge(S["f_h"], 8)
                if j >= 4:
                    pe.wait_ge(S["f_kdone"], j - 3)
                for t in range(2):
                    m = mm(bank(j % 4), dft_fwd[:, t, comp * SEQ + ft * P:comp * SEQ + ft * P + P],
                           f_sd[:, comp, t, half * 512:half * 512 + 512], start=(t == 0), stop=(t == 1))
                m.then_inc(S["f_k"], 1)

            def ada_piece(name, q, i):
                wait_piece(pe, name, i)
                w = piece(name).rearrange("p (c n) -> p c n", c=DC)
                for j in range(4):
                    for c in range(DC):
                        m = mm(psum[:, 6, bass.ds(q * 8 + 2 * j, 2)], w[:, c, j * P:(j + 1) * P], scT[:, c, :],
                               start=(c == 0), stop=(c == DC - 1))
                freed(m, name)

            pe.wait_ge(S["silu_c"], 1)
            with pe.Fori(0, 2) as i:
                for u in range(6):
                    ada_piece(f"ada0_{u}", 6 * i + u, i)
            pe.drain().then_inc(S["ada_done"], 1)

            def turn_mod(l):
                pe.wait_ge(S["modT_ready"], l + 1)
                pe.transpose(psum[0:96, 7, 0:P], modT, ident).then_inc(S["mod_turned"], 1)

            turn_mod(0)

            def norm_turn(k):
                h = norm_places(k)[3]
                for t in range(NORM_TILES[k]):
                    g = NORM_BASE[k] + t
                    pe.wait_ge(S["n_h"], g + 1)
                    if t >= 2:
                        pe.wait_ge(S["n_hT"], g - 1)
                    for c in range(DC):
                        m = pe.transpose(banks(2 * (t % 2), 2)[:, c * P:(c + 1) * P],
                                         h[:, (t % 2) * D + c:(t % 2) * D + D:DC], ident)
                    m.then_inc(S["n_T"], 1)

            end_phase(pe, 1)
            norm_turn(0)
            end_phase(pe, 2)

            with pe.Fori(0, 4) as i:
                for u in range(2):
                    m_ = 2 * i + u
                    name = f"hy_in_{u}"
                    w = piece(name, 3072).rearrange("p (q c n) -> p q c n", q=3, c=DC)
                    pe.wait_ge(w_loaded_in[u], 48 * i + 48)
                    for o, part in enumerate((1, 2, 0)):
                        pe.wait_ge(S["ip_u"], 3 * m_ + o + 1)
                        for c in range(DC):
                            m = mm(bank(3 * u + o), w[:, part, c, :], hT[:, c, :], start=(c == 0), stop=(c == DC - 1))
                        m.then_inc(S["ip_z"], 1)
                    pe.drain().then_inc(w_used[W[name][0]], 1)
                    ada_piece(f"ada1_{u}", m_, i)
                    pe.wait_ge(S["ip_vg"], m_ + 1)
                    pe.wait_ge(S["ip_ve"], m_ + 1)
                    for t in range(TILES):
                        m = pe.transpose(bank(7)[:, t * P:(t + 1) * P], ip_vgb[:, t * P:(t + 1) * P], ident)
                    m.then_inc(S["ip_vt"], 1)
            end_phase(pe, 3)

            def conv_back(k):
                s, half = k % 2, k // 2
                pe.wait_ge(S["cv_y"], k + 1)
                for m4 in range(4):
                    n = 4 * k + m4
                    if n >= 2:
                        pe.wait_ge(S["cv_yt"], n - 1)
                    for f in range(4):
                        m = mm(bank(4 + m4 % 2, SEQ), cv_Y[:, k % 2, f, m4 * P:(m4 + 1) * P], dft_inv[:, f, :],
                               start=(f == 0), stop=(f == 3))
                    m.then_inc(S["cv_inv"], 1)

            for k in range(4):
                s, half = k % 2, k // 2
                if k >= 1:
                    pe.wait_ge(S["cv_xfree"], k)
                for f in range(4):
                    for t in range(2):
                        m = mm(bank(f), dft_fwd[:, t, f * P:(f + 1) * P], vgtok[:, 2 * s + t, half * 512:half * 512 + 512],
                               start=(t == 0), stop=(t == 1))
                m.then_inc(S["cv_x"], 1)
                ada_piece(f"ada1_tail{k}", 8 + k, 0)
                if k >= 1:
                    conv_back(k - 1)
            conv_back(3)
            pe.drain().then_inc(S["ada_done"], 1)
            end_phase(pe, 4)

            def project(names, lhs, tiles, done, free):
                for n in range(2):
                    for t in range(tiles):
                        j = n * tiles + t
                        if t == 0:
                            wait_piece(pe, names[n])
                        if j >= 4:
                            pe.wait_ge(free, j - 3)
                        w = piece(names[n]).rearrange("p (c n) -> p c n", c=DC)
                        for c in range(DC):
                            m = mm(bank(j % 4), lhs[:, c, t * P:(t + 1) * P], w[:, c, :], start=(c == 0), stop=(c == 7))
                        m.then_inc(done, 1)
                    pe.drain().then_inc(w_used[W[names[n]][0]], 1)

            turn_mod(1)
            project(("hy_out0", "hy_out1"), x0T, TILES, S["op_y"], S["op_x"])
            end_phase(pe, 5)
            norm_turn(1)
            end_phase(pe, 6)

            def moe(l):
                m_, nt, nx = M[l], TOKEN_TILES[l], EXPERT_TILES[l]
                xT = moe_xT
                pe.wait_ge(m_["rw"], 16)
                for t in range(nt):
                    for c in range(DC):
                        m = mm(bank(7)[:, t * E:(t + 1) * E], hT[:, c, t * P:(t + 1) * P], moe_rw[:, c, :],
                               start=(c == 0), stop=(c == DC - 1))
                m.then_inc(m_["logits"], 1)

                def up(g, lhs, names, i=0, last=True):
                    for k, name in enumerate(names):
                        wait_piece(pe, name, i)
                        w = piece(name).rearrange("p (c n) -> p c n", c=DC)
                        for c in range(DC):
                            m = mm(bank(k), lhs(c), w[:, c, :], start=(c == 0), stop=(c == DC - 1))
                        if last and k == 0:
                            freed(m, name)
                    m.then_inc(m_["h13"], 1)
                    if last:
                        pe.drain().then_inc(w_used[W[names[1]][0]], 1)

                def down(g, b, name, i=0, last=True, first=False):
                    pe.wait_ge(m_["hidT"], g + 1)
                    if not first:
                        pe.wait_ge(m_["yev"], g)
                    wait_piece(pe, name, i)
                    w = piece(name).rearrange("p (c n) -> p c n", c=FC)
                    for n in range(2):
                        for c in range(FC):
                            m = mm(bank(5 + n), moe_hidT[b][:, c, :], w[:, c, n * 512:(n + 1) * 512],
                                   start=(c == 0), stop=(c == FC - 1))
                    m.then_inc(m_["y"], 1)
                    if last:
                        pe.drain().then_inc(w_used[W[name][0]], 1)

                def turn_hidden(g, b):
                    pe.wait_ge(m_["hid"], g + 1)
                    for c in range(FC):
                        m = pe.transpose(bank(4)[:, c * P:(c + 1) * P], moe_hid[b][:, c::FC], ident)
                    m.then_inc(m_["hT"], 1)

                def turn_tokens(j, b, count):
                    pe.wait_ge(m_[f"xg{b}"], count)
                    for c in range(DC):
                        m = pe.transpose(banks(2, 2)[:, c * P:(c + 1) * P], moe_xg[b][:, c::DC], ident)
                    m.then_inc(m_["xT"], 1)

                for t in range(nt):
                    up(t, lambda c, t=t: hT[:, c, t * P:(t + 1) * P], (f"sh1_{l}", f"sh3_{l}"), 0, t == nt - 1)
                    if t == 0:
                        pe.wait_ge(m_["sel"], 1)
                        for q in range(nt + 1):
                            for r in range(min(q, nt - 1) + 1):
                                lhs = C(C_UPPER, P) if r == q else C(C_ONES, P)
                                m = mm(bank(7)[:, 64 + q * E:64 + (q + 1) * E], lhs, moe_sel[:, r, :],
                                       start=(r == 0), stop=(r == min(q, nt - 1)))
                        m.then_inc(m_["pos"], 1)
                    if t == 1:
                        pe.wait_ge(m_["hot"], 1)
                        for q in range(2 * nt):
                            m = mm(bank(7)[:, 192:192 + nx], moe_hot[:, q, :], moe_hit[:, q, 0:nx],
                                   start=(q == 0), stop=(q == 2 * nt - 1))
                        m.then_inc(m_["idxp"], 1)
                    if t >= 1:
                        down(t - 1, (t - 1) % 2, f"sh2_{l}", 0, False, t == 1)
                    turn_hidden(t, t % 2)
                turn_tokens(0, 0, 16)

                def step(j, b, name_j, i=0, last=False, count=None):
                    pe.wait_ge(m_["xTe"], j + 1)
                    up(nt + j, lambda c: xT[b][:, c, :], (f"e1_{l}_{name_j}", f"e3_{l}_{name_j}"), i)
                    if not last:
                        turn_tokens(j + 1, 1 - b, count)

                def before(j, b, name, i=0):
                    down(nt + j - 1, 1 - b, name, i)
                    turn_hidden(nt + j, b)

                step(0, 0, 0, 0, False, 16)
                before(0, 0, f"sh2_{l}")
                step(1, 1, 1, 0, False, 32)
                before(1, 1, f"e2_{l}_0")
                with pe.Fori(0, LOOPED[l] // 2) as i:
                    step(2 * i + 2, 0, 2, i, False, 16 * i + 32)
                    before(2 * i + 2, 0, f"e2_{l}_1", i)
                    step(2 * i + 3, 1, 3, i, False, 16 * i + 48)
                    before(2 * i + 3, 1, f"e2_{l}_2", i)
                j = nx - 1
                step(j, j % 2, j, 0, True)
                before(j, j % 2, f"e2_{l}_{j - 1}")
                down(nt + j, j % 2, f"e2_{l}_{j}")

            moe(0)
            end_phase(pe, 7)
            norm_turn(2)
            end_phase(pe, 8)

            def latent(n, tile, name, width, chunks, dst):
                w = piece(name, DC * width).rearrange("p (c n) -> p c n", c=DC)
                wait_piece(pe, name)
                if n >= 1:
                    pe.wait_ge(S["l_lat"], n)
                for c in range(DC):
                    m = mm(bank(0, width), hT[:, c, tile * P:(tile + 1) * P], w[:, c, :],
                           start=(c == 0), stop=(c == DC - 1))
                m.then_inc(S["l_down"], 1)
                pe.wait_ge(S["l_lat"], n + 1)
                for c in range(chunks):
                    m = pe.transpose(bank(1)[:, c * P:(c + 1) * P], mla_lat[:, c * P:(c + 1) * P], ident)
                m.then_inc(S["l_T"], 1)

            for n in range(6):
                is_q = n >= 4
                tile = n - 4 if is_q else n
                chunks = 3 if is_q else 2
                latent(n, tile, "wqd" if is_q else "wkvd", Q_LORA if is_q else KV_LORA + ROPE, chunks, None)
                pe.wait_ge(S["l_TT"], n + 1)
                if n >= 1:
                    pe.wait_ge(S["l_hn"], n)
                    if n <= 4:
                        pe.wait_ge(S["l_v"], n)
                for q in range(4):
                    if is_q:
                        name = f"wqu{q // 2}"
                        wait_piece(pe, name)
                        w = piece(name, 2304).rearrange("p (c n) -> p c n", c=3)[:, :, (q % 2) * 384:(q % 2) * 384 + 384]
                        width = 384
                    else:
                        wait_piece(pe, "wkvu")
                        w = piece("wkvu").rearrange("p (c n) -> p c n", c=2)[:, :, q * 512:(q + 1) * 512]
                        width = 512
                    for c in range(chunks):
                        m = mm(bank(2 + q, width), mla_latT[:, c, :], w[:, c, :], start=(c == 0), stop=(c == chunks - 1))
                m.then_inc(S["l_up"], 1)
                pe.wait_ge(S["l_hr"], n + 1)
                for h in range(H):
                    pe.transpose(banks(6, 2)[:, h * P:(h + 1) * P], mla_hn[:, h, :], ident)
                for h in range(H // 2):
                    m = pe.transpose(bank(1)[:, h * P:(h + 1) * P], B(4, 2048 + h * P, P), ident)
                m.then_inc(S["l_HT"], 1)
                pe.wait_ge(S["l_hevac"], n + 1)
            pe.drain().then_inc(w_used[W["wqd"][0]], 1)
            for name in ("wkvd", "wkvu", "wqu0", "wqu1"):
                pe.sem_inc(w_used[W[name][0]], 1)
            end_phase(pe, 9)

            units = [(h, t) for h in range(H) for t in range(LAT_TILES)]

            def scores(u):
                h, t = units[u]
                r = 64 * (h % 2)
                if u >= 4:
                    pe.wait_ge(S["a_p"], u - 3)
                bk = (0, 1, 6, 7)[u % 4]
                mm(bank(bk), qTn[:, h, t * P:(t + 1) * P], kTn[:, h, :], start=True, stop=False)
                mm(bank(bk), qTr[r:r + 64, h // 2, t * P:(t + 1) * P], kTr[r:r + 64, h // 2, :],
                   start=False, stop=True).then_inc(S["a_s"], 1)

            def turn_probs(u):
                pe.wait_ge(S["a_pn"], u + 1)
                if u >= 2:
                    pe.wait_ge(S["a_PT"], u - 1)
                for k in range(4):
                    m = pe.transpose(bank(2 + u % 2)[:, k * P:(k + 1) * P], a_P[:, u % 4, k * P:(k + 1) * P], ident)
                m.then_inc(S["a_pT"], 1)

            def values(h):
                pe.wait_ge(S["a_PT"], 2 * h + 2)
                if h >= 2:
                    pe.wait_ge(S["a_ot"], h - 1)
                for k in range(4):
                    m = mm(bank(4 + h % 2, SEQ), a_V[:, k, h * P:(h + 1) * P], a_PT[:, h % 2, k, :],
                           start=(k == 0), stop=(k == 3))
                m.then_inc(S["a_o"], 1)

            for u in range(2):
                scores(u)
            for u in range(16):
                if u + 2 < 16:
                    scores(u + 2)
                turn_probs(u)
                if u >= 2 and u % 2 == 0:
                    values(u // 2 - 1)
            values(7)
            end_phase(pe, 10)
            for n in range(2):
                wait_piece(pe, f"wo{n}")
                w = piece(f"wo{n}").rearrange("p (c n) -> p c n", c=DC)
                for t in range(LAT_TILES):
                    for h in range(H):
                        m = mm(bank(2 * n + t), OT[:, h, t * P:(t + 1) * P], w[:, h, :], start=(h == 0), stop=(h == 7))
                    m.then_inc(S["op_y"], 1)
                pe.drain().then_inc(w_used[W[f"wo{n}"][0]], 1)
            end_phase(pe, 11)
            norm_turn(3)
            end_phase(pe, 12)
            moe(1)

        @block.scalar
        def _(act):
            A = nc.scalar.activation
            link = Link(act, S["link_act"])
            dma = act.dma_start

            for q, (w, k) in enumerate((("hy_in_b", 24), ("hy_conv_w", 72), ("hy_conv_b", 24))):
                at = (0, 24, 96)[q]
                src = a[w][0].rearrange("(r n) -> r n", n=P) if w != "hy_conv_w" else \
                    a[w][0].rearrange("k (r n) -> (k r) n", n=P)
                dma(hy_rows[at:at + k, :], src).then_inc(S["ld_hy"], 16)
            dma(f_pos[0:EMB, :], a["c_pos"]).then_inc(S["ld_filt"], 16)
            dma(f_w1[0:EMB, :], a["hy_f_w1"][0]).then_inc(S["ld_filt"], 16)
            for k in range(2):
                dma(f_w2[k][0:HID, :], a["hy_f_w2"][0, k]).then_inc(S["ld_filt"], 16)
                dma(f_par[0:HID, 1 + k:2 + k], a["hy_f_b2"][0, k].rearrange("(n o) -> n o", o=1)
                    ).then_inc(S["ld_filt"], 16)
            dma(f_par[0:HID, 0:1], a["hy_f_b1"][0].rearrange("(n o) -> n o", o=1)).then_inc(S["ld_filt"], 16)
            dma(f_par[0:HID, 3:4], a["hy_sin_freq"][0].rearrange("(n o) -> n o", o=1)).then_inc(S["ld_filt"], 16)
            dma(f_w3[0:HID, :], a["hy_f_w3"][0]).then_inc(S["ld_filt"], 16)
            dma(f_decay, a["c_decay"].rearrange("(t p) d -> p t d", p=P)).then_inc(S["ld_filt"], 16)
            dma(dft_t[:, :], a["c_dft"]).then_inc(S["ld_filt"], 16)
            dma(f_bias, row(a["hy_f_bias"][0])).then_inc(S["ld_filt"], 16)
            dma(X[:, 0:2, :], a["x"][0].rearrange("(t p) d -> p t d", p=P)).then_inc(S["ld_x"], 16)
            dma(X[:, 2:4, :], a["ctx"][0].rearrange("(t p) d -> p t d", p=P)).then_inc(S["ld_x"], 16)
            for l in range(DEPTH):
                for s in range(2):
                    dma(adab[l][48 * s:48 * s + 48, :], a["ada_b"][l].rearrange("(r n) -> r n", n=P)
                        ).then_inc(S["ld_adab"], 16)
            dma(router_b, row(a["router_bias"])).then_inc(S["ld_lat"], 16)
            for k, (w, c) in enumerate([("mla_q_norm_g", c) for c in range(3)] + [("mla_kv_norm_g", c) for c in range(2)]):
                dma(lat_g[:, k:k + 1], a[w][0, c * P:(c + 1) * P].rearrange("(p o) -> p o", o=1)
                    ).then_inc(S["ld_lat"], 16)

            act.wait_ge(S["ld_cond"], 32)
            A(scT, cT.rearrange("p (s c) -> p c s", s=2), ACT.Silu).then_inc(S["silu_c"], 1)

            for k in range(3):
                act.wait_ge(S["f_arg"], k + 1)
                A(f_h[k][0:HID, :], f_arg[0:HID, :], ACT.Sin).then_inc(S["f_sin"], 1)
            act.wait_ge(S["f_h"], 8)
            A(f_mag.rearrange("p t n -> p (t n)"), f_hfb.rearrange("p t n -> p (t n)"), ACT.Abs).then_inc(S["f_abs"], 1)

            def store_mod(l):
                act.wait_ge(S["modr_ready"], l + 1)
                dma(mod_d[l].rearrange("s (j n) -> (s j) n", n=P), mod_r[0:96, :]).then_inc(S["mod_stored"], 16)
                act.wait_ge(S["mod_stored"], 16 * (l + 1))

            store_mod(0)
            end_phase(act, 1)

            n_rows = [0]

            def load_rows(k):
                l, which = k // 2, k % 2
                rows, gain = norm_places(k)[:2]
                sh, sc = ((SHIFT1, SCALE1), (SHIFT2, SCALE2))[which]
                streams = 2 if k < 3 else 1
                for s in range(streams):
                    dma(rows[:, 2 * s * D:(2 * s + 1) * D], mod_row(l, s, sc)).then_inc(S["ld_rows"], 16)
                    dma(rows[:, (2 * s + 1) * D:(2 * s + 2) * D], mod_row(l, s, sh)).then_inc(S["ld_rows"], 16)
                dma(gain, row((a["norm_mix_g"], a["norm_ffn_g"])[which][l])).then_inc(S["ld_rows"], 16)

            def norm(k):
                junk, h = norm_places(k)[2:]
                nt = NORM_TILES[k]
                for t in range(nt):
                    m = A(junk, X[:, t, :], ACT.Square, accum_out=ssq[:, t:t + 1])
                    link(m)
                act.drain().then_inc(S["n_ssq"], 1)
                act.wait_ge(S["n_var"], k + 1)
                A(std[:, 0:nt], var[:, 0:nt], ACT.Sqrt).then_inc(S["n_std"], 1)
                for t in range(nt):
                    g = NORM_BASE[k] + t
                    if k % 2 == 1:
                        act.wait_ge(S["n_h"], g + 1)
                        dma(h2_d[k // 2][t * P:(t + 1) * P, :], h[:, (t % 2) * D:(t % 2 + 1) * D]
                            ).then_inc(S[f"n_st{t % 2}"], 16)
                    act.wait_ge(S["n_T"], g + 1)
                    A(hT[:, :, t * P:(t + 1) * P], banks(2 * (t % 2), 2).rearrange("p (c n) -> p c n", n=P), ACT.Copy
                      ).then_inc(S["n_hT"], 1)
                if k % 2 == 1:
                    base = 16 * (0 if k == 1 else 2)
                    for b in range(2):
                        act.wait_ge(S[f"n_st{b}"], base + 16 * (nt // 2))

            act.wait_ge(S["ld_x"], 32)
            load_rows(0)
            norm(0)
            end_phase(act, 2)

            act.sem_inc(S["ip_u"], 6)
            with act.Fori(0, 4) as i:
                for u in range(2):
                    m_ = 2 * i + u
                    act.wait_ge(S["ip_pm"], m_ + 1)
                    for o, part in enumerate((1, 2, 0)):
                        act.wait_ge(S["ip_z"], 3 * m_ + o + 1)
                        act.wait_ge(S["ip_c"], 3 * m_ + o + 1)
                        A(ip_u[:, o, :, 1:SEQ + 1], bank(3 * u + o).rearrange("p (s t) -> p s t", s=2), ACT.Identity,
                          bias=pm[u][:, part:part + 1]).then_inc(S["ip_u"], 1)
            end_phase(act, 3)

            dma(op_rows[:, 0, :], row(a["hy_out_b"][0])).then_inc(S["g_rows"], 16)
            for s in range(2):
                dma(op_rows[:, 1 + s, :], mod_row(0, s, GATE1)).then_inc(S["g_rows"], 16)
            end_phase(act, 4)
            store_mod(1)
            load_rows(1)
            end_phase(act, 5)
            norm(1)
            act.wait_ge(S["n_h"], NORM_BASE[1] + 4)

            def moe_loads(l):
                dma(moe_rw, a["router_w"].rearrange("(p c) e -> p c e", c=DC)).then_inc(M[l]["rw"], 16)
                dma(moe_g2[:, 0, :], mod_row(l, 0, GATE2)).then_inc(M[l]["ld"], 16)
                if l == 0:
                    dma(moe_g2[:, 1, :], mod_row(l, 1, GATE2)).then_inc(M[l]["ld"], 16)

            end_phase(act, 6)
            moe_loads(0)

            def moe(l):
                m_, nt, nx = M[l], TOKEN_TILES[l], EXPERT_TILES[l]
                act.wait_ge(m_["logits"], 1)
                A(moe_aff[:, 0:nt * E], bank(7)[:, 0:nt * E], ACT.Sigmoid).then_inc(m_["aff"], 1)

                def silu(g, b):
                    act.wait_ge(m_["h13"], g + 1)
                    A(moe_hid[b], bank(0), ACT.Silu).then_inc(m_["silu"], 1)

                def hidden_t(g, b):
                    act.wait_ge(m_["hT"], g + 1)
                    A(moe_hidT[b].rearrange("p c n -> p (c n)"), bank(4), ACT.Copy).then_inc(m_["hidT"], 1)

                def result(g, dst):
                    act.wait_ge(m_["y"], g + 1)
                    A(dst, banks(5, 2), ACT.Copy).then_inc(m_["yev"], 1)

                def expert_result(j, first=False):
                    if not first:
                        act.wait_ge(m_["yst"], 16 * j)
                    result(nt + j, moe_y)
                    act.wait_ge(m_["yev"], nt + j + 1)
                    act.dma_start(y_d[l].rearrange("(t p) d -> p t d", p=P)[:, bass.ds(j, 1), :]
                                  .rearrange("p o d -> p (o d)"), moe_y).then_inc(m_["yst"], 16)

                for t in range(nt):
                    silu(t, t % 2)
                    if t >= 1:
                        result(t - 1, moe_S[:, t - 1, :])
                    hidden_t(t, t % 2)
                silu(nt, 0)
                result(nt - 1, moe_S[:, nt - 1, :])
                hidden_t(nt, 0)
                silu(nt + 1, 1)
                expert_result(0, True)
                hidden_t(nt + 1, 1)
                with act.Fori(0, LOOPED[l] // 2) as i:
                    for u in range(2):
                        silu(2 * i + nt + 2 + u, u)
                        expert_result(2 * i + 1 + u)
                        hidden_t(2 * i + nt + 2 + u, u)
                j = nx - 1
                silu(nt + j, j % 2)
                expert_result(j - 1)
                hidden_t(nt + j, j % 2)
                expert_result(j)
                act.wait_ge(m_["yst"], 16 * nx)

            moe(0)
            end_phase(act, 7)
            load_rows(2)
            norm(2)
            end_phase(act, 8)

            dma(mla_g[:, 0:QK], row(a["mla_q_head_g"][0])).then_inc(S["ld_rows2"], 16)
            dma(mla_g[:, QK:2 * QK], row(a["mla_k_head_g"][0])).then_inc(S["ld_rows2"], 16)
            for n in range(6):
                is_q = n >= 4
                width = Q_LORA if is_q else KV_LORA
                act.wait_ge(S["l_down"], n + 1)
                link(A(mla_sq[:, 0:width], bank(0, width), ACT.Square, accum_out=ssq[:, 0:1]))
                if not is_q:
                    link(A(mla_sq[:, 0:ROPE], psum[:, 0, KV_LORA:KV_LORA + ROPE], ACT.Square, accum_out=ssq[:, 1:2]))
                act.drain().then_inc(S["l_ssq"], 1)
                act.wait_ge(S["l_var"], n + 1)
                A(std[:, 0:1], var[:, 0:1], ACT.Sqrt).then_inc(S["l_std"], 1)
                act.wait_ge(S["l_up"], n + 1)
                if not is_q:
                    act.wait_ge(S["l_v"], n + 1)
                for h in range(H):
                    src = psum[:, 2 + h // 2, (h % 2) * QK:(h % 2) * QK + QK] if is_q else \
                        psum[:, 2 + h // 2, (h % 2) * 256:(h % 2) * 256 + NOPE]
                    link(A(mla_sq[:, 0:src.shape[1]], src, ACT.Square, accum_out=hssq[:, h:h + 1]))
                act.drain().then_inc(S["l_hssq"], 1)
                act.wait_ge(S["l_hvar"], n + 1)
                A(hstd, hvar, ACT.Sqrt).then_inc(S["l_hstd"], 1)
                act.wait_ge(S["l_hevac"], n + 1)
            end_phase(act, 9)

            dma(o_gate, mod_row(1, 0, GATE1)).then_inc(S["ld_rows2"], 16)
            for u in range(16):
                h, t = u // 2, u % 2
                act.wait_ge(S["a_m"], u + 1)
                A(a_P[:, u % 4, :], bank((0, 1, 6, 7)[u % 4]), ACT.Exp, bias=a_nm[:, u % 4:u % 4 + 1], scale=SM_SCALE,
                  accum_out=a_sum[:, u % 4:u % 4 + 1])
                act.drain().then_inc(S["a_p"], 1)
                if u >= 1:
                    v, hv, tv = u - 1, (u - 1) // 2, (u - 1) % 2
                    act.wait_ge(S["a_pT"], v + 1)
                    if hv >= 2:
                        act.wait_ge(S["a_o"], hv - 1)
                    A(a_PT[:, hv % 2, :, tv * P:(tv + 1) * P], bank(2 + v % 2).rearrange("p (k n) -> p k n", n=P),
                      ACT.Copy).then_inc(S["a_PT"], 1)
            act.wait_ge(S["a_pT"], 16)
            act.wait_ge(S["a_o"], 6)
            A(a_PT[:, 1, :, P:2 * P], bank(3).rearrange("p (k n) -> p k n", n=P), ACT.Copy).then_inc(S["a_PT"], 1)
            end_phase(act, 10)
            load_rows(3)
            end_phase(act, 11)
            norm(3)
            end_phase(act, 12)
            moe_loads(1)
            moe(1)

        @block.vector
        def _(dve):
            link = Link(dve, S["link_dve"])
            tt, ts, stt, cp = dve.tensor_tensor, dve.tensor_scalar, dve.scalar_tensor_tensor, dve.tensor_copy
            red = dve.tensor_reduce

            dve.wait_ge(S["hy_turned"], 1)
            link(cp(hy_par, bank(7, 120)))

            dve.wait_ge(S["ld_filt"], 16 * N_FILT)
            for k in range(3):
                dve.wait_ge(S["f_pre"], k + 1)
                if k:
                    dve.wait_ge(S["f_sin"], k)
                link(ts(f_arg[0:HID, :], bank(k, SEQ, HID), f_par[0:HID, k:k + 1], f_par[0:HID, 3:4], ALU.add, ALU.mult))
                link(ts(f_n[0:HID, :], f_arg[0:HID, :], 1.0 / (2.0 * np.pi), ROUND, ALU.mult, ALU.add))
                link(ts(f_n[0:HID, :], f_n[0:HID, :], -ROUND, None, ALU.add))
                link(stt(f_arg[0:HID, :], f_n[0:HID, :], -TWO_PI_HI, f_arg[0:HID, :], ALU.mult, ALU.add))
                link(stt(f_arg[0:HID, :], f_n[0:HID, :], -TWO_PI_LO, f_arg[0:HID, :], ALU.mult, ALU.add))
                ts(f_arg[0:HID, :], f_arg[0:HID, :], 3.1415925, -3.1415925, ALU.min, ALU.max).then_inc(S["f_arg"], 1)
            for j in range(8):
                t, n = j % 2, j // 2
                dve.wait_ge(S["f_w3"], j + 1)
                m = tt(f_hfb[:, t, n * 512:(n + 1) * 512], bank(j % 4),
                       f_decay[:, t, (n % 2) * 512:(n % 2) * 512 + 512], ALU.mult)
                if j < 7:
                    m.then_inc(S["f_h"], 1)
                else:
                    link(m)
            dve.wait_ge(S["f_h"], 7)
            dve.memset(f_hfb[0:1, 0, D:2 * D], 0.0).then_inc(S["f_h"], 1)
            dve.wait_ge(S["f_norm"], 1)
            dve.wait_ge(S["f_h"], 8)
            link(dve.reciprocal(f_rn, banks(4, 2)))
            link(tt(f_sd[:, 0], f_hfb[:, :, 0:D], f_hfb[:, :, D:2 * D], ALU.add))
            tt(f_sd[:, 1], f_hfb[:, :, 0:D], f_hfb[:, :, D:2 * D], ALU.subtract).then_inc(S["f_sd"], 1)
            for j in range(8):
                comp, ft, half = j // 4, (j // 2) % 2, j % 2
                dve.wait_ge(S["f_k"], j + 1)
                cols = slice(half * 512, half * 512 + 512)
                m = tt(f_K[:, 2 * comp + ft, cols], bank(j % 4), f_rn[:, cols], ALU.mult)
                m.then_inc(S["f_kdone"], 1)
                if comp == 0:
                    dve.wait_ge(S["f_kdone"], j + 1)
                    link(tt(f_K[:, ft, cols], f_K[:, ft, cols], f_bias[:, cols], ALU.add))

            def mod_rows(l):
                dve.wait_ge(S["ada_done"], l + 1)
                cp(modT.rearrange("p (s j) -> p s j", s=2), psum[:, 6, 0:96].rearrange("p (j s) -> p s j", s=2)
                   ).then_inc(S["modT_ready"], 1)
                dve.wait_ge(S["mod_turned"], l + 1)
                dve.wait_ge(S["ld_adab"], 64)
                tt(mod_r[0:96, :], psum[0:96, 7, 0:P], adab[l][0:96, :], ALU.add).then_inc(S["modr_ready"], 1)

            mod_rows(0)
            end_phase(dve, 1)

            rows_seen = [0]

            def norm(k):
                rows, gain, junk, h = norm_places(k)
                nt = NORM_TILES[k]
                streams = 2 if k < 3 else 1
                dve.wait_ge(S["n_ssq"], k + 1)
                ts(var[:, 0:nt], ssq[:, 0:nt], 1.0 / D, EPS, ALU.mult, ALU.add).then_inc(S["n_var"], 1)
                rows_seen[0] += 16 * (2 * streams + 1)
                dve.wait_ge(S["ld_rows"], rows_seen[0])
                for s in range(streams):
                    r = rows[:, 2 * s * D:(2 * s + 1) * D]
                    link(stt(r, r, 1.0, gain, ALU.add, ALU.mult))
                dve.wait_ge(S["n_std"], k + 1)
                link(dve.reciprocal(rstd[:, 0:nt], std[:, 0:nt]))
                for t in range(nt):
                    g, s = NORM_BASE[k] + t, t // 2
                    hb = h[:, (t % 2) * D:(t % 2 + 1) * D]
                    if t >= 2:
                        dve.wait_ge(S["n_T"], g - 1)
                        if k % 2 == 1:
                            dve.wait_ge(S[f"n_st{t % 2}"], 16)
                    link(stt(hb, X[:, t, :], rstd[:, t:t + 1], rows[:, 2 * s * D:(2 * s + 1) * D], ALU.mult, ALU.mult))
                    tt(hb, hb, rows[:, (2 * s + 1) * D:(2 * s + 2) * D], ALU.add).then_inc(S["n_h"], 1)

            dve.wait_ge(S["ld_x"], 32)
            norm(0)
            end_phase(dve, 2)

            dve.memset(B(3, 0, 3 * 516), 0.0).then_inc(S["ip_c"], 3)
            dve.sem_inc(S["ip_ve"], 1)
            par = hy_par.rearrange("p (v m) -> p v m", m=8)
            with dve.Fori(0, 4) as i:
                link.enter(i, 2 * 6)
                for u in range(2):
                    m_ = 2 * i + u
                    cp(pm[u], par[:, :, bass.ds(m_, 1)].rearrange("p v o -> p (v o)")).then_inc(S["ip_pm"], 1)
                    dve.wait_ge(S["ip_pm"], m_ + 1)
                    for o, part in enumerate((1, 2, 0)):
                        k = [pm[u][:, (1 + j) * 3 + part:(1 + j) * 3 + part + 1] for j in range(4)]
                        src, tmp = ip_u[:, o], ip_t[:, o]
                        dve.wait_ge(S["ip_u"], 6 + 3 * m_ + o + 1)
                        link(ts(tmp, src[:, :, 1:SEQ + 1], k[1], k[3], ALU.mult, ALU.add))
                        link(stt(tmp, src[:, :, 0:SEQ], k[0], tmp, ALU.mult, ALU.add))
                        dst = tmp if o < 2 else x0T[:, bass.ds(m_, 1), :].rearrange("p o (s t) -> p (o s) t", s=2)
                        stt(dst, src[:, :, 2:SEQ + 2], k[2], tmp, ALU.mult, ALU.add).then_inc(S["ip_c"], 1)
                        if o == 1:
                            dve.wait_ge(S["ip_c"], 3 + 3 * m_ + 2)
                            tt(ip_vgb.rearrange("p (s t) -> p s t", s=2), ip_t[:, 0], ip_t[:, 1], ALU.mult
                               ).then_inc(S["ip_vg"], 1)
                    dve.wait_ge(S["ip_vt"], m_ + 1)
                    ts(vgtok[:, :, bass.ds(m_ * P, P)], bank(7).rearrange("p (t n) -> p t n", n=P), 1.0, None, ALU.mult
                       ).then_inc(S["ip_ve"], 1)
                link.leave(4)
            end_phase(dve, 3)

            def back(k):
                s, half = k % 2, k // 2
                for m4 in range(4):
                    dve.wait_ge(S["cv_inv"], 4 * k + m4 + 1)
                    dst = x0T[:, 4 * half + m4, s * SEQ:(s + 1) * SEQ]
                    tt(dst, bank(4 + m4 % 2, SEQ), dst, ALU.mult).then_inc(S["cv_yt"], 1)

            for k in range(4):
                half = k // 2
                cols = slice(half * 512, half * 512 + 512)
                dve.wait_ge(S["cv_x"], k + 1)
                if k >= 1:
                    dve.wait_ge(S["cv_y"], k)
                if k >= 2:
                    dve.wait_ge(S["cv_inv"], 4 * (k - 1))
                Y = cv_Y[:, k % 2]
                for f in range(2):
                    Kr, Ki, t0, t1 = f_K[:, f, cols], f_K[:, 2 + f, cols], cv_t[:, 0], cv_t[:, 1]
                    tt(Y[:, f], bank(f), Kr, ALU.mult)
                    tt(t0, bank(2 + f), Ki, ALU.mult)
                    tt(Y[:, 2 + f], bank(f), Ki, ALU.mult)
                    link(tt(t1, bank(2 + f), Kr, ALU.mult))
                    if f == 1:
                        dve.sem_inc(S["cv_xfree"], 1)
                    tt(Y[:, f], Y[:, f], t0, ALU.subtract)
                    m = tt(Y[:, 2 + f], Y[:, 2 + f], t1, ALU.add)
                    if f == 0:
                        link(m)
                m.then_inc(S["cv_y"], 1)
                if k >= 1:
                    back(k - 1)
            back(3)
            end_phase(dve, 4)

            mod_rows(1)
            dve.wait_ge(S["g_rows"], 48)
            for n in range(2):
                for t in range(TILES):
                    j = n * TILES + t
                    cols = slice(n * 512, n * 512 + 512)
                    dve.wait_ge(S["op_y"], j + 1)
                    tmp = op_t[:, j % 2]
                    tt(tmp, bank(j % 4), op_rows[:, 0, cols], ALU.add).then_inc(S["op_x"], 1)
                    dve.wait_ge(S["op_x"], j + 1)
                    link(tt(tmp, tmp, op_rows[:, 1 + t // 2, cols], ALU.mult))
                    tt(X[:, t, cols], X[:, t, cols], tmp, ALU.add)
            end_phase(dve, 5)
            norm(1)
            end_phase(dve, 6)

            def moe(l):
                m_, nt, nx = M[l], TOKEN_TILES[l], EXPERT_TILES[l]
                nte = nt * E
                dve.wait_ge(S["ld_lat"], 96)
                v3 = lambda ap: ap.rearrange("p (t e) -> p t e", e=E)
                aff, sb_, w0, w1 = moe_aff[:, 0:nte], moe_r[0][:, 0:nte], moe_r[1][:, 0:nte], moe_r[2][:, 0:nte]
                pair, gs, g1, g2 = moe_pair[:, 0:nt * G, :], moe_g4[0][:, 0:nt * G], moe_g4[1][:, 0:nt * G], moe_g4[2][:, 0:nt]

                dve.wait_ge(m_["aff"], 1)
                link(tt(v3(sb_), v3(aff), bc(router_b, 1, nt), ALU.add))
                q = sb_.rearrange("p (g e) -> p g e", e=PER_G)
                tt(pair[:, :, 0:3], q[:, :, 0:3], q[:, :, 1:4], ALU.add)
                tt(pair[:, :, 3:5], q[:, :, 0:2], q[:, :, 2:4], ALU.add)
                link(tt(pair[:, :, 5:6], q[:, :, 0:1], q[:, :, 3:4], ALU.add))
                link(red(gs, pair, AX.X, ALU.max))
                gs3, g13 = (x.rearrange("p (t g) -> p t g", g=G) for x in (gs, g1))

                def first_max(dst3, val3, best, desc, n):
                    link(red(best, val3, AX.X, ALU.max))
                    link(tt(dst3, val3, bc(best, 2, n), ALU.is_equal))
                    link(tt(dst3, dst3, bc(desc, 1, nt), ALU.mult))
                    link(red(best, dst3, AX.X, ALU.max))
                    link(tt(dst3, dst3, bc(best, 2, n), ALU.is_equal))

                first_max(g13, gs3, g2, C(C_DESC4, G), G)
                gm = bc(g1, 2, PER_G)
                qw = w0.rearrange("p (g e) -> p g e", e=PER_G)
                link(tt(qw, q, gm, ALU.mult))
                link(ts(g1, g1, -1.0, BIG, ALU.add, ALU.mult))
                link(tt(qw, qw, gm, ALU.add))
                best = moe_g4[2][:, 0:nt]
                desc = C(C_DESC, E)
                sa, sb2 = sel_a[:, 0:nte], sel_b[:, 0:nte]
                first_max(v3(sa), v3(w0), best, desc, E)
                link(stt(w0, sa, -2.0 * BIG, w0, ALU.mult, ALU.add))
                first_max(v3(sb2), v3(w0), best, desc, E)
                tt(moe_sel[:, 0:nt, :].rearrange("p t e -> p (t e)"), sa, sb2, ALU.add).then_inc(m_["sel"], 1)
                for k, s_ in enumerate((sa, sb2)):
                    link(tt(w1, s_, aff, ALU.mult))
                    link(red(gates[:, k * TILES:k * TILES + nt], v3(w1), AX.X, ALU.add))
                link(tt(best, gates[:, 0:nt], gates[:, TILES:TILES + nt], ALU.add))
                link(dve.reciprocal(best, best))
                for k in range(2):
                    gk = gates[:, k * TILES:k * TILES + nt]
                    link(tt(gk, gk, best, ALU.mult))

                def hidden(g, b):
                    dve.wait_ge(m_["silu"], g + 1)
                    tt(moe_hid[b], moe_hid[b], bank(1), ALU.mult).then_inc(m_["hid"], 1)

                def tokens_t(j, b):
                    dve.wait_ge(m_["xT"], j + 1)
                    cp(moe_xT[b].rearrange("p c n -> p (c n)"), banks(2, 2)).then_inc(m_["xTe"], 1)

                hidden(0, 0)

                dve.wait_ge(m_["pos"], 1)
                cnt = bank(7)[:, 64 + nt * E:64 + (nt + 1) * E]
                link(ts(cnt16, cnt, 0.0, None, ALU.is_gt))
                for k in range(1, nt):
                    link(stt(cnt16, cnt, float(k * P), cnt16, ALU.is_gt, ALU.add))
                link(dve.memset(scan[0], 0.0))
                link(dve.memset(scan[1], 0.0))
                link(cp(scan[0][:, E:2 * E], cnt16))
                src = 0
                for d in (1, 2, 4, 8):
                    link(tt(scan[1 - src][:, E:2 * E], scan[src][:, E:2 * E], scan[src][:, E - d:2 * E - d], ALU.add))
                    src = 1 - src
                first = scan[src][:, E - 1:2 * E - 1]
                link(tt(moe_cmp[:, 0:nx * E].rearrange("p (t e) -> p t e", e=E), bc(C(C_TILE, nx), 2, E),
                        bc(first, 1, nx), ALU.is_ge))
                link(red(moe_r[2][:, 0:nx], moe_cmp[:, 0:nx * E].rearrange("p (t e) -> p t e", e=E), AX.X, ALU.add))
                ts(eid_i[:, 0:nx], moe_r[2][:, 0:nx], -1.0, None, ALU.add).then_inc(m_["eid"], 1)
                link(stt(v3(w0), bc(first, 1, nt), float(P), v3(bank(7)[:, 64:64 + nte]), ALU.mult, ALU.add))
                for k, s_ in enumerate((sa, sb2)):
                    link(tt(w1, s_, w0, ALU.mult))
                    link(red(moe_slot[:, k * nt:(k + 1) * nt], v3(w1), AX.X, ALU.add))
                sl = moe_slot[:, 0:2 * nt]
                cp(slot_i[:, 0:2 * nt], sl)
                ge = moe_cmp[:, 0:2 * nt * (nx + 1)].rearrange("p (q t) -> p q t", t=nx + 1)
                link(tt(ge, bc(sl, 2, nx + 1), bc(C(C_GRID, nx + 1), 1, 2 * nt), ALU.is_ge))
                hi = moe_slot[:, 2 * nt:4 * nt]
                link(red(hi, ge, AX.X, ALU.add))
                link(stt(sl, hi, float(-P), sl, ALU.mult, ALU.add))
                link(ts(sl, sl, float(P), None, ALU.add))
                link(tt(moe_hot[:, 0:2 * nt, :], bc(C(C_IOTA, P), 1, 2 * nt), bc(sl, 2, P), ALU.is_equal))
                hit = moe_hit[:, 0:2 * nt, 0:nx]
                link(tt(hit, ge[:, :, 0:nx], ge[:, :, 1:nx + 1], ALU.subtract))
                for k in range(2):
                    h_ = moe_hit[:, k * nt:(k + 1) * nt, 0:nx]
                    m = tt(h_, h_, bc(C(C_TOK, nt), 2, nx), ALU.mult)
                m.then_inc(m_["hot"], 1)

                hidden(1, 1)
                dve.wait_ge(m_["idxp"], 1)
                cp(idx_i[:, 0:nx], bank(7)[:, 192:192 + nx]).then_inc(m_["idx"], 1)
                for t in range(2, nt):
                    hidden(t, t % 2)
                tokens_t(0, 0)
                hidden(nt, 0)
                tokens_t(1, 1)
                hidden(nt + 1, 1)
                tokens_t(2, 0)
                dve.wait_ge(m_["yev"], nt)
                dve.wait_ge(m_["ld"], 16 * (2 - l))
                for t in range(nt):
                    st = moe_S[:, t, :]
                    link(tt(st, st, moe_g2[:, t // 2, :], ALU.mult))
                    link(tt(X[:, t, :], X[:, t, :], st, ALU.add))
                with dve.Fori(0, LOOPED[l] // 2) as i:
                    for u in range(2):
                        hidden(2 * i + nt + 2 + u, u)
                        tokens_t(2 * i + 3 + u, 1 - u)
                hidden(nt + nx - 1, (nx - 1) % 2)

                for t in range(nt):
                    dve.wait_ge(m_[f"ga{t % 2}"], 32 * (t // 2 + 1))
                    ya, yb = (moe_gat[:, t % 2, k, :] for k in range(2))
                    link(ts(ya, ya, gates[:, t:t + 1], None, ALU.mult))
                    link(stt(yb, yb, gates[:, TILES + t:TILES + t + 1], ya, ALU.mult, ALU.add))
                    link(tt(yb, yb, moe_g2[:, t // 2, :], ALU.mult))
                    tt(X[:, t, :], X[:, t, :], yb, ALU.add).then_inc(m_["comb"], 1)

            moe(0)
            end_phase(dve, 7)
            norm(2)
            end_phase(dve, 8)

            dve.wait_ge(S["ld_rows2"], 32)
            for n in range(6):
                is_q = n >= 4
                tile = n - 4 if is_q else n
                width, chunks = (Q_LORA, 3) if is_q else (KV_LORA, 2)
                dve.wait_ge(S["l_ssq"], n + 1)
                ts(var[:, 0:1], ssq[:, 0:1], 1.0 / width, EPS, ALU.mult, ALU.add).then_inc(S["l_var"], 1)
                dve.wait_ge(S["l_std"], n + 1)
                link(dve.reciprocal(rstd[:, 0:1], std[:, 0:1]))
                if not is_q:
                    link(cp(mla_pe, psum[:, 0, KV_LORA:KV_LORA + ROPE]))
                ts(mla_lat[:, 0:width], bank(0, width), rstd[:, 0:1], None, ALU.mult).then_inc(S["l_lat"], 1)
                dve.wait_ge(S["l_T"], n + 1)
                for c in range(chunks):
                    g = (0 if is_q else 3) + c
                    m = ts(mla_latT[:, c, :], bank(1)[:, c * P:(c + 1) * P], lat_g[:, g:g + 1], None, ALU.mult)
                m.then_inc(S["l_TT"], 1)
                if not is_q:
                    dve.wait_ge(S["l_up"], n + 1)
                    up4 = psum[:, 2:6, :].rearrange("p b (h d) -> p (b h) d", d=256)
                    cp(a_V[:, tile, :].rearrange("p (h d) -> p h d", d=VD), up4[:, :, NOPE:256]).then_inc(S["l_v"], 1)
                dve.wait_ge(S["l_hssq"], n + 1)
                if is_q:
                    ts(hvar, hssq, 1.0 / QK, EPS, ALU.mult, ALU.add).then_inc(S["l_hvar"], 1)
                else:
                    link(ts(hssq, hssq, ssq[:, 1:2], 1.0 / QK, ALU.add, ALU.mult))
                    ts(hvar, hssq, EPS, None, ALU.add).then_inc(S["l_hvar"], 1)
                dve.wait_ge(S["l_hstd"], n + 1)
                link(dve.reciprocal(hrstd, hstd))
                if is_q:
                    for b in range(4):
                        src = psum[:, 2 + b, 0:384].rearrange("p (h d) -> p h d", d=QK)
                        pair_r = hrstd[:, 2 * b:2 * b + 2]
                        tt(mla_hn[:, 2 * b:2 * b + 2, :], src[:, :, 0:NOPE], bc(pair_r, 2, NOPE), ALU.mult)
                        m = tt(mla_hr[:, 2 * b:2 * b + 2, :], src[:, :, NOPE:QK], bc(pair_r, 2, ROPE), ALU.mult)
                else:
                    tt(mla_hr, bc(mla_pe, 1, H), bc(hrstd, 2, ROPE), ALU.mult)
                    m = tt(mla_hn, up4[:, :, 0:NOPE], bc(hrstd, 2, NOPE), ALU.mult)
                m.then_inc(S["l_hn"], 1)
                dve.wait_ge(S["l_hn"], n + 1)
                gain = mla_g[:, 0:QK] if is_q else mla_g[:, QK:2 * QK]
                link(tt(mla_hn, mla_hn, bc(gain[:, 0:NOPE], 1, H), ALU.mult))
                m = tt(mla_hr, mla_hr, bc(gain[:, NOPE:QK], 1, H), ALU.mult)
                if is_q or n < LAT_TILES:
                    link(m)
                    t0 = C_ROPE + 64 * tile
                    cos = bc(C(t0, 32).rearrange("p (a k) -> p a k", a=2), 1, H)
                    sin = bc(C(t0 + 32, 32).rearrange("p (a k) -> p a k", a=2), 1, H)
                    r = mla_hr.rearrange("p h (a b k) -> p h a b k", a=2, b=2)
                    t4 = [mla_t[:, k * 256:(k + 1) * 256].rearrange("p (h a k) -> p h a k", h=H, a=2) for k in range(4)]
                    x1, x2 = r[:, :, :, 0, :], r[:, :, :, 1, :]
                    tt(t4[0], x1, cos, ALU.mult)
                    tt(t4[1], x2, sin, ALU.mult)
                    tt(t4[2], x2, cos, ALU.mult)
                    link(tt(t4[3], x1, sin, ALU.mult))
                    tt(x1, t4[0], t4[1], ALU.subtract)
                    tt(x2, t4[2], t4[3], ALU.add).then_inc(S["l_hr"], 1)
                else:
                    m.then_inc(S["l_hr"], 1)
                dve.wait_ge(S["l_HT"], n + 1)
                nope, rope = (qTn, qTr) if is_q else (kTn, kTr)
                cols = slice(tile * P, (tile + 1) * P)
                cp(nope[:, :, cols], banks(6, 2).rearrange("p (h n) -> p h n", n=P))
                cp(rope[:, :, cols], bank(1).rearrange("p (h n) -> p h n", n=P)).then_inc(S["l_hevac"], 1)
            end_phase(dve, 9)

            def head_out(h):
                dve.wait_ge(S["a_o"], h + 1)
                cp(OT[:, h, :], bank(4 + h % 2, SEQ)).then_inc(S["a_ot"], 1)

            def probs(u):
                dve.wait_ge(S["a_p"], u + 1)
                s = a_sum[:, u % 4:u % 4 + 1]
                link(dve.reciprocal(s, s))
                ts(a_P[:, u % 4, :], a_P[:, u % 4, :], s, None, ALU.mult).then_inc(S["a_pn"], 1)

            for u in range(16):
                dve.wait_ge(S["a_s"], u + 1)
                if u >= 4:
                    dve.wait_ge(S["a_p"], u - 3)
                nm = a_nm[:, u % 4:u % 4 + 1]
                link(red(nm, bank((0, 1, 6, 7)[u % 4]), AX.X, ALU.max))
                ts(nm, nm, -SM_SCALE, None, ALU.mult).then_inc(S["a_m"], 1)
                if u >= 1:
                    probs(u - 1)
                if u >= 4 and u % 2 == 0:
                    head_out(u // 2 - 2)
            probs(15)
            head_out(6)
            head_out(7)
            end_phase(dve, 10)
            dve.wait_ge(S["ld_rows2"], 48)
            for n in range(2):
                for t in range(LAT_TILES):
                    j = 2 * n + t
                    cols = slice(n * 512, n * 512 + 512)
                    dve.wait_ge(S["op_y"], 8 + j + 1)
                    tmp = o_t[:, j % 2]
                    link(tt(tmp, bank(j), o_gate[:, cols], ALU.mult))
                    tt(X[:, t, cols], X[:, t, cols], tmp, ALU.add)
            end_phase(dve, 11)
            norm(3)
            end_phase(dve, 12)
            moe(1)

        @block.gpsimd
        def _(pool):
            def moe(l):
                m_, nt, nx = M[l], TOKEN_TILES[l], EXPERT_TILES[l]
                pool.wait_ge(m_["idx"], 1)

                def gather(j, b):
                    nc.gpsimd.tensor_copy(idx_cur[:, b:b + 1], idx_i[:, bass.ds(j, 1)]).then_inc(m_["cur"], 1)
                    pool.wait_ge(m_["cur"], j + 1)
                    pool.sem_inc(m_["go"], 1)
                    nc.gpsimd.indirect_dma_start(
                        moe_xg[b], None, h2_d[l][:, :],
                        bass.IndirectOffsetOnAxis(ap=idx_cur[:, b:b + 1], axis=0)).then_inc(m_[f"xg{b}"], 16)

                gather(0, 0)
                gather(1, 1)
                pool.wait_ge(m_["xT"], 1)
                gather(2, 0)
                with pool.Fori(0, LOOPED[l] // 2) as i:
                    for u in range(2):
                        pool.wait_ge(m_["xT"], 2 * i + 2 + u)
                        gather(2 * i + 3 + u, 1 - u)
                pool.wait_ge(m_["yst"], 16 * nx)
                for t in range(nt):
                    if t >= 2:
                        pool.wait_ge(m_["comb"], t - 1)
                    for k in range(2):
                        nc.gpsimd.indirect_dma_start(
                            moe_gat[:, t % 2, k, :], None, y_d[l][:, :],
                            bass.IndirectOffsetOnAxis(ap=slot_i[:, k * nt + t:k * nt + t + 1], axis=0)
                        ).then_inc(m_[f"ga{t % 2}"], 16)

            for k in range(1, 7):
                end_phase(pool, k)
            moe(0)
            for k in range(7, 13):
                end_phase(pool, k)
            moe(1)
            pool.wait_ge(M[1]["comb"], LAT_TILES)
            pool.dma_start(out[0].rearrange("(t p) d -> p t d", p=P), X[:, 0:LAT_TILES, :]).then_inc(S["out_st"], 16)
            pool.wait_ge(S["out_st"], 16)


INPUTS = ["x", "c", "ctx", "c_ctx", "ada_w", "ada_b", "norm_mix_g", "norm_ffn_g", "hy_in_w", "hy_in_b", "hy_conv_w",
          "hy_conv_b", "hy_f_w1", "hy_f_b1", "hy_f_w2", "hy_f_b2", "hy_f_w3", "hy_sin_freq", "hy_f_bias", "hy_out_w",
          "hy_out_b", "mla_wq_down", "mla_q_norm_g", "mla_wq_up", "mla_wkv_down", "mla_kv_norm_g", "mla_wkv_up",
          "mla_q_head_g", "mla_k_head_g", "mla_wo", "router_w", "router_bias", "exp_w1", "exp_w3", "exp_w2", "sh_w1",
          "sh_w3", "sh_w2"]


def kernel(**inputs):
    import concourse.bacc as bacc
    from concourse.bass_utils import run_bass_kernel_spmd as run

    nc = bacc.Bacc("TRN2", target_bir_lowering=False, num_devices=1)
    arrays = {f"in_{n}": np.ascontiguousarray(inputs[n]) for n in INPUTS}
    arrays.update(shape_constants())
    aps = {n.removeprefix("in_"): nc.dram_tensor(n, v.shape, F32, kind="ExternalInput").ap() for n, v in arrays.items()}
    out = nc.dram_tensor("out", [1, SEQ, D], F32, kind="ExternalOutput").ap()
    build(nc, aps, out)
    return run(nc, [arrays], core_ids=[0]).results[0]["out"]
```

```python
from contextlib import ExitStack

import numpy as np
import concourse.bass as bass
from concourse import mybir

ACT = mybir.ActivationFunctionType
ALU = mybir.AluOpType
AX = mybir.AxisListType
F32 = mybir.dt.float32
I32 = mybir.dt.int32

P = 128
D = 1024
DC = D // P
SEQ = 256
TILES = 2 * SEQ // P
LAT_TILES = SEQ // P
DEPTH = 2
EPS = 1e-6
N_MOD = 6
SHIFT1, SCALE1, GATE1, SHIFT2, SCALE2, GATE2 = range(N_MOD)

HID = 64
EMB = 33
BANDS = 16
TWO_PI_HI = 6.28125
TWO_PI_LO = 2.0 * np.pi - TWO_PI_HI
ROUND = 1.5 * 2.0 ** 23

H = 8
NOPE, ROPE, QK, VD = 128, 64, 192, 128
Q_LORA, KV_LORA = 384, 256
SM_SCALE = QK ** -0.5

E, G, PER_G = 16, 4, 4
FF = 512
FC = FF // P
TOP_K = 2


def expert_tiles(tokens):
    return ((tokens * TOP_K - E) // P + E + 1) // 2 * 2


TOKEN_TILES = [TILES, LAT_TILES]
EXPERT_TILES = [expert_tiles(t * P) for t in TOKEN_TILES]
T_MAX = max(EXPERT_TILES)

SLOTS = 6
SLOT_W = 4096
BIG = 1.0e30

C_IDENT, C_UPPER, C_ONES, C_IOTA = 0, 128, 256, 384
C_GRID = 512
C_TILE = C_GRID + T_MAX + 1
C_DESC = C_TILE + T_MAX + 1
C_DESC4 = C_DESC + E
C_TOK = C_DESC4 + G
C_ROPE = C_TOK + TILES
C_END = C_ROPE + LAT_TILES * 64


def shape_constants():
    f = np.float32
    small = np.zeros((P, C_END), f)
    small[:, C_IDENT:C_IDENT + P] = np.eye(P)
    small[:, C_UPPER:C_UPPER + P] = np.triu(np.ones((P, P)), 1)
    small[:, C_ONES:C_ONES + P] = 1
    small[:, C_IOTA:C_IOTA + P] = np.arange(P)
    small[:, C_GRID:C_GRID + T_MAX + 1] = P * np.arange(T_MAX + 1)
    small[:, C_TILE:C_TILE + T_MAX + 1] = np.arange(T_MAX + 1)
    small[:, C_DESC:C_DESC + E] = E - np.arange(E)
    small[:, C_DESC4:C_DESC4 + G] = G - np.arange(G)
    small[:, C_TOK:C_TOK + TILES] = np.arange(P)[:, None] + P * np.arange(TILES)[None]
    grid_w, half = 64, ROPE // 2
    inv = (f(10000.0) ** (-np.arange(0, half, 2, dtype=f) / f(half))).astype(f)
    tok = np.arange(SEQ)
    ang = np.stack([(tok // grid_w).astype(f)[:, None] * inv, (tok % grid_w).astype(f)[:, None] * inv], 1)
    for t in range(LAT_TILES):
        a = ang[t * P:(t + 1) * P].reshape(P, 32)
        small[:, C_ROPE + 64 * t:C_ROPE + 64 * t + 32] = np.cos(a)
        small[:, C_ROPE + 64 * t + 32:C_ROPE + 64 * t + 64] = np.sin(a)
    w = np.pi * np.outer(np.arange(SEQ), 2 * np.arange(SEQ) + 1) / (2.0 * SEQ)
    fwd = np.concatenate([np.cos(w), -np.sin(w)], 1).reshape(2, P, 2 * SEQ).transpose(1, 0, 2)
    inv_t = np.concatenate([np.cos(w.T), -np.sin(w.T)], 0).reshape(4, P, SEQ).transpose(1, 0, 2) / SEQ
    dft = np.concatenate([fwd.reshape(P, -1), inv_t.reshape(P, -1)], 1).astype(f)
    t_norm = np.linspace(0.0, 1.0, SEQ, dtype=f)[:, None]
    bands = np.linspace(1e-4, BANDS - 1, BANDS, dtype=f)[None]
    a = (f(2.0 * np.pi) * bands * np.arange(SEQ, dtype=f)[:, None] / f(SEQ)).astype(f)
    pos = np.ascontiguousarray(np.concatenate([t_norm, np.cos(a), -np.sin(a)], 1).T.astype(f))
    lo, hi = np.log(1e-2) / 1.5, np.log(1e-2) / 0.3
    deltas = np.linspace(lo, hi, D, dtype=f)
    decay = np.exp(-t_norm * np.abs(deltas)).astype(f)
    return {"c_small": small, "c_dft": dft, "c_pos": pos, "c_decay": decay}


class Link:

    def __init__(self, eng, sem):
        self.eng, self.sem, self.n, self.off = eng, sem, 0, 0

    def __call__(self, ins):
        self.n += 1
        ins.then_inc(self.sem, 1)
        self.eng.wait_ge(self.sem, self.off + self.n)

    def enter(self, i, per):
        self.at, self.per, self.off = self.n, per, i * per

    def leave(self, iterations):
        assert self.n == self.at + self.per, (self.n - self.at, self.per)
        self.n, self.off = self.at + self.per * iterations, 0


def build(nc, a, out):
    with ExitStack() as ctx:
        def sb(name, words, dt=F32):
            return ctx.enter_context(nc.sbuf_tensor(name, [P, words], dt))

        def sem(name):
            return ctx.enter_context(nc.semaphore(name))

        def dram(name, shape):
            return nc.dram_tensor(name, shape, F32, kind="Internal").ap()

        mod_d = dram("mod_rows", [DEPTH, 2, N_MOD * D])
        h2_d = [dram(f"h2_{l}", [TOKEN_TILES[l] * P, D]) for l in range(DEPTH)]
        y_d = dram("expert_out", [T_MAX * P, D])

        ring = sb("weight_ring", SLOTS * SLOT_W)
        Xt = sb("residual", TILES * D)
        blk = sb("blocks", 5 * 4096)
        dft_t = sb("dft", 2048)
        cst = sb("small_constants", C_END)
        hy_rows_t = sb("hyena_rows", P)
        mod_t = sb("mod_pieces", 512)
        small = sb("small_values", 560)
        ints = sb("int_values", 2 * T_MAX + 2 * TILES + 4, I32)
        psum = ctx.enter_context(nc.psum_tensor("psum", [P, 8, 512], F32))

        def slot(s, words=SLOT_W):
            return ring[:, s * SLOT_W:s * SLOT_W + words]

        def B(block, at, words):
            return blk[:, block * 4096 + at:block * 4096 + at + words]

        def C(at, words):
            return cst[:, at:at + words]

        small_at = [0]

        def sm(words):
            at = small_at[0]
            small_at[0] += words
            assert small_at[0] <= 560
            return small[:, at:at + words]

        X = Xt[:, :].rearrange("p (t d) -> p t d", d=D)
        ident = C(C_IDENT, P)
        dft_fwd = dft_t[:, 0:1024].rearrange("p (t f) -> p t f", t=2)
        dft_inv = dft_t[:, 1024:2048].rearrange("p (k t) -> p k t", k=4)

        cT = sm(16)
        scT = sm(16).rearrange("p (c s) -> p c s", s=2)
        ssq, var, std, rstd = sm(8), sm(8), sm(8), sm(8)
        hy_par = sm(120)
        pm = [sm(15), sm(15)]
        router_b = sm(E)
        sel_a, sel_b = sm(TILES * E), sm(TILES * E)
        gates = sm(2 * TILES)
        cnt16 = sm(E)
        scan = [sm(2 * E), sm(2 * E)]
        mod_cols = sm(32).rearrange("p (k s c) -> p k s c", k=2, s=2)
        gain_col = sm(DC)
        lat_g = sm(5)
        idx_i = ints[:, 0:T_MAX + 1]
        eid_i = ints[:, T_MAX + 1:2 * T_MAX + 1]
        slot_i = ints[:, 2 * T_MAX + 1:2 * T_MAX + 1 + 2 * TILES]
        idx_cur = ints[:, 2 * T_MAX + 1 + 2 * TILES:2 * T_MAX + 3 + 2 * TILES]
        pairs_i = ints[:, 2 * T_MAX + 3 + 2 * TILES:2 * T_MAX + 4 + 2 * TILES]

        def bc(ap, axis, n):
            u = ap.unsqueeze(axis)
            shape = list(u.shape)
            shape[axis] = n
            return u.broadcast_to(shape)

        def bank(k, words=512, parts=P):
            return psum[0:parts, k, 0:words]

        def banks(k, n):
            return psum[:, k:k + n, :].rearrange("p b n -> p (b n)")

        w_loaded = [sem(f"w_loaded{s}") for s in range(SLOTS)]
        w_loaded_in = [sem(f"w_loaded_in{u}") for u in range(2)]
        w_used = [sem(f"w_used{s}") for s in range(SLOTS)]
        names = """phase link_dve link_act ld_const ld_cond ld_x ld_hy ld_filt ld_taps ld_dft ld_rows ld_rows2 ld_lat ld_cols
            silu_c f_pre f_arg f_sin f_w3 f_h f_k f_kdone
            ad_done ad_ready ad_ld0 ad_ld1 ad_st0 ad_st1 
            n_ssq n_var n_std n_h n_T n_hT n_st0 n_st1 
            ip_pm ip_z ip_u ip_c ip_vg ip_vt ip_ve
            cv_x cv_y cv_xfree cv_inv cv_yt op_y op_x x_done
            l_down l_ssq l_var l_std l_lat l_T l_TT l_up l_hssq l_hvar l_hstd l_hn l_v l_hr l_HT l_hevac
            a_s a_m a_p a_pn a_pT a_PT a_o a_ot pool_st ordered""".split()
        S = {n: sem(n) for n in names}
        once = {n: sem(n) for n in "logits aff sel pos hot idxp idx eid rw ld ga0 ga1 comb".split()}
        moe_names = "h13 silu hid hT hidT y yev xT xTe xg0 xg1 cur yst".split()
        e_loaded = [[sem(f"expert_loaded{s}_{l}") for s in range(SLOTS)] for l in range(DEPTH)]
        e_used = [[sem(f"expert_used{s}_{l}") for s in range(SLOTS)] for l in range(DEPTH)]
        M = [once | {n: sem(f"{n}_{l}") for n in moe_names} for l in range(DEPTH)]

        loads, landed = [0] * SLOTS, [0] * SLOTS
        W, LANDED = {}, {}
        before_experts = []

        def book(name, s, times=1, own_sem=False):
            W[name], LANDED[name] = (s, loads[s]), landed[s]
            loads[s] += times
            landed[s] += 0 if own_sem else times

        for u in range(4):
            book(f"ada_first{u}", u)
        for u in range(2):
            book(f"hy_in_{u}", 4 + u, 4, True)
            book(f"ada0_{u}", u, 4)
            book(f"ada1_{u}", 2 + u, 4)
        for k, s in enumerate((4, 0, 2, 5)):
            book(f"ada_last{k}", s)
        book("hy_out0", 1)
        book("hy_out1", 0)

        def book_moe(l):
            for w, s in ((1, 3), (3, 4), (2, 5)):
                book(f"sh{w}_{l}", s)
            before_experts.append([n + 1 for n in loads])

        book_moe(0)
        for name, s in (("wqd", 0), ("wkvd", 1), ("wkvu", 2), ("wqu0", 3), ("wqu1", 4), ("wo0", 5), ("wo1", 2)):
            book(name, s)
        book_moe(1)

        def wait_piece(pe, name, i=0):
            pe.wait_ge(w_loaded[W[name][0]], 16 * (LANDED[name] + 1) + 16 * i)

        def piece(name, words=SLOT_W):
            return slot(W[name][0], words)

        def freed(ins, name):
            ins.then_inc(w_used[W[name][0]], 1)

        def looped_pairs(eng, l):
            eng.wait_ge(M[l]["eid"], l + 1)
            return eng.value_load(pairs_i[0:1, 0:1], min_val=1, max_val=(EXPERT_TILES[l] - 2) // 2)

        def norm_places(k):
            if k == 0:
                return None, None, B(0, 3072, 1024), B(3, 1024, 2048)
            if k == 1:
                return B(4, 0, 4096), B(2, 0, 1024), B(2, 1024, 1024), B(2, 2048, 2048)
            return B(1, 0, 4096), B(2, 0, 1024), B(2, 1024, 1024), B(2, 2048, 2048)

        NORM_TILES = [4, 4, 4, 2]
        NORM_BASE = [0, 4, 8, 12]
        hT = B(0, 0, 4096).rearrange("p (c t) -> p c t", c=DC)

        mod_first = [B(4, 512 * (n // 2), 512)[32 * (n % 2):32 * (n % 2) + 2, :] for n in range(4)]
        mod_piece = [mod_t[32 * b:32 * b + 2, :] for b in range(2)]
        mod_psum = [psum[32 * b:32 * b + 2, 6, :] for b in range(2)]
        hy_rows = hy_rows_t[:, :]
        f_own = slot(5)
        f_rn, f_bias = f_own[:, 0:D], f_own[:, D:2 * D]
        f_pos, f_arg, f_n = (f_own[:, 2 * D + 256 * k:2 * D + 256 * (k + 1)] for k in range(3))
        f_h = [f_own[:, 2 * D + 256 * (3 + k):2 * D + 256 * (4 + k)] for k in range(3)]
        f_w1, f_par = f_own[:, 3584:3584 + HID], f_own[:, 3584 + 3 * HID:3584 + 3 * HID + 4]
        f_w2 = [f_own[:, 3584 + HID * (1 + k):3584 + HID * (2 + k)] for k in range(2)]
        f_hfb = B(1, 0, 4096).rearrange("p (t n) -> p t n", t=2)
        f_mag = B(2, 0, 4096).rearrange("p (t n) -> p t n", t=2)
        f_sd = B(2, 0, 4096).rearrange("p (k t n) -> p k t n", k=2, t=2)
        f_decay = B(3, 0, 2048).rearrange("p (t n) -> p t n", t=2)
        f_w3 = B(3, 2048, 2048)
        f_K = B(4, 0, 4096).rearrange("p (k n) -> p k n", k=4)
        N_FILT = 8
        x0T = B(1, 0, 4096).rearrange("p (m t) -> p m t", m=8)
        vgtok = B(2, 0, 4096).rearrange("p (t d) -> p t d", d=D)
        ip_u = B(3, 0, 1548).rearrange("p (o s t) -> p o s t", o=3, s=2)
        ip_t = B(3, 1548, 1536).rearrange("p (o s t) -> p o s t", o=3, s=2)
        ip_vgb = B(3, 3084, 512)
        cv_Y = B(0, 0, 4096).rearrange("p (k f n) -> p k f n", k=2, f=4)
        cv_t = B(3, 3072, 1024).rearrange("p (k n) -> p k n", k=2)
        op_rows = B(3, 0, 3072).rearrange("p (k n) -> p k n", k=3)
        op_t = B(0, 0, 1024).rearrange("p (k n) -> p k n", k=2)
        moe_S = B(1, 0, 4096).rearrange("p (t d) -> p t d", d=D)
        moe_xg = [B(2, b * D, D) for b in range(2)]
        moe_xT = [B(2, (2 + b) * D, D).rearrange("p (c n) -> p c n", c=DC) for b in range(2)]
        moe_hid = [B(3, b * FF, FF) for b in range(2)]
        moe_hidT = [B(3, (2 + b) * FF, FF).rearrange("p (c n) -> p c n", c=FC) for b in range(2)]
        moe_y = B(3, 2048, D)
        moe_rw = B(3, 3072, 128).rearrange("p (c e) -> p c e", c=DC)
        moe_aff = B(3, 3200, 64)
        moe_sel = B(3, 3264, 64).rearrange("p (t e) -> p t e", e=E)
        moe_g2 = B(4, 0, 2048).rearrange("p (s d) -> p s d", s=2)
        moe_hot = B(4, 2048, 1024).rearrange("p (q n) -> p q n", q=2 * TILES)
        moe_hit = B(4, 3072, 2 * TILES * (T_MAX + 1)).rearrange("p (q t) -> p q t", t=T_MAX + 1)
        moe_cmp = B(4, 3272, 384)
        moe_r = [B(4, 3656 + 64 * k, 64) for k in range(3)]
        moe_pair = B(4, 3848, 96).rearrange("p (g s) -> p g s", s=6)
        moe_g4 = [B(4, 3944 + 16 * k, 16) for k in range(3)]
        moe_slot = B(4, 3992, 4 * TILES)
        moe_gat = B(0, 0, 4096).rearrange("p (b k d) -> p b k d", b=2, k=2)
        a_V = B(1, 0, 4096).rearrange("p (t d) -> p t d", d=D)
        kTn = B(2, 0, 4096).rearrange("p (h t) -> p h t", h=H)
        kTr = B(3, 0, 2048).rearrange("p (h t) -> p h t", h=H // 2)
        qTn = B(3, 2048, 2048).rearrange("p (h t) -> p h t", h=H)
        qTr = B(4, 0, 1024).rearrange("p (h t) -> p h t", h=H // 2)
        mla_hn = B(4, 1024, H * NOPE).rearrange("p (h d) -> p h d", h=H)
        mla_hr = B(4, 2048, H * ROPE).rearrange("p (h d) -> p h d", h=H)
        mla_t, mla_sq = B(4, 2560, 1024), B(4, 3584, 384)
        mla_lat, mla_latT = dft_t[:, 0:384], dft_t[:, 384:768].rearrange("p (c n) -> p c n", c=3)
        mla_g = dft_t[:, 768:768 + 2 * QK]
        mla_pe = [dft_t[:, 1152 + k * ROPE:1152 + (k + 1) * ROPE] for k in range(2)]
        o_gate = dft_t[:, 768:1792]
        hssq, hvar, hstd, hrstd = (dft_t[:, 1792 + 8 * k:1800 + 8 * k] for k in range(4))
        a_nm, a_sum = dft_t[:, 1824:1828], dft_t[:, 1828:1832]
        OT = B(0, 0, 2048).rearrange("p (h t) -> p h t", h=H)
        a_PT = B(0, 2048, 2048).rearrange("p (b k t) -> p b k t", b=2, k=4)
        a_P = B(4, 1024, 2048).rearrange("p (u n) -> p u n", u=4)
        o_t = B(4, 3072, 1024).rearrange("p (k n) -> p k n", k=2)

        def mod_row(l, stream, k):
            return mod_d[l, stream:stream + 1, k * D:(k + 1) * D].partition_broadcast(P)

        def row(ap):
            return ap.rearrange("(o n) -> o n", o=1).partition_broadcast(P)

        block = ctx.enter_context(nc.Block())

        ended = {}

        def end_phase(eng, name):
            ended.setdefault(name, len(ended) + 1)
            eng.drain().then_inc(S["phase"], 1)
            eng.wait_ge(S["phase"], 3 * ended[name])

        def mod_stored(eng, pieces):
            for b in range(2):
                eng.wait_ge(S[f"ad_st{b}"], 8 * pieces)

        def load_cols(eng, l):
            for s in range(2):
                for k, which in enumerate((SCALE1, SHIFT1)):
                    eng.dma_start(mod_cols[:, k, s, :], mod_d[l, s, which * D:(which + 1) * D]
                                  .rearrange("(p c) -> p c", c=DC)).then_inc(S["ld_cols"], 16)
            eng.dma_start(gain_col, a["norm_mix_g"][l].rearrange("(p c) -> p c", c=DC)).then_inc(S["ld_cols"], 16)

        @block.sync
        def _(sp):
            def load(name, dst_words, src, i=0, shape=None):
                s, n = W[name]
                sp.wait_ge(w_used[s], n + 1 + i)
                dst = slot(s, dst_words)
                if shape:
                    dst = dst.rearrange(shape[0], **shape[1])
                sp.dma_start(dst, src).then_inc(w_loaded[s], 16)

            def ada(l, q):
                return a["ada_w"][l, :, bass.ds(q * 512, 512)].rearrange("(p c) n -> p c n", c=DC)

            k8 = ("p (c n) -> p c n", {"c": DC})
            sp.dma_start(cst[:, :], a["c_small"]).then_inc(S["ld_const"], 16)
            for s, v in enumerate((a["c"][0], a["c_ctx"])):
                sp.dma_start(cT[:, 8 * s:8 * s + 8], v.rearrange("(p c) -> p c", c=DC)).then_inc(S["ld_cond"], 16)
            dma = sp.dma_start
            dma(f_pos[0:EMB, :], a["c_pos"]).then_inc(S["ld_filt"], 16)
            dma(f_w1[0:EMB, :], a["hy_f_w1"][0]).then_inc(S["ld_filt"], 16)
            dma(f_par[0:HID, 0:1], a["hy_f_b1"][0].rearrange("(n o) -> n o", o=1)).then_inc(S["ld_filt"], 16)
            dma(f_par[0:HID, 3:4], a["hy_sin_freq"][0].rearrange("(n o) -> n o", o=1)).then_inc(S["ld_filt"], 16)
            for k in range(2):
                dma(f_w2[k][0:HID, :], a["hy_f_w2"][0, k]).then_inc(S["ld_filt"], 16)
                dma(f_par[0:HID, 1 + k:2 + k], a["hy_f_b2"][0, k].rearrange("(n o) -> n o", o=1)
                    ).then_inc(S["ld_filt"], 16)
            for q, (w, k) in enumerate((("hy_in_b", 24), ("hy_conv_w", 72), ("hy_conv_b", 24))):
                at = (0, 24, 96)[q]
                src = a[w][0].rearrange("(r n) -> r n", n=P) if w != "hy_conv_w" else \
                    a[w][0].rearrange("k (r n) -> (k r) n", n=P)
                dma(hy_rows[at:at + k, :], src).then_inc(S["ld_hy"], 16)
            for u in range(4):
                load(f"ada_first{u}", 4096, ada(0, u), 0, k8)
                if u == 0:
                    dma(f_w3[0:HID, :], a["hy_f_w3"][0]).then_inc(S["ld_taps"], 16)
                    dma(f_decay, a["c_decay"].rearrange("(t p) d -> p t d", p=P)).then_inc(S["ld_taps"], 16)
                if u == 2:
                    dma(X[:, 0:2, :], a["x"][0].rearrange("(t p) d -> p t d", p=P)).then_inc(S["ld_x"], 16)
                    dma(X[:, 2:4, :], a["ctx"][0].rearrange("(t p) d -> p t d", p=P)).then_inc(S["ld_x"], 16)
            dma(dft_t[:, :], a["c_dft"]).then_inc(S["ld_dft"], 16)
            dma(f_bias, row(a["hy_f_bias"][0])).then_inc(S["ld_dft"], 16)
            mod_stored(sp, 4)
            load_cols(sp, 0)
            with sp.Fori(0, 4) as i:
                for u in range(2):
                    s, n = W[f"hy_in_{u}"]
                    sp.wait_ge(w_used[s], n + 1 + i)
                    src = a["hy_in_w"][0].rearrange("(p c) (q m n) -> p c q m n", c=DC, q=3, n=P)
                    dst = slot(s, 3072).rearrange("p (q c n) -> p q c n", q=3, c=DC)
                    for q in range(3):
                        sp.dma_start(dst[:, q], src[:, :, q, bass.ds(2 * i + u, 1), :].rearrange("p c o n -> p c (o n)")
                                     ).then_inc(w_loaded_in[u], 16)
                    load(f"ada0_{u}", 4096, ada(0, 4 + 2 * i + u), i, k8)
                    load(f"ada1_{u}", 4096, ada(1, 1 + 2 * i + u), i, k8)
            for k in range(4):
                load(f"ada_last{k}", 4096, ada(1, (0, 9, 10, 11)[k]), 0, k8)
            for n in range(2):
                load(f"hy_out{n}", 4096, a["hy_out_w"][0, :, n * 512:(n + 1) * 512]
                     .rearrange("(m p) n -> p m n", p=P), 0, k8)

            def experts(l):
                up = "(p c) n -> p c n"
                load(f"sh1_{l}", 4096, a["sh_w1"][l].rearrange(up, c=DC), 0, k8)
                load(f"sh3_{l}", 4096, a["sh_w3"][l].rearrange(up, c=DC), 0, k8)
                load(f"sh2_{l}", 4096, a["sh_w2"][l].rearrange(up, c=FC), 0, ("p (c n) -> p c n", {"c": FC}))
                pairs = looped_pairs(sp, l)

                def tile_weights(j, b, i=None):
                    e = sp.value_load(eid_i[0:1, bass.ds(j, 1)], min_val=0, max_val=E - 1)
                    for k, (w, c) in enumerate(((1, DC), (3, DC), (2, FC))):
                        s = 3 * b + k
                        if i is None:
                            sp.wait_ge(w_used[s], before_experts[l][s])
                        else:
                            sp.wait_ge(e_used[l][s], i + 1)
                        src = a[f"exp_w{w}"][l, bass.ds(e, 1), :, :].rearrange("o (p c) n -> p (o c) n", c=c)
                        sp.dma_start(slot(s).rearrange("p (c n) -> p c n", c=c), src).then_inc(e_loaded[l][s], 16)

                for j in range(2):
                    tile_weights(j, j)
                with sp.Fori(0, pairs) as i:
                    for b in range(2):
                        tile_weights(2 * i + 2 + b, b, i)
                return pairs

            pairs = experts(0)
            for s in range(3):
                sp.wait_ge(e_used[0][s], pairs + 1)
            load("wqd", 3072, a["mla_wq_down"][0].rearrange("(p c) n -> p c n", c=DC), 0, k8)
            load("wkvd", 2560, a["mla_wkv_down"][0].rearrange("(p c) n -> p c n", c=DC), 0, k8)
            load("wkvu", 4096, a["mla_wkv_up"][0].rearrange("(c p) n -> p c n", p=P), 0,
                 ("p (c n) -> p c n", {"c": 2}))
            for s in range(3, SLOTS):
                sp.wait_ge(e_used[0][s], pairs + 1)
            for b in range(2):
                sp.wait_ge(M[0][f"ga{b}"], 64)
            for n in range(2):
                load(f"wqu{n}", 2304, a["mla_wq_up"][0, :, n * 768:(n + 1) * 768].rearrange("(c p) n -> p c n", p=P),
                     0, ("p (c n) -> p c n", {"c": 3}))
            for n in range(2):
                load(f"wo{n}", 4096, a["mla_wo"][0, :, n * 512:(n + 1) * 512].rearrange("(h p) n -> p h n", p=P), 0, k8)
            experts(1)

        @block.tensor
        def _(pe):
            mm = pe.matmul
            for s in range(SLOTS - 1):
                pe.sem_inc(w_used[s], 1)

            pe.wait_ge(S["ld_const"], 16)
            pe.wait_ge(S["ld_hy"], 48)
            pe.transpose(bank(7, 120), hy_rows[0:120, :], ident[0:120, 0:120]).then_inc(S["f_pre"], 1)
            def filter_layer(k):
                if k == 0:
                    pe.wait_ge(S["ld_filt"], 16 * N_FILT)
                    mm(bank(0, SEQ, HID), f_w1[0:EMB, :], f_pos[0:EMB, :], start=True, stop=True
                       ).then_inc(S["f_pre"], 1)
                else:
                    pe.wait_ge(S["f_sin"], k)
                    mm(bank(k, SEQ, HID), f_w2[k - 1][0:HID, :], f_h[k - 1][0:HID, :], start=True, stop=True
                       ).then_inc(S["f_pre"], 1)

            def filter_taps():
                pe.wait_ge(S["f_sin"], 3)
                pe.wait_ge(S["ld_taps"], 32)
                for j in range(8):
                    t, n = j % 2, j // 2
                    if j >= 4:
                        pe.wait_ge(S["f_h"], j - 3)
                    mm(bank(j % 4), f_h[2][0:HID, t * P:(t + 1) * P], f_w3[0:HID, n * 512:(n + 1) * 512],
                       start=True, stop=True).then_inc(S["f_w3"], 1)

            def filter_norm():
                pe.wait_ge(S["f_sin"], 4)
                for half in range(2):
                    for k in range(4):
                        t, side = k % 2, k // 2
                        m = mm(bank(4 + half), C(C_ONES, P),
                               f_mag[:, t, side * D + half * 512:side * D + half * 512 + 512],
                               start=(k == 0), stop=(k == 3))
                m.then_inc(S["f_w3"], 1)

            def filter_transform():
                pe.wait_ge(S["f_h"], 9)
                pe.wait_ge(S["ld_dft"], 32)
                for j in range(8):
                    comp, ft, half = j // 4, (j // 2) % 2, j % 2
                    if j >= 4:
                        pe.wait_ge(S["f_kdone"], j - 3)
                    for t in range(2):
                        m = mm(bank(j % 4), dft_fwd[:, t, comp * SEQ + ft * P:comp * SEQ + ft * P + P],
                               f_sd[:, comp, t, half * 512:half * 512 + 512], start=(t == 0), stop=(t == 1))
                    m.then_inc(S["f_k"], 1)

            def ada_piece(name, n, b, i=0):
                if not isinstance(n, int) or n >= 2:
                    pe.wait_ge(S["ad_ready"], n - 1)
                wait_piece(pe, name, i)
                w = piece(name).rearrange("p (c n) -> p c n", c=DC)
                for c in range(DC):
                    m = mm(mod_psum[b], scT[:, c, :], w[:, c, :], start=(c == 0), stop=(c == DC - 1))
                m.then_inc(S["ad_done"], 1)
                pe.drain().then_inc(w_used[W[name][0]], 1)

            def norm_turn(k):
                h = norm_places(k)[3]
                for t in range(NORM_TILES[k]):
                    g = NORM_BASE[k] + t
                    pe.wait_ge(S["n_h"], g + 1)
                    if t >= 2:
                        pe.wait_ge(S["n_hT"], g - 1)
                    for c in range(DC):
                        m = pe.transpose(banks(2 * (t % 2), 2)[:, c * P:(c + 1) * P],
                                         h[:, (t % 2) * D + c:(t % 2) * D + D:DC], ident)
                    m.then_inc(S["n_T"], 1)

            filter_layer(0)
            pe.wait_ge(S["silu_c"], 1)
            for n in range(4):
                ada_piece(f"ada_first{n}", n, n % 2)
                if n < 2:
                    filter_layer(n + 1)
            filter_taps()
            pe.wait_ge(S["f_h"], 7)
            norm_turn(0)
            filter_norm()
            pe.wait_ge(S["n_hT"], NORM_TILES[0])
            filter_transform()
            end_phase(pe, "start")
            pe.sem_inc(w_used[5], 1)

            with pe.Fori(0, 4) as i:
                for u in range(2):
                    m_ = 2 * i + u
                    name = f"hy_in_{u}"
                    w = piece(name, 3072).rearrange("p (q c n) -> p q c n", q=3, c=DC)
                    pe.wait_ge(w_loaded_in[u], 48 * i + 48)
                    for o, part in enumerate((1, 2, 0)):
                        pe.wait_ge(S["ip_u"], 3 * m_ + o + 1)
                        for c in range(DC):
                            m = mm(bank(3 * u + o), w[:, part, c, :], hT[:, c, :], start=(c == 0), stop=(c == DC - 1))
                        m.then_inc(S["ip_z"], 1)
                    pe.drain().then_inc(w_used[W[name][0]], 1)
                    ada_piece(f"ada0_{u}", 4 * i + 2 * u + 4, 0, i)
                    pe.wait_ge(S["ip_vg"], m_ + 1)
                    pe.wait_ge(S["ip_ve"], m_ + 1)
                    for t in range(TILES):
                        m = pe.transpose(bank(7)[:, t * P:(t + 1) * P], ip_vgb[:, t * P:(t + 1) * P], ident)
                    m.then_inc(S["ip_vt"], 1)
                    ada_piece(f"ada1_{u}", 4 * i + 2 * u + 5, 1, i)
            end_phase(pe, 3)

            def conv_back(k):
                s, half = k % 2, k // 2
                pe.wait_ge(S["cv_y"], k + 1)
                for m4 in range(4):
                    n = 4 * k + m4
                    if n >= 2:
                        pe.wait_ge(S["cv_yt"], n - 1)
                    for f in range(4):
                        m = mm(bank(4 + m4 % 2, SEQ), cv_Y[:, k % 2, f, m4 * P:(m4 + 1) * P], dft_inv[:, f, :],
                               start=(f == 0), stop=(f == 3))
                    m.then_inc(S["cv_inv"], 1)

            for k in range(4):
                s, half = k % 2, k // 2
                if k >= 1:
                    pe.wait_ge(S["cv_xfree"], k)
                for f in range(4):
                    for t in range(2):
                        m = mm(bank(f), dft_fwd[:, t, f * P:(f + 1) * P], vgtok[:, 2 * s + t, half * 512:half * 512 + 512],
                               start=(t == 0), stop=(t == 1))
                m.then_inc(S["cv_x"], 1)
                ada_piece(f"ada_last{k}", 20 + k, k % 2)
                if k >= 1:
                    conv_back(k - 1)
            conv_back(3)
            end_phase(pe, 4)

            def project(names, lhs, tiles, done, free):
                for n in range(2):
                    for t in range(tiles):
                        j = n * tiles + t
                        if t == 0:
                            wait_piece(pe, names[n])
                        if j >= 4:
                            pe.wait_ge(free, j - 3)
                        w = piece(names[n]).rearrange("p (c n) -> p c n", c=DC)
                        for c in range(DC):
                            m = mm(bank(j % 4), lhs[:, c, t * P:(t + 1) * P], w[:, c, :], start=(c == 0), stop=(c == 7))
                        m.then_inc(done, 1)
                    pe.drain().then_inc(w_used[W[names[n]][0]], 1)

            project(("hy_out0", "hy_out1"), x0T, TILES, S["op_y"], S["op_x"])
            pe.wait_ge(S["op_x"], 2 * TILES)
            norm_turn(1)
            end_phase(pe, 6)

            def moe(l):
                m_, nt, nx = M[l], TOKEN_TILES[l], EXPERT_TILES[l]
                xT = moe_xT
                pe.wait_ge(m_["rw"], 16 * l + 16)
                for t in range(nt):
                    for c in range(DC):
                        m = mm(bank(7)[:, t * E:(t + 1) * E], hT[:, c, t * P:(t + 1) * P], moe_rw[:, c, :],
                               start=(c == 0), stop=(c == DC - 1))
                m.then_inc(m_["logits"], 1)

                def shared_piece(w, last):
                    name = f"sh{w}_{l}"
                    return W[name][0], w_loaded[W[name][0]], 16 * (LANDED[name] + 1), w_used[W[name][0]] if last else None

                def expert_piece(w, b, i):
                    s = 3 * b + (1, 3, 2).index(w)
                    return s, e_loaded[l][s], 16 * i + 16, e_used[l][s]

                def up(pieces, lhs):
                    for k, (s, loaded, count, used) in enumerate(pieces):
                        pe.wait_ge(loaded, count)
                        w = slot(s).rearrange("p (c n) -> p c n", c=DC)
                        for c in range(DC):
                            m = mm(bank(k), lhs(c), w[:, c, :], start=(c == 0), stop=(c == DC - 1))
                        if used and k == 0:
                            m.then_inc(used, 1)
                    m.then_inc(m_["h13"], 1)
                    if used:
                        pe.drain().then_inc(used, 1)

                def down(g, b, piece_, first=False):
                    s, loaded, count, used = piece_
                    pe.wait_ge(m_["hidT"], g + 1)
                    if not first:
                        pe.wait_ge(m_["yev"], g)
                    pe.wait_ge(loaded, count)
                    w = slot(s).rearrange("p (c n) -> p c n", c=FC)
                    for n in range(2):
                        for c in range(FC):
                            m = mm(bank(5 + n), moe_hidT[b][:, c, :], w[:, c, n * 512:(n + 1) * 512],
                                   start=(c == 0), stop=(c == FC - 1))
                    m.then_inc(m_["y"], 1)
                    if used:
                        pe.drain().then_inc(used, 1)

                def turn_hidden(g, b):
                    pe.wait_ge(m_["hid"], g + 1)
                    for c in range(FC):
                        m = pe.transpose(bank(4)[:, c * P:(c + 1) * P], moe_hid[b][:, c::FC], ident)
                    m.then_inc(m_["hT"], 1)

                def turn_tokens(j, b, count):
                    pe.wait_ge(m_[f"xg{b}"], count)
                    for c in range(DC):
                        m = pe.transpose(banks(2, 2)[:, c * P:(c + 1) * P], moe_xg[b][:, c::DC], ident)
                    m.then_inc(m_["xT"], 1)

                for t in range(nt):
                    up([shared_piece(w, t == nt - 1) for w in (1, 3)], lambda c, t=t: hT[:, c, t * P:(t + 1) * P])
                    if t == 0:
                        pe.wait_ge(m_["sel"], l + 1)
                        for q in range(nt + 1):
                            for r in range(min(q, nt - 1) + 1):
                                lhs = C(C_UPPER, P) if r == q else C(C_ONES, P)
                                m = mm(bank(7)[:, 64 + q * E:64 + (q + 1) * E], lhs, moe_sel[:, r, :],
                                       start=(r == 0), stop=(r == min(q, nt - 1)))
                        m.then_inc(m_["pos"], 1)
                    if t == 1:
                        pe.wait_ge(m_["hot"], l + 1)
                        for q in range(2 * nt):
                            m = mm(bank(7)[:, 192:192 + nx], moe_hot[:, q, :], moe_hit[:, q, 0:nx],
                                   start=(q == 0), stop=(q == 2 * nt - 1))
                        m.then_inc(m_["idxp"], 1)
                    if t >= 1:
                        down(t - 1, (t - 1) % 2, shared_piece(2, False), t == 1)
                    turn_hidden(t, t % 2)
                turn_tokens(0, 0, 16)

                def step(j, b, i, count):
                    pe.wait_ge(m_["xTe"], j + 1)
                    up([expert_piece(w, b, i) for w in (1, 3)], lambda c: xT[b][:, c, :])
                    turn_tokens(j + 1, 1 - b, count)

                step(0, 0, 0, 16)
                down(nt - 1, 1, shared_piece(2, True))
                turn_hidden(nt, 0)
                step(1, 1, 0, 32)
                down(nt, 0, expert_piece(2, 0, 0))
                turn_hidden(nt + 1, 1)
                pairs = looped_pairs(pe, l)
                with pe.Fori(0, pairs) as i:
                    step(2 * i + 2, 0, i + 1, 16 * i + 32)
                    down(2 * i + nt + 1, 1, expert_piece(2, 1, i))
                    turn_hidden(2 * i + nt + 2, 0)
                    step(2 * i + 3, 1, i + 1, 16 * i + 48)
                    down(2 * i + nt + 2, 0, expert_piece(2, 0, i + 1))
                    turn_hidden(2 * i + nt + 3, 1)
                down(2 * pairs + nt + 1, 1, expert_piece(2, 1, pairs))

            moe(0)
            norm_turn(2)
            end_phase(pe, 8)

            def latent(n):
                is_q, tile = n >= 4, n % 4
                name, width, chunks = ("wqd", Q_LORA, 3) if is_q else ("wkvd", KV_LORA + ROPE, 2)
                w = piece(name, DC * width).rearrange("p (c n) -> p c n", c=DC)
                wait_piece(pe, name)
                for c in range(DC):
                    m = mm(bank(0, width), hT[:, c, tile * P:(tile + 1) * P], w[:, c, :],
                           start=(c == 0), stop=(c == DC - 1))
                m.then_inc(S["l_down"], 1)
                if n >= 2:
                    pe.wait_ge(S["l_hevac"], n - 1)
                pe.wait_ge(S["l_lat"], n + 1)
                for c in range(chunks):
                    m = pe.transpose(bank(1)[:, c * P:(c + 1) * P], mla_lat[:, c * P:(c + 1) * P], ident)
                m.then_inc(S["l_T"], 1)

            def heads_up(n):
                is_q = n >= 4
                chunks = 3 if is_q else 2
                pe.wait_ge(S["l_TT"], n + 1)
                if n:
                    pe.wait_ge(S["l_hn"], n)
                for q in range(4):
                    if is_q:
                        name, width = f"wqu{q // 2}", 384
                        w = piece(name, 2304).rearrange("p (c n) -> p c n", c=3)[:, :, (q % 2) * 384:(q % 2) * 384 + 384]
                    else:
                        name, width = "wkvu", 512
                        w = piece(name).rearrange("p (c n) -> p c n", c=2)[:, :, q * 512:(q + 1) * 512]
                    wait_piece(pe, name)
                    for c in range(chunks):
                        m = mm(bank(2 + q, width), mla_latT[:, c, :], w[:, c, :], start=(c == 0), stop=(c == chunks - 1))
                m.then_inc(S["l_up"], 1)

            def heads_turn(n):
                pe.wait_ge(S["l_hr"], n + 1)
                for h in range(H):
                    pe.transpose(banks(6, 2)[:, h * P:(h + 1) * P], mla_hn[:, h, :], ident)
                for h in range(H // 2):
                    m = pe.transpose(bank(1)[:, h * P:(h + 1) * P], B(4, 2048 + h * P, P), ident)
                m.then_inc(S["l_HT"], 1)

            latent(0)
            heads_up(0)
            for n in range(6):
                if n < 5:
                    latent(n + 1)
                    heads_up(n + 1)
                heads_turn(n)
            pe.drain().then_inc(w_used[W["wqd"][0]], 1)
            for name in ("wkvd", "wkvu", "wqu0", "wqu1"):
                pe.sem_inc(w_used[W[name][0]], 1)
            end_phase(pe, 9)

            units = [(h, t) for h in range(H) for t in range(LAT_TILES)]

            def scores(u):
                h, t = units[u]
                r = 64 * (h % 2)
                if u >= 4:
                    pe.wait_ge(S["a_p"], u - 3)
                bk = (0, 1, 6, 7)[u % 4]
                mm(bank(bk), qTn[:, h, t * P:(t + 1) * P], kTn[:, h, :], start=True, stop=False)
                mm(bank(bk), qTr[r:r + 64, h // 2, t * P:(t + 1) * P], kTr[r:r + 64, h // 2, :],
                   start=False, stop=True).then_inc(S["a_s"], 1)

            def turn_probs(u):
                pe.wait_ge(S["a_pn"], u + 1)
                if u >= 2:
                    pe.wait_ge(S["a_PT"], u - 1)
                for k in range(4):
                    m = pe.transpose(bank(2 + u % 2)[:, k * P:(k + 1) * P], a_P[:, u % 4, k * P:(k + 1) * P], ident)
                m.then_inc(S["a_pT"], 1)

            def values(h):
                pe.wait_ge(S["a_PT"], 2 * h + 2)
                if h >= 2:
                    pe.wait_ge(S["a_ot"], h - 1)
                for k in range(4):
                    m = mm(bank(4 + h % 2, SEQ), a_V[:, k, h * P:(h + 1) * P], a_PT[:, h % 2, k, :],
                           start=(k == 0), stop=(k == 3))
                m.then_inc(S["a_o"], 1)

            for u in range(2):
                scores(u)
            for u in range(16):
                if u + 2 < 16:
                    scores(u + 2)
                turn_probs(u)
                if u >= 2 and u % 2 == 0:
                    values(u // 2 - 1)
            values(7)
            end_phase(pe, 10)
            for n in range(2):
                wait_piece(pe, f"wo{n}")
                w = piece(f"wo{n}").rearrange("p (c n) -> p c n", c=DC)
                for t in range(LAT_TILES):
                    for h in range(H):
                        m = mm(bank(2 * n + t), OT[:, h, t * P:(t + 1) * P], w[:, h, :], start=(h == 0), stop=(h == 7))
                    m.then_inc(S["op_y"], 1)
                pe.drain().then_inc(w_used[W[f"wo{n}"][0]], 1)
            pe.wait_ge(S["op_x"], 2 * TILES + 2 * LAT_TILES)
            norm_turn(3)
            end_phase(pe, 12)
            moe(1)

        @block.scalar
        def _(act):
            A = nc.scalar.activation
            link = Link(act, S["link_act"])
            dma = act.dma_start

            dma(router_b, row(a["router_bias"])).then_inc(S["ld_lat"], 16)
            for k, (w, c) in enumerate([("mla_q_norm_g", c) for c in range(3)] + [("mla_kv_norm_g", c) for c in range(2)]):
                dma(lat_g[:, k:k + 1], a[w][0, c * P:(c + 1) * P].rearrange("(p o) -> p o", o=1)
                    ).then_inc(S["ld_lat"], 16)

            act.wait_ge(S["ld_cond"], 32)
            A(scT, cT.rearrange("p (s c) -> p c s", s=2), ACT.Silu).then_inc(S["silu_c"], 1)

            def load_rows(k):
                l = k // 2
                rows, gain = norm_places(k)[:2]
                for s in range(2 if l == 0 else 1):
                    dma(rows[:, 2 * s * D:(2 * s + 1) * D], mod_row(l, s, SCALE2)).then_inc(S["ld_rows"], 16)
                    dma(rows[:, (2 * s + 1) * D:(2 * s + 2) * D], mod_row(l, s, SHIFT2)).then_inc(S["ld_rows"], 16)
                dma(gain, row(a["norm_ffn_g"][l])).then_inc(S["ld_rows"], 16)

            def square(k, t):
                if k:
                    done, before = {1: (S["x_done"], 0), 2: (M[0]["comb"], 0), 3: (S["x_done"], TILES)}[k]
                    act.wait_ge(done, before + t + 1)
                link(A(norm_places(k)[2], X[:, t, :], ACT.Square, accum_out=ssq[:, t:t + 1]))

            def norm_root(k):
                nt = NORM_TILES[k]
                if k != 2:
                    for t in range(nt):
                        square(k, t)
                act.drain().then_inc(S["n_ssq"], 1)
                act.wait_ge(S["n_var"], k + 1)
                A(std[:, 0:nt], var[:, 0:nt], ACT.Sqrt).then_inc(S["n_std"], 1)

            def norm_turned(k):
                h, nt = norm_places(k)[3], NORM_TILES[k]
                for t in range(nt):
                    g = NORM_BASE[k] + t
                    if k % 2 == 1:
                        act.wait_ge(S["n_h"], g + 1)
                        dma(h2_d[k // 2][t * P:(t + 1) * P, :], h[:, (t % 2) * D:(t % 2 + 1) * D]
                            ).then_inc(S[f"n_st{t % 2}"], 16)
                    act.wait_ge(S["n_T"], g + 1)
                    A(hT[:, :, t * P:(t + 1) * P], banks(2 * (t % 2), 2).rearrange("p (c n) -> p c n", n=P), ACT.Copy
                      ).then_inc(S["n_hT"], 1)

            def load_router(l):
                dma(moe_rw, a["router_w"].rearrange("(p c) e -> p c e", c=DC)).then_inc(M[l]["rw"], 16)

            def norm(k):
                norm_root(k)
                norm_turned(k)

            for k in range(3):
                act.wait_ge(S["f_arg"], k + 1)
                A(f_h[k][0:HID, :], f_arg[0:HID, :], ACT.Sin).then_inc(S["f_sin"], 1)
            act.wait_ge(S["ld_x"], 32)
            norm_root(0)
            act.wait_ge(S["f_h"], 8)
            A(f_mag.rearrange("p t n -> p (t n)"), f_hfb.rearrange("p t n -> p (t n)"), ACT.Abs).then_inc(S["f_sin"], 1)
            norm_turned(0)
            end_phase(act, "start")

            act.sem_inc(S["ip_u"], 6)
            with act.Fori(0, 4) as i:
                for u in range(2):
                    m_ = 2 * i + u
                    act.wait_ge(S["ip_pm"], m_ + 1)
                    for o, part in enumerate((1, 2, 0)):
                        act.wait_ge(S["ip_z"], 3 * m_ + o + 1)
                        act.wait_ge(S["ip_c"], 3 * m_ + o + 1)
                        A(ip_u[:, o, :, 1:SEQ + 1], bank(3 * u + o).rearrange("p (s t) -> p s t", s=2), ACT.Identity,
                          bias=pm[u][:, part:part + 1]).then_inc(S["ip_u"], 1)
            end_phase(act, 3)

            mod_stored(act, 20)
            dma(op_rows[:, 0, :], row(a["hy_out_b"][0])).then_inc(S["ld_rows2"], 16)
            for s in range(2):
                dma(op_rows[:, 1 + s, :], mod_row(0, s, GATE1)).then_inc(S["ld_rows2"], 16)
            end_phase(act, 4)
            load_rows(1)
            load_router(0)
            norm(1)

            def moe_loads(l):
                dma(moe_g2[:, 0, :], mod_row(l, 0, GATE2)).then_inc(M[l]["ld"], 16)
                if l == 0:
                    dma(moe_g2[:, 1, :], mod_row(l, 1, GATE2)).then_inc(M[l]["ld"], 16)

            end_phase(act, 6)
            moe_loads(0)
            act.wait_ge(S["pool_st"], 16)

            def moe(l):
                m_, nt, nx = M[l], TOKEN_TILES[l], EXPERT_TILES[l]
                act.wait_ge(m_["logits"], l + 1)
                A(moe_aff[:, 0:nt * E], bank(7)[:, 0:nt * E], ACT.Sigmoid).then_inc(m_["aff"], 1)

                def silu(g, b):
                    act.wait_ge(m_["h13"], g + 1)
                    A(moe_hid[b], bank(0), ACT.Silu).then_inc(m_["silu"], 1)

                def hidden_t(g, b):
                    act.wait_ge(m_["hT"], g + 1)
                    A(moe_hidT[b].rearrange("p c n -> p (c n)"), bank(4), ACT.Copy).then_inc(m_["hidT"], 1)

                def result(g, dst):
                    act.wait_ge(m_["y"], g + 1)
                    A(dst, banks(5, 2), ACT.Copy).then_inc(m_["yev"], 1)

                def expert_result(j, first=False):
                    if not first:
                        act.wait_ge(m_["yst"], 16 * j)
                    result(nt + j, moe_y)
                    act.wait_ge(m_["yev"], nt + j + 1)
                    act.dma_start(y_d.rearrange("(t p) d -> p t d", p=P)[:, bass.ds(j, 1), :]
                                  .rearrange("p o d -> p (o d)"), moe_y).then_inc(m_["yst"], 16)

                for t in range(nt):
                    silu(t, t % 2)
                    if t >= 1:
                        result(t - 1, moe_S[:, t - 1, :])
                    hidden_t(t, t % 2)
                silu(nt, 0)
                result(nt - 1, moe_S[:, nt - 1, :])
                hidden_t(nt, 0)
                silu(nt + 1, 1)
                expert_result(0, True)
                hidden_t(nt + 1, 1)
                pairs = looped_pairs(act, l)
                with act.Fori(0, pairs) as i:
                    for u in range(2):
                        silu(2 * i + nt + 2 + u, u)
                        expert_result(2 * i + 1 + u)
                        hidden_t(2 * i + nt + 2 + u, u)
                expert_result(2 * pairs + 1)
                for t in range(nt):
                    act.wait_ge(m_[f"ga{t % 2}"], 64 * l + 32 * (t // 2 + 1))
                    A(moe_gat[:, t % 2, 0, :], moe_gat[:, t % 2, 0, :], ACT.Copy, scale=gates[:, t:t + 1]
                      ).then_inc(m_["yev"], 1)
                    if l == 0 and t >= 1:
                        square(2, t - 1)
                if l == 0:
                    square(2, nt - 1)

            moe(0)
            mod_stored(act, 24)
            load_cols(act, 1)
            norm(2)
            end_phase(act, 8)

            dma(mla_g[:, 0:QK], row(a["mla_q_head_g"][0])).then_inc(S["ld_rows2"], 16)
            dma(mla_g[:, QK:2 * QK], row(a["mla_k_head_g"][0])).then_inc(S["ld_rows2"], 16)
            def latent(n):
                is_q, k = n >= 4, 2 * (n % 2)
                width = Q_LORA if is_q else KV_LORA
                act.wait_ge(S["l_down"], n + 1)
                m = A(mla_sq[:, 0:width], bank(0, width), ACT.Square, accum_out=ssq[:, k:k + 1])
                if not is_q:
                    link(m)
                    m = A(mla_sq[:, 0:ROPE], psum[:, 0, KV_LORA:KV_LORA + ROPE], ACT.Square,
                          accum_out=ssq[:, k + 1:k + 2])
                link(m)
                act.drain().then_inc(S["l_ssq"], 1)
                act.wait_ge(S["l_var"], n + 1)
                A(std[:, 0:1], var[:, 0:1], ACT.Sqrt).then_inc(S["l_std"], 1)

            latent(0)
            for n in range(6):
                act.wait_ge(S["l_up"], n + 1)
                if n < 4:
                    act.wait_ge(S["l_v"], n + 1)
                for h in range(H):
                    src = psum[:, 2 + h // 2, (h % 2) * QK:(h % 2) * QK + QK] if n >= 4 else \
                        psum[:, 2 + h // 2, (h % 2) * 256:(h % 2) * 256 + NOPE]
                    link(A(mla_sq[:, 0:src.shape[1]], src, ACT.Square, accum_out=hssq[:, h:h + 1]))
                act.drain().then_inc(S["l_hssq"], 1)
                act.wait_ge(S["l_hvar"], n + 1)
                A(hstd, hvar, ACT.Sqrt).then_inc(S["l_hstd"], 1)
                if n < 5:
                    latent(n + 1)
            end_phase(act, 9)

            dma(o_gate, mod_row(1, 0, GATE1)).then_inc(S["ld_rows2"], 16)
            for u in range(16):
                h, t = u // 2, u % 2
                act.wait_ge(S["a_m"], u + 1)
                A(a_P[:, u % 4, :], bank((0, 1, 6, 7)[u % 4]), ACT.Exp, bias=a_nm[:, u % 4:u % 4 + 1], scale=SM_SCALE,
                  accum_out=a_sum[:, u % 4:u % 4 + 1])
                act.drain().then_inc(S["a_p"], 1)
                if u >= 1:
                    v, hv, tv = u - 1, (u - 1) // 2, (u - 1) % 2
                    act.wait_ge(S["a_pT"], v + 1)
                    if hv >= 2:
                        act.wait_ge(S["a_o"], hv - 1)
                    A(a_PT[:, hv % 2, :, tv * P:(tv + 1) * P], bank(2 + v % 2).rearrange("p (k n) -> p k n", n=P),
                      ACT.Copy).then_inc(S["a_PT"], 1)
            act.wait_ge(S["a_pT"], 16)
            act.wait_ge(S["a_o"], 6)
            A(a_PT[:, 1, :, P:2 * P], bank(3).rearrange("p (k n) -> p k n", n=P), ACT.Copy).then_inc(S["a_PT"], 1)
            end_phase(act, 10)
            load_rows(3)
            load_router(1)
            norm(3)
            end_phase(act, 12)
            moe_loads(1)
            moe(1)

        @block.vector
        def _(dve):
            link = Link(dve, S["link_dve"])
            tt, ts, stt, cp = dve.tensor_tensor, dve.tensor_scalar, dve.scalar_tensor_tensor, dve.tensor_copy
            red = dve.tensor_reduce

            dve.wait_ge(S["f_pre"], 1)
            link(cp(hy_par, bank(7, 120)))

            def sine_argument(k):
                if k == 0:
                    dve.wait_ge(S["ld_filt"], 16 * N_FILT)
                dve.wait_ge(S["f_pre"], k + 2)
                if k:
                    dve.wait_ge(S["f_sin"], k)
                link(ts(f_arg[0:HID, :], bank(k, SEQ, HID), f_par[0:HID, k:k + 1], f_par[0:HID, 3:4], ALU.add, ALU.mult))
                link(ts(f_n[0:HID, :], f_arg[0:HID, :], 1.0 / (2.0 * np.pi), ROUND, ALU.mult, ALU.add))
                link(ts(f_n[0:HID, :], f_n[0:HID, :], -ROUND, None, ALU.add))
                link(stt(f_arg[0:HID, :], f_n[0:HID, :], -TWO_PI_HI, f_arg[0:HID, :], ALU.mult, ALU.add))
                link(stt(f_arg[0:HID, :], f_n[0:HID, :], -TWO_PI_LO, f_arg[0:HID, :], ALU.mult, ALU.add))
                ts(f_arg[0:HID, :], f_arg[0:HID, :], 3.1415925, -3.1415925, ALU.min, ALU.max).then_inc(S["f_arg"], 1)

            def taps():
                dve.wait_ge(S["ld_taps"], 32)
                for j in range(8):
                    t, n = j % 2, j // 2
                    dve.wait_ge(S["f_w3"], j + 1)
                    m = tt(f_hfb[:, t, n * 512:(n + 1) * 512], bank(j % 4),
                           f_decay[:, t, (n % 2) * 512:(n % 2) * 512 + 512], ALU.mult)
                    if j < 7:
                        m.then_inc(S["f_h"], 1)
                    else:
                        link(m)
                dve.wait_ge(S["f_h"], 7)
                dve.memset(f_hfb[0:1, 0, D:2 * D], 0.0).then_inc(S["f_h"], 1)

            def even_odd():
                dve.wait_ge(S["f_w3"], 9)
                dve.wait_ge(S["f_h"], 8)
                link(dve.reciprocal(f_rn, banks(4, 2)))
                link(tt(f_sd[:, 0], f_hfb[:, :, 0:D], f_hfb[:, :, D:2 * D], ALU.add))
                tt(f_sd[:, 1], f_hfb[:, :, 0:D], f_hfb[:, :, D:2 * D], ALU.subtract).then_inc(S["f_h"], 1)

            def transform():
                dve.wait_ge(S["ld_dft"], 32)
                mod_stored(dve, 4)
                for j in range(8):
                    comp, ft, half = j // 4, (j // 2) % 2, j % 2
                    dve.wait_ge(S["f_k"], j + 1)
                    cols = slice(half * 512, half * 512 + 512)
                    tt(f_K[:, 2 * comp + ft, cols], bank(j % 4), f_rn[:, cols], ALU.mult).then_inc(S["f_kdone"], 1)
                    if comp == 0:
                        dve.wait_ge(S["f_kdone"], j + 1)
                        link(tt(f_K[:, ft, cols], f_K[:, ft, cols], f_bias[:, cols], ALU.add))

            def ada_bias(n, b, count):
                dve.wait_ge(S[f"ad_ld{b}"], count)
                dve.wait_ge(S["ad_done"], n + 1)
                dst = mod_first[n] if isinstance(n, int) and n < 4 else mod_piece[b]
                tt(dst, mod_psum[b], dst, ALU.add).then_inc(S["ad_ready"], 1)

            def norm_cols(k):
                norm_var(k)
                norm_scale(k)
                norm_modulate(k)

            def norm_var(k):
                dve.wait_ge(S["n_ssq"], k + 1)
                ts(var[:, 0:TILES], ssq[:, 0:TILES], 1.0 / D, EPS, ALU.mult, ALU.add).then_inc(S["n_var"], 1)

            def norm_scale(k):
                h = norm_places(k)[3]
                dve.wait_ge(S["n_std"], k + 1)
                link(dve.reciprocal(rstd[:, 0:TILES], std[:, 0:TILES]))
                for t in range(TILES):
                    g = NORM_BASE[k] + t
                    if t >= 2:
                        dve.wait_ge(S["n_T"], g - 1)
                    ts(h[:, (t % 2) * D:(t % 2 + 1) * D], X[:, t, :], rstd[:, t:t + 1], None, ALU.mult
                       ).then_inc(S["n_h"], 1)

            def norm_modulate(k):
                dve.wait_ge(S["ld_cols"], 80 * (k // 2 + 1))
                link(stt(mod_cols[:, 0], mod_cols[:, 0], 1.0, bc(gain_col, 1, 2), ALU.add, ALU.mult))
                dve.wait_ge(S["n_hT"], NORM_BASE[k] + TILES)
                for s in range(2):
                    for c in range(DC):
                        part = hT[:, c, s * SEQ:(s + 1) * SEQ]
                        ts(part, part, mod_cols[:, 0, s, c:c + 1], mod_cols[:, 1, s, c:c + 1], ALU.mult, ALU.add)

            sine_argument(0)
            for n in range(4):
                ada_bias(n, n % 2, 16)
                if n < 2:
                    sine_argument(n + 1)
            norm_var(0)
            taps()
            norm_scale(0)
            even_odd()
            transform()
            norm_modulate(0)
            end_phase(dve, "start")

            rows_seen = [0]

            def norm(k):
                rows, gain, junk, h = norm_places(k)
                nt = NORM_TILES[k]
                streams = 2 if k < 3 else 1
                dve.wait_ge(S["n_ssq"], k + 1)
                ts(var[:, 0:nt], ssq[:, 0:nt], 1.0 / D, EPS, ALU.mult, ALU.add).then_inc(S["n_var"], 1)
                rows_seen[0] += 16 * (2 * streams + 1)
                dve.wait_ge(S["ld_rows"], rows_seen[0])
                for s in range(streams):
                    r = rows[:, 2 * s * D:(2 * s + 1) * D]
                    link(stt(r, r, 1.0, gain, ALU.add, ALU.mult))
                dve.wait_ge(S["n_std"], k + 1)
                link(dve.reciprocal(rstd[:, 0:nt], std[:, 0:nt]))
                for t in range(nt):
                    g, s = NORM_BASE[k] + t, t // 2
                    hb = h[:, (t % 2) * D:(t % 2 + 1) * D]
                    if t >= 2:
                        dve.wait_ge(S["n_T"], g - 1)
                        if k % 2 == 1:
                            dve.wait_ge(S[f"n_st{t % 2}"], 16)
                    link(stt(hb, X[:, t, :], rstd[:, t:t + 1], rows[:, 2 * s * D:(2 * s + 1) * D], ALU.mult, ALU.mult))
                    tt(hb, hb, rows[:, (2 * s + 1) * D:(2 * s + 2) * D], ALU.add).then_inc(S["n_h"], 1)


            dve.memset(B(3, 0, 3 * 516), 0.0).then_inc(S["ip_c"], 3)
            dve.sem_inc(S["ip_ve"], 1)
            par = hy_par.rearrange("p (v m) -> p v m", m=8)
            with dve.Fori(0, 4) as i:
                link.enter(i, 2 * 6)
                for u in range(2):
                    m_ = 2 * i + u
                    cp(pm[u], par[:, :, bass.ds(m_, 1)].rearrange("p v o -> p (v o)")).then_inc(S["ip_pm"], 1)
                    dve.wait_ge(S["ip_pm"], m_ + 1)
                    for o, part in enumerate((1, 2, 0)):
                        k = [pm[u][:, (1 + j) * 3 + part:(1 + j) * 3 + part + 1] for j in range(4)]
                        src, tmp = ip_u[:, o], ip_t[:, o]
                        dve.wait_ge(S["ip_u"], 6 + 3 * m_ + o + 1)
                        link(ts(tmp, src[:, :, 1:SEQ + 1], k[1], k[3], ALU.mult, ALU.add))
                        link(stt(tmp, src[:, :, 0:SEQ], k[0], tmp, ALU.mult, ALU.add))
                        dst = tmp if o < 2 else x0T[:, bass.ds(m_, 1), :].rearrange("p o (s t) -> p (o s) t", s=2)
                        stt(dst, src[:, :, 2:SEQ + 2], k[2], tmp, ALU.mult, ALU.add).then_inc(S["ip_c"], 1)
                        if o == 1:
                            dve.wait_ge(S["ip_c"], 3 + 3 * m_ + 2)
                            tt(ip_vgb.rearrange("p (s t) -> p s t", s=2), ip_t[:, 0], ip_t[:, 1], ALU.mult
                               ).then_inc(S["ip_vg"], 1)
                    ada_bias(4 * i + 2 * u + 4, 0, 32 * i + 16 * u + 32)
                    dve.wait_ge(S["ip_vt"], m_ + 1)
                    ts(vgtok[:, :, bass.ds(m_ * P, P)], bank(7).rearrange("p (t n) -> p t n", n=P), 1.0, None, ALU.mult
                       ).then_inc(S["ip_ve"], 1)
                    ada_bias(4 * i + 2 * u + 5, 1, 32 * i + 16 * u + 32)
                link.leave(4)
            end_phase(dve, 3)

            def back(k):
                s, half = k % 2, k // 2
                for m4 in range(4):
                    dve.wait_ge(S["cv_inv"], 4 * k + m4 + 1)
                    dst = x0T[:, 4 * half + m4, s * SEQ:(s + 1) * SEQ]
                    tt(dst, bank(4 + m4 % 2, SEQ), dst, ALU.mult).then_inc(S["cv_yt"], 1)

            for k in range(4):
                half = k // 2
                cols = slice(half * 512, half * 512 + 512)
                dve.wait_ge(S["cv_x"], k + 1)
                if k >= 1:
                    dve.wait_ge(S["cv_y"], k)
                if k >= 2:
                    dve.wait_ge(S["cv_inv"], 4 * (k - 1))
                Y = cv_Y[:, k % 2]
                for f in range(2):
                    Kr, Ki, t0, t1 = f_K[:, f, cols], f_K[:, 2 + f, cols], cv_t[:, 0], cv_t[:, 1]
                    tt(Y[:, f], bank(f), Kr, ALU.mult)
                    tt(t0, bank(2 + f), Ki, ALU.mult)
                    tt(Y[:, 2 + f], bank(f), Ki, ALU.mult)
                    link(tt(t1, bank(2 + f), Kr, ALU.mult))
                    if f == 1:
                        dve.sem_inc(S["cv_xfree"], 1)
                    tt(Y[:, f], Y[:, f], t0, ALU.subtract)
                    m = tt(Y[:, 2 + f], Y[:, 2 + f], t1, ALU.add)
                    if f == 0:
                        link(m)
                m.then_inc(S["cv_y"], 1)
                ada_bias(20 + k, k % 2, 16 * (10 + k // 2))
                if k >= 1:
                    back(k - 1)
            back(3)
            end_phase(dve, 4)

            dve.wait_ge(S["ld_rows2"], 48)
            for n in range(2):
                for t in range(TILES):
                    j = n * TILES + t
                    cols = slice(n * 512, n * 512 + 512)
                    dve.wait_ge(S["op_y"], j + 1)
                    tmp = op_t[:, j % 2]
                    tt(tmp, bank(j % 4), op_rows[:, 0, cols], ALU.add).then_inc(S["op_x"], 1)
                    dve.wait_ge(S["op_x"], j + 1)
                    link(tt(tmp, tmp, op_rows[:, 1 + t // 2, cols], ALU.mult))
                    m = tt(X[:, t, cols], X[:, t, cols], tmp, ALU.add)
                    if n == 1:
                        m.then_inc(S["x_done"], 1)
            norm(1)
            end_phase(dve, 6)

            def moe(l):
                m_, nt, nx = M[l], TOKEN_TILES[l], EXPERT_TILES[l]
                nte = nt * E
                dve.wait_ge(S["ld_lat"], 96)
                v3 = lambda ap: ap.rearrange("p (t e) -> p t e", e=E)
                aff, sb_, w0, w1 = moe_aff[:, 0:nte], moe_r[0][:, 0:nte], moe_r[1][:, 0:nte], moe_r[2][:, 0:nte]
                pair, gs, g1, g2 = moe_pair[:, 0:nt * G, :], moe_g4[0][:, 0:nt * G], moe_g4[1][:, 0:nt * G], moe_g4[2][:, 0:nt]

                dve.wait_ge(m_["aff"], l + 1)
                link(tt(v3(sb_), v3(aff), bc(router_b, 1, nt), ALU.add))
                q = sb_.rearrange("p (g e) -> p g e", e=PER_G)
                tt(pair[:, :, 0:3], q[:, :, 0:3], q[:, :, 1:4], ALU.add)
                tt(pair[:, :, 3:5], q[:, :, 0:2], q[:, :, 2:4], ALU.add)
                link(tt(pair[:, :, 5:6], q[:, :, 0:1], q[:, :, 3:4], ALU.add))
                link(red(gs, pair, AX.X, ALU.max))
                gs3, g13 = (x.rearrange("p (t g) -> p t g", g=G) for x in (gs, g1))

                def first_max(dst3, val3, best, desc, n):
                    link(red(best, val3, AX.X, ALU.max))
                    link(tt(dst3, val3, bc(best, 2, n), ALU.is_equal))
                    link(tt(dst3, dst3, bc(desc, 1, nt), ALU.mult))
                    link(red(best, dst3, AX.X, ALU.max))
                    link(tt(dst3, dst3, bc(best, 2, n), ALU.is_equal))

                first_max(g13, gs3, g2, C(C_DESC4, G), G)
                gm = bc(g1, 2, PER_G)
                qw = w0.rearrange("p (g e) -> p g e", e=PER_G)
                link(tt(qw, q, gm, ALU.mult))
                link(ts(g1, g1, -1.0, BIG, ALU.add, ALU.mult))
                link(tt(qw, qw, gm, ALU.add))
                best = moe_g4[2][:, 0:nt]
                desc = C(C_DESC, E)
                sa, sb2 = sel_a[:, 0:nte], sel_b[:, 0:nte]
                first_max(v3(sa), v3(w0), best, desc, E)
                link(stt(w0, sa, -2.0 * BIG, w0, ALU.mult, ALU.add))
                first_max(v3(sb2), v3(w0), best, desc, E)
                tt(moe_sel[:, 0:nt, :].rearrange("p t e -> p (t e)"), sa, sb2, ALU.add).then_inc(m_["sel"], 1)
                for k, s_ in enumerate((sa, sb2)):
                    link(tt(w1, s_, aff, ALU.mult))
                    link(red(gates[:, k * TILES:k * TILES + nt], v3(w1), AX.X, ALU.add))
                link(tt(best, gates[:, 0:nt], gates[:, TILES:TILES + nt], ALU.add))
                link(dve.reciprocal(best, best))
                for k in range(2):
                    gk = gates[:, k * TILES:k * TILES + nt]
                    link(tt(gk, gk, best, ALU.mult))

                def hidden(g, b):
                    dve.wait_ge(m_["silu"], g + 1)
                    tt(moe_hid[b], moe_hid[b], bank(1), ALU.mult).then_inc(m_["hid"], 1)

                def tokens_t(j, b):
                    dve.wait_ge(m_["xT"], j + 1)
                    cp(moe_xT[b].rearrange("p c n -> p (c n)"), banks(2, 2)).then_inc(m_["xTe"], 1)

                hidden(0, 0)

                dve.wait_ge(m_["pos"], l + 1)
                cnt = bank(7)[:, 64 + nt * E:64 + (nt + 1) * E]
                link(ts(cnt16, cnt, 0.0, None, ALU.is_gt))
                for k in range(1, nt):
                    link(stt(cnt16, cnt, float(k * P), cnt16, ALU.is_gt, ALU.add))
                link(dve.memset(scan[0], 0.0))
                link(dve.memset(scan[1], 0.0))
                link(cp(scan[0][:, E:2 * E], cnt16))
                src = 0
                for d in (1, 2, 4, 8):
                    link(tt(scan[1 - src][:, E:2 * E], scan[src][:, E:2 * E], scan[src][:, E - d:2 * E - d], ALU.add))
                    src = 1 - src
                first = scan[src][:, E - 1:2 * E - 1]
                link(tt(moe_cmp[:, 0:nx * E].rearrange("p (t e) -> p t e", e=E), bc(C(C_TILE, nx), 2, E),
                        bc(first, 1, nx), ALU.is_ge))
                link(red(moe_r[2][:, 0:nx], moe_cmp[:, 0:nx * E].rearrange("p (t e) -> p t e", e=E), AX.X, ALU.add))
                ts(eid_i[:, 0:nx], moe_r[2][:, 0:nx], -1.0, None, ALU.add)
                ts(pairs_i, scan[src][:, 2 * E - 1:2 * E], 0.5, -0.75, ALU.mult, ALU.add).then_inc(m_["eid"], 1)
                link(stt(v3(w0), bc(first, 1, nt), float(P), v3(bank(7)[:, 64:64 + nte]), ALU.mult, ALU.add))
                for k, s_ in enumerate((sa, sb2)):
                    link(tt(w1, s_, w0, ALU.mult))
                    link(red(moe_slot[:, k * nt:(k + 1) * nt], v3(w1), AX.X, ALU.add))
                sl = moe_slot[:, 0:2 * nt]
                cp(slot_i[:, 0:2 * nt], sl)
                ge = moe_cmp[:, 0:2 * nt * (nx + 1)].rearrange("p (q t) -> p q t", t=nx + 1)
                link(tt(ge, bc(sl, 2, nx + 1), bc(C(C_GRID, nx + 1), 1, 2 * nt), ALU.is_ge))
                hi = moe_slot[:, 2 * nt:4 * nt]
                link(red(hi, ge, AX.X, ALU.add))
                link(stt(sl, hi, float(-P), sl, ALU.mult, ALU.add))
                link(ts(sl, sl, float(P), None, ALU.add))
                link(tt(moe_hot[:, 0:2 * nt, :], bc(C(C_IOTA, P), 1, 2 * nt), bc(sl, 2, P), ALU.is_equal))
                hit = moe_hit[:, 0:2 * nt, 0:nx]
                link(tt(hit, ge[:, :, 0:nx], ge[:, :, 1:nx + 1], ALU.subtract))
                for k in range(2):
                    h_ = moe_hit[:, k * nt:(k + 1) * nt, 0:nx]
                    m = tt(h_, h_, bc(C(C_TOK, nt), 2, nx), ALU.mult)
                m.then_inc(m_["hot"], 1)

                hidden(1, 1)
                dve.wait_ge(m_["idxp"], l + 1)
                dve.memset(idx_i[:, nx:nx + 1], 0)
                cp(idx_i[:, 0:nx], bank(7)[:, 192:192 + nx]).then_inc(m_["idx"], 1)
                for t in range(2, nt):
                    hidden(t, t % 2)
                tokens_t(0, 0)
                hidden(nt, 0)
                tokens_t(1, 1)
                hidden(nt + 1, 1)
                tokens_t(2, 0)
                dve.wait_ge(m_["yev"], nt)
                dve.wait_ge(m_["ld"], 32 + 16 * l)
                for t in range(nt):
                    st = moe_S[:, t, :]
                    link(tt(st, st, moe_g2[:, t // 2, :], ALU.mult))
                    link(tt(X[:, t, :], X[:, t, :], st, ALU.add))
                pairs = looped_pairs(dve, l)
                with dve.Fori(0, pairs) as i:
                    for u in range(2):
                        hidden(2 * i + nt + 2 + u, u)
                        tokens_t(2 * i + 3 + u, 1 - u)

                for t in range(nt):
                    dve.wait_ge(m_[f"ga{t % 2}"], 64 * l + 32 * (t // 2 + 1))
                    ya, yb = (moe_gat[:, t % 2, k, :] for k in range(2))
                    dve.wait_ge(m_["yev"], 2 * pairs + nt + 3 + t)
                    link(stt(yb, yb, gates[:, TILES + t:TILES + t + 1], ya, ALU.mult, ALU.add))
                    link(tt(yb, yb, moe_g2[:, t // 2, :], ALU.mult))
                    tt(X[:, t, :], X[:, t, :], yb, ALU.add).then_inc(m_["comb"], 1)

            moe(0)
            norm_cols(2)
            end_phase(dve, 8)

            dve.wait_ge(S["ld_rows2"], 80)
            up4 = psum[:, 2:6, :].rearrange("p b (h d) -> p (b h) d", d=256)

            def latent(n):
                is_q, k = n >= 4, 2 * (n % 2)
                width = Q_LORA if is_q else KV_LORA
                dve.wait_ge(S["l_ssq"], n + 1)
                ts(var[:, 0:1], ssq[:, k:k + 1], 1.0 / width, EPS, ALU.mult, ALU.add).then_inc(S["l_var"], 1)
                dve.wait_ge(S["l_std"], n + 1)
                link(dve.reciprocal(rstd[:, 0:1], std[:, 0:1]))
                if not is_q:
                    link(cp(mla_pe[n % 2], psum[:, 0, KV_LORA:KV_LORA + ROPE]))
                ts(mla_lat[:, 0:width], bank(0, width), rstd[:, 0:1], None, ALU.mult).then_inc(S["l_lat"], 1)

            def latent_turned(n):
                is_q, chunks = n >= 4, 3 if n >= 4 else 2
                dve.wait_ge(S["l_T"], n + 1)
                if n:
                    dve.wait_ge(S["l_up"], n)
                for c in range(chunks):
                    g = (0 if is_q else 3) + c
                    m = ts(mla_latT[:, c, :], bank(1)[:, c * P:(c + 1) * P], lat_g[:, g:g + 1], None, ALU.mult)
                m.then_inc(S["l_TT"], 1)

            def values_out(n):
                dve.wait_ge(S["l_up"], n + 1)
                cp(a_V[:, n, :].rearrange("p (h d) -> p h d", d=VD), up4[:, :, NOPE:256]).then_inc(S["l_v"], 1)

            latent(0)
            latent_turned(0)
            values_out(0)
            for n in range(6):
                is_q, tile = n >= 4, n % 4
                dve.wait_ge(S["l_hssq"], n + 1)
                if is_q:
                    ts(hvar, hssq, 1.0 / QK, EPS, ALU.mult, ALU.add).then_inc(S["l_hvar"], 1)
                else:
                    link(ts(hssq, hssq, ssq[:, 2 * (n % 2) + 1:2 * (n % 2) + 2], 1.0 / QK, ALU.add, ALU.mult))
                    ts(hvar, hssq, EPS, None, ALU.add).then_inc(S["l_hvar"], 1)
                dve.wait_ge(S["l_hstd"], n + 1)
                link(dve.reciprocal(hrstd, hstd))
                if is_q:
                    for b in range(4):
                        src = psum[:, 2 + b, 0:384].rearrange("p (h d) -> p h d", d=QK)
                        pair_r = hrstd[:, 2 * b:2 * b + 2]
                        tt(mla_hn[:, 2 * b:2 * b + 2, :], src[:, :, 0:NOPE], bc(pair_r, 2, NOPE), ALU.mult)
                        m = tt(mla_hr[:, 2 * b:2 * b + 2, :], src[:, :, NOPE:QK], bc(pair_r, 2, ROPE), ALU.mult)
                else:
                    tt(mla_hr, bc(mla_pe[n % 2], 1, H), bc(hrstd, 2, ROPE), ALU.mult)
                    m = tt(mla_hn, up4[:, :, 0:NOPE], bc(hrstd, 2, NOPE), ALU.mult)
                m.then_inc(S["l_hn"], 1)
                if n < 5:
                    latent(n + 1)
                dve.wait_ge(S["l_hn"], n + 1)
                gain = mla_g[:, 0:QK] if is_q else mla_g[:, QK:2 * QK]
                link(tt(mla_hn, mla_hn, bc(gain[:, 0:NOPE], 1, H), ALU.mult))
                m = tt(mla_hr, mla_hr, bc(gain[:, NOPE:QK], 1, H), ALU.mult)
                if is_q or n < LAT_TILES:
                    link(m)
                    t0 = C_ROPE + 64 * tile
                    cos = bc(C(t0, 32).rearrange("p (a k) -> p a k", a=2), 1, H)
                    sin = bc(C(t0 + 32, 32).rearrange("p (a k) -> p a k", a=2), 1, H)
                    r = mla_hr.rearrange("p h (a b k) -> p h a b k", a=2, b=2)
                    t4 = [mla_t[:, k * 256:(k + 1) * 256].rearrange("p (h a k) -> p h a k", h=H, a=2) for k in range(4)]
                    x1, x2 = r[:, :, :, 0, :], r[:, :, :, 1, :]
                    tt(t4[0], x1, cos, ALU.mult)
                    tt(t4[1], x2, sin, ALU.mult)
                    tt(t4[2], x2, cos, ALU.mult)
                    link(tt(t4[3], x1, sin, ALU.mult))
                    tt(x1, t4[0], t4[1], ALU.subtract)
                    tt(x2, t4[2], t4[3], ALU.add).then_inc(S["l_hr"], 1)
                else:
                    m.then_inc(S["l_hr"], 1)
                if n < 5:
                    latent_turned(n + 1)
                if n < 3:
                    values_out(n + 1)
                dve.wait_ge(S["l_HT"], n + 1)
                nope, rope = (qTn, qTr) if is_q else (kTn, kTr)
                cols = slice(tile * P, (tile + 1) * P)
                cp(nope[:, :, cols], banks(6, 2).rearrange("p (h n) -> p h n", n=P))
                cp(rope[:, :, cols], bank(1).rearrange("p (h n) -> p h n", n=P)).then_inc(S["l_hevac"], 1)
            end_phase(dve, 9)

            def head_out(h):
                dve.wait_ge(S["a_o"], h + 1)
                cp(OT[:, h, :], bank(4 + h % 2, SEQ)).then_inc(S["a_ot"], 1)

            def probs(u):
                dve.wait_ge(S["a_p"], u + 1)
                s = a_sum[:, u % 4:u % 4 + 1]
                link(dve.reciprocal(s, s))
                ts(a_P[:, u % 4, :], a_P[:, u % 4, :], s, None, ALU.mult).then_inc(S["a_pn"], 1)

            for u in range(16):
                dve.wait_ge(S["a_s"], u + 1)
                if u >= 4:
                    dve.wait_ge(S["a_p"], u - 3)
                nm = a_nm[:, u % 4:u % 4 + 1]
                link(red(nm, bank((0, 1, 6, 7)[u % 4]), AX.X, ALU.max))
                ts(nm, nm, -SM_SCALE, None, ALU.mult).then_inc(S["a_m"], 1)
                if u >= 1:
                    probs(u - 1)
                if u >= 4 and u % 2 == 0:
                    head_out(u // 2 - 2)
            probs(15)
            head_out(6)
            head_out(7)
            end_phase(dve, 10)
            dve.wait_ge(S["ld_rows2"], 96)
            for n in range(2):
                for t in range(LAT_TILES):
                    j = 2 * n + t
                    cols = slice(n * 512, n * 512 + 512)
                    dve.wait_ge(S["op_y"], 8 + j + 1)
                    tmp = o_t[:, j % 2]
                    tt(tmp, bank(j), o_gate[:, cols], ALU.mult).then_inc(S["op_x"], 1)
                    dve.wait_ge(S["op_x"], 8 + j + 1)
                    m = tt(X[:, t, cols], X[:, t, cols], tmp, ALU.add)
                    if n == 1:
                        m.then_inc(S["x_done"], 1)
            norm(3)
            end_phase(dve, 12)
            moe(1)

        @block.gpsimd
        def _(pool):
            def moe(l):
                m_, nt, nx = M[l], TOKEN_TILES[l], EXPERT_TILES[l]
                pool.wait_ge(m_["idx"], l + 1)
                for b in range(2):
                    pool.wait_ge(S[f"n_st{b}"], 32 + 16 * l)

                def gather(j, b):
                    nc.gpsimd.tensor_copy(idx_cur[:, b:b + 1], idx_i[:, bass.ds(j, 1)]).then_inc(m_["cur"], 1)
                    pool.wait_ge(m_["cur"], j + 1)
                    pool.sem_inc(S["ordered"], 1)
                    nc.gpsimd.indirect_dma_start(
                        moe_xg[b], None, h2_d[l][:, :],
                        bass.IndirectOffsetOnAxis(ap=idx_cur[:, b:b + 1], axis=0)).then_inc(m_[f"xg{b}"], 16)

                gather(0, 0)
                gather(1, 1)
                pool.wait_ge(m_["xT"], 1)
                gather(2, 0)
                pairs = looped_pairs(pool, l)
                with pool.Fori(0, pairs) as i:
                    for u in range(2):
                        pool.wait_ge(m_["xT"], 2 * i + 2 + u)
                        gather(2 * i + 3 + u, 1 - u)
                pool.wait_ge(m_["yst"], 32 * pairs + 32)
                pool.sem_inc(S["ordered"], 1)
                for t in range(nt):
                    if t >= 2:
                        pool.wait_ge(m_["comb"], t - 1)
                    for k in range(2):
                        nc.gpsimd.indirect_dma_start(
                            moe_gat[:, t % 2, k, :], None, y_d[:, :],
                            bass.IndirectOffsetOnAxis(ap=slot_i[:, k * nt + t:k * nt + t + 1], axis=0)
                        ).then_inc(m_[f"ga{t % 2}"], 16)

            flat_bias = a["ada_b"].rearrange("l n -> (l n)")

            def bias_piece(q, b):
                pool.dma_start(mod_piece[b], flat_bias[bass.ds(q * 512, 512)].rearrange("(o n) -> o n", o=1)
                               .partition_broadcast(2)).then_inc(S[f"ad_ld{b}"], 16)

            def store_piece(n, l, q, b, count, then=None):
                pool.wait_ge(S["ad_ready"], n + 1)
                pool.sem_inc(S["ordered"], 1)
                pool.dma_start(mod_d[l, :, bass.ds(q * 512, 512)], mod_piece[b]).then_inc(S[f"ad_st{b}"], 16)
                if then is not None:
                    pool.wait_ge(S[f"ad_st{b}"], count)
                    pool.sem_inc(S["ordered"], 1)
                    bias_piece(then, b)

            for b in range(2):
                pool.dma_start(B(4, 0, D)[32 * b:32 * b + 2, :].rearrange("p (k n) -> p k n", k=2),
                               flat_bias[0:2 * D].rearrange("(k two n) -> two k n", two=2, n=512)[b]
                               .partition_broadcast(2)).then_inc(S[f"ad_ld{b}"], 16)
            for n in range(4):
                pool.wait_ge(S["ad_ready"], n + 1)
                pool.dma_start(mod_d[0, :, n * 512:(n + 1) * 512], mod_first[n]).then_inc(S[f"ad_st{n % 2}"], 16)
                if n < 2:
                    bias_piece((4, 13)[n], n)
            with pool.Fori(0, 4) as i:
                for u in range(2):
                    n, count = 4 * i + 2 * u + 4, 32 * i + 16 * u + 48
                    store_piece(n, 0, 2 * i + u + 4, 0, count, 2 * i + u + 5)
                    store_piece(n + 1, 1, 2 * i + u + 1, 1, count, 2 * i + u + 14)
            store_piece(20, 1, 0, 0, 16 * 11, 22)
            store_piece(21, 1, 9, 1, 16 * 11, 23)
            store_piece(22, 1, 10, 0, 16 * 12)
            store_piece(23, 1, 11, 1, 16 * 12)
            pool.wait_ge(S["op_y"], 1)
            first_unsure = TOKEN_TILES[0] * TOP_K
            pool.dma_start(y_d[first_unsure * P:, :].rearrange("(t p) d -> p t d", p=P),
                           bc(dft_t[:, 0:D], 1, T_MAX - first_unsure)).then_inc(S["pool_st"], 16)
            moe(0)
            moe(1)
            pool.wait_ge(M[1]["comb"], TILES + LAT_TILES)
            pool.dma_start(out[0].rearrange("(t p) d -> p t d", p=P), X[:, 0:LAT_TILES, :]).then_inc(S["pool_st"], 16)
            pool.wait_ge(S["pool_st"], 32)


INPUTS = ["x", "c", "ctx", "c_ctx", "ada_w", "ada_b", "norm_mix_g", "norm_ffn_g", "hy_in_w", "hy_in_b", "hy_conv_w",
          "hy_conv_b", "hy_f_w1", "hy_f_b1", "hy_f_w2", "hy_f_b2", "hy_f_w3", "hy_sin_freq", "hy_f_bias", "hy_out_w",
          "hy_out_b", "mla_wq_down", "mla_q_norm_g", "mla_wq_up", "mla_wkv_down", "mla_kv_norm_g", "mla_wkv_up",
          "mla_q_head_g", "mla_k_head_g", "mla_wo", "router_w", "router_bias", "exp_w1", "exp_w3", "exp_w2", "sh_w1",
          "sh_w3", "sh_w2"]


def kernel(**inputs):
    import concourse.bacc as bacc
    from concourse.bass_utils import run_bass_kernel_spmd as run

    nc = bacc.Bacc("TRN2", target_bir_lowering=False, num_devices=1)
    arrays = {f"in_{n}": np.ascontiguousarray(inputs[n]) for n in INPUTS}
    arrays.update(shape_constants())
    aps = {n.removeprefix("in_"): nc.dram_tensor(n, v.shape, F32, kind="ExternalInput").ap() for n, v in arrays.items()}
    out = nc.dram_tensor("out", [1, SEQ, D], F32, kind="ExternalOutput").ap()
    build(nc, aps, out)
    return run(nc, [arrays], core_ids=[0]).results[0]["out"]
```

```python
from contextlib import ExitStack

import numpy as np
import concourse.bass as bass
from concourse import mybir

ACT = mybir.ActivationFunctionType
ALU = mybir.AluOpType
AX = mybir.AxisListType
F32 = mybir.dt.float32
I32 = mybir.dt.int32

P = 128
D = 1024
DC = D // P
SEQ = 256
TILES = 2 * SEQ // P
LAT_TILES = SEQ // P
DEPTH = 2
EPS = 1e-6
N_MOD = 6
SHIFT1, SCALE1, GATE1, SHIFT2, SCALE2, GATE2 = range(N_MOD)

HID = 64
EMB = 33
BANDS = 16
TWO_PI_HI = 6.28125
TWO_PI_LO = 2.0 * np.pi - TWO_PI_HI
ROUND = 1.5 * 2.0 ** 23

H = 8
NOPE, ROPE, QK, VD = 128, 64, 192, 128
Q_LORA, KV_LORA = 384, 256
SM_SCALE = QK ** -0.5

E, G, PER_G = 16, 4, 4
FF = 512
FC = FF // P
TOP_K = 2


def expert_tiles(tokens):
    return ((tokens * TOP_K - E) // P + E + 1) // 2 * 2


TOKEN_TILES = [TILES, LAT_TILES]
EXPERT_TILES = [expert_tiles(t * P) for t in TOKEN_TILES]
T_MAX = max(EXPERT_TILES)

SLOTS = 6
SLOT_W = 4096
BIG = 1.0e30

C_IDENT, C_UPPER, C_ONES, C_IOTA = 0, 128, 256, 384
C_GRID = 512
C_TILE = C_GRID + T_MAX + 1
C_DESC = C_TILE + T_MAX + 1
C_DESC4 = C_DESC + E
C_TOK = C_DESC4 + G
C_ROPE = C_TOK + TILES
C_PICK = C_ROPE + LAT_TILES * 64
C_END = C_PICK + 4


def shape_constants():
    f = np.float32
    small = np.zeros((P, C_END), f)
    small[:, C_IDENT:C_IDENT + P] = np.eye(P)
    small[:, C_UPPER:C_UPPER + P] = np.triu(np.ones((P, P)), 1)
    small[:, C_ONES:C_ONES + P] = 1
    small[:, C_IOTA:C_IOTA + P] = np.arange(P)
    small[:, C_GRID:C_GRID + T_MAX + 1] = P * np.arange(T_MAX + 1)
    small[:, C_TILE:C_TILE + T_MAX + 1] = np.arange(T_MAX + 1)
    small[:, C_DESC:C_DESC + E] = E - np.arange(E)
    small[:, C_DESC4:C_DESC4 + G] = G - np.arange(G)
    small[:, C_TOK:C_TOK + TILES] = np.arange(P)[:, None] + P * np.arange(TILES)[None]
    grid_w, half = 64, ROPE // 2
    inv = (f(10000.0) ** (-np.arange(0, half, 2, dtype=f) / f(half))).astype(f)
    tok = np.arange(SEQ)
    ang = np.stack([(tok // grid_w).astype(f)[:, None] * inv, (tok % grid_w).astype(f)[:, None] * inv], 1)
    for t in range(LAT_TILES):
        a = ang[t * P:(t + 1) * P].reshape(P, 32)
        small[:, C_ROPE + 64 * t:C_ROPE + 64 * t + 32] = np.cos(a)
        small[:, C_ROPE + 64 * t + 32:C_ROPE + 64 * t + 64] = np.sin(a)
    small[:, [C_PICK, C_PICK + 3]] = 1
    w = np.pi * np.outer(np.arange(SEQ), 2 * np.arange(SEQ) + 1) / (2.0 * SEQ)
    fwd = np.concatenate([np.cos(w), -np.sin(w)], 1).reshape(2, P, 2 * SEQ).transpose(1, 0, 2)
    inv_t = np.concatenate([np.cos(w.T), -np.sin(w.T)], 0).reshape(4, P, SEQ).transpose(1, 0, 2) / SEQ
    dft = np.concatenate([fwd.reshape(P, -1), inv_t.reshape(P, -1)], 1).astype(f)
    t_norm = np.linspace(0.0, 1.0, SEQ, dtype=f)[:, None]
    bands = np.linspace(1e-4, BANDS - 1, BANDS, dtype=f)[None]
    a = (f(2.0 * np.pi) * bands * np.arange(SEQ, dtype=f)[:, None] / f(SEQ)).astype(f)
    pos = np.ascontiguousarray(np.concatenate([t_norm, np.cos(a), -np.sin(a)], 1).T.astype(f))
    lo, hi = np.log(1e-2) / 1.5, np.log(1e-2) / 0.3
    deltas = np.linspace(lo, hi, D, dtype=f)
    decay = np.exp(-t_norm * np.abs(deltas)).astype(f)
    return {"c_small": small, "c_dft": dft, "c_pos": pos, "c_decay": decay}


class Link:

    def __init__(self, eng, sem):
        self.eng, self.sem, self.n, self.off = eng, sem, 0, 0

    def __call__(self, ins):
        self.n += 1
        ins.then_inc(self.sem, 1)
        self.eng.wait_ge(self.sem, self.off + self.n)

    def enter(self, i, per):
        self.at, self.per, self.off = self.n, per, i * per

    def leave(self, iterations):
        assert self.n == self.at + self.per, (self.n - self.at, self.per)
        self.n, self.off = self.at + self.per * iterations, 0


def build(nc, a, out):
    with ExitStack() as ctx:
        def sb(name, words, dt=F32):
            return ctx.enter_context(nc.sbuf_tensor(name, [P, words], dt))

        def sem(name):
            return ctx.enter_context(nc.semaphore(name))

        def dram(name, shape):
            return nc.dram_tensor(name, shape, F32, kind="Internal").ap()

        mod_d = dram("mod_rows", [DEPTH, 2, N_MOD * D])
        h2_d = [dram(f"h2_{l}", [TOKEN_TILES[l] * P, D]) for l in range(DEPTH)]
        y_d = dram("expert_out", [T_MAX * P, D])

        ring = sb("weight_ring", SLOTS * SLOT_W)
        Xt = sb("residual", TILES * D)
        blk = sb("blocks", 5 * 4096)
        dft_t = sb("dft", 2048)
        cst = sb("small_constants", C_END)
        hy_rows_t = sb("hyena_rows", P)
        mod_t = sb("mod_pieces", 512)
        small = sb("small_values", 560)
        ints = sb("int_values", 2 * T_MAX + 2 * TILES + 4, I32)
        psum = ctx.enter_context(nc.psum_tensor("psum", [P, 8, 512], F32))

        def slot(s, words=SLOT_W):
            return ring[:, s * SLOT_W:s * SLOT_W + words]

        def B(block, at, words):
            return blk[:, block * 4096 + at:block * 4096 + at + words]

        def C(at, words):
            return cst[:, at:at + words]

        small_at = [0]

        def sm(words):
            at = small_at[0]
            small_at[0] += words
            assert small_at[0] <= 560
            return small[:, at:at + words]

        X = Xt[:, :].rearrange("p (t d) -> p t d", d=D)
        ident = C(C_IDENT, P)
        dft_fwd = dft_t[:, 0:1024].rearrange("p (t f) -> p t f", t=2)
        dft_inv = dft_t[:, 1024:2048].rearrange("p (k t) -> p k t", k=4)

        cT = sm(16)
        scT = sm(16).rearrange("p (c s) -> p c s", s=2)
        ssq, var, std, rstd = sm(8), sm(8), sm(8), sm(8)
        hy_par = sm(120)
        pm = [sm(15), sm(15)]
        router_b = sm(E)
        sel_a, sel_b = sm(TILES * E), sm(TILES * E)
        gates = sm(2 * TILES)
        cnt16 = sm(E)
        scan = [sm(2 * E), sm(2 * E)]
        mod_cols = sm(32).rearrange("p (k s c) -> p k s c", k=2, s=2)
        gain_col = sm(DC)
        lat_g = sm(5)
        idx_i = ints[:, 0:T_MAX + 1]
        eid_i = ints[:, T_MAX + 1:2 * T_MAX + 1]
        slot_i = ints[:, 2 * T_MAX + 1:2 * T_MAX + 1 + 2 * TILES]
        idx_cur = ints[:, 2 * T_MAX + 1 + 2 * TILES:2 * T_MAX + 3 + 2 * TILES]
        pairs_i = ints[:, 2 * T_MAX + 3 + 2 * TILES:2 * T_MAX + 4 + 2 * TILES]

        def bc(ap, axis, n):
            u = ap.unsqueeze(axis)
            shape = list(u.shape)
            shape[axis] = n
            return u.broadcast_to(shape)

        def bank(k, words=512, parts=P):
            return psum[0:parts, k, 0:words]

        def banks(k, n):
            return psum[:, k:k + n, :].rearrange("p b n -> p (b n)")

        w_loaded = [sem(f"w_loaded{s}") for s in range(SLOTS)]
        w_loaded_in = [sem(f"w_loaded_in{u}") for u in range(2)]
        w_used = [sem(f"w_used{s}") for s in range(SLOTS)]
        names = """phase link_dve link_act ld_const ld_cond ld_x ld_hy ld_filt ld_taps ld_dft ld_rows ld_rows2 ld_lat ld_cols
            silu_c f_pre f_arg f_sin f_w3 f_h f_k f_kdone
            ad_done ad_ready ad_ld0 ad_ld1 ad_st0 ad_st1
            n_ssq n_var n_std n_h n_T n_hT n_st0 n_st1
            ip_pm ip_z ip_u ip_c ip_vg ip_vt ip_ve
            cv_x cv_y cv_xfree cv_inv cv_yt op_y op_x x_done
            l_down l_ssq l_var l_std l_lat l_T l_TT l_up l_hssq l_hvar l_hstd l_hn l_v l_hr l_HT l_hevac
            a_s a_m a_p a_pn a_pT a_PT a_o a_ot pool_st ordered""".split()
        S = {n: sem(n) for n in names}
        once = {n: sem(n) for n in "routing aff sel hot idx eid rw ld ga0 ga1 ga2 ga3 comb".split()}
        moe_names = "h13 silu hid hT hidT y yev xT xTe xg0 xg1 cur yst".split()
        e_loaded = [[sem(f"expert_loaded{s}_{l}") for s in range(SLOTS)] for l in range(DEPTH)]
        e_used = [[sem(f"expert_w1_used{b}_{l}") for b in range(2)] for l in range(DEPTH)]
        M = [once | {n: sem(f"{n}_{l}") for n in moe_names} for l in range(DEPTH)]

        loads, landed = [0] * SLOTS, [0] * SLOTS
        W, LANDED = {}, {}
        before_experts = []

        def book(name, s, times=1, own_sem=False):
            W[name], LANDED[name] = (s, loads[s]), landed[s]
            loads[s] += times
            landed[s] += 0 if own_sem else times

        for u in range(4):
            book(f"ada_first{u}", u)
        for u in range(2):
            book(f"hy_in_{u}", 4 + u, 4, True)
            book(f"ada0_{u}", u, 4)
            book(f"ada1_{u}", 2 + u, 4)
        for k, s in enumerate((0, 2, 4, 5)):
            book(f"ada_last{k}", s)
        book("hy_out0", 1)
        book("hy_out1", 0)

        def book_moe(l):
            for w, s in ((1, 3), (3, 4), (2, 5)):
                book(f"sh{w}_{l}", s)
            before_experts.append([n + 1 for n in loads])

        book_moe(0)
        for name, s in (("wqd", 0), ("wkvd", 1), ("wkvu", 2), ("wqu0", 3), ("wqu1", 4), ("wo0", 5), ("wo1", 2)):
            book(name, s)
        book_moe(1)

        def wait_piece(pe, name, i=0):
            pe.wait_ge(w_loaded[W[name][0]], 16 * (LANDED[name] + 1) + 16 * i)

        def piece(name, words=SLOT_W):
            return slot(W[name][0], words)

        def freed(ins, name):
            ins.then_inc(w_used[W[name][0]], 1)

        def looped_pairs(eng, l):
            eng.wait_ge(M[l]["eid"], l + 1)
            return eng.value_load(pairs_i[0:1, 0:1], min_val=1, max_val=(EXPERT_TILES[l] - 2) // 2)

        def norm_places(k):
            if k == 0:
                return None, None, B(0, 3072, 1024), B(3, 1024, 2048)
            if k == 1:
                return B(4, 0, 4096), B(2, 0, 1024), B(2, 1024, 1024), B(2, 2048, 2048)
            return B(1, 0, 4096), B(2, 0, 1024), B(2, 1024, 1024), B(2, 2048, 2048)

        NORM_TILES = [4, 4, 4, 2]
        NORM_BASE = [0, 4, 8, 12]
        ROOT_BASE = [0, 1, 5, 6]
        TURN_BANK = [0, 4, 0, 4]
        hT = B(0, 0, 4096).rearrange("p (c t) -> p c t", c=DC)

        mod_first = [slot(4)[32 * (n % 2):32 * (n % 2) + 2, 3072 + 512 * (n // 2):3584 + 512 * (n // 2)] for n in range(4)]
        mod_piece = [mod_t[32 * b:32 * b + 2, :] for b in range(2)]
        mod_psum = [psum[32 * b:32 * b + 2, 6, :] for b in range(2)]
        ada_sums = [slot(4 + u)[:, 3072:4096].rearrange("p (s n) -> p s n", s=2) for u in range(2)]
        hy_rows = hy_rows_t[:, :]
        f_own = slot(5)
        f_rn, f_bias = f_own[:, 0:D], f_own[:, D:2 * D]
        f_pos, f_arg, f_n = (f_own[:, 2 * D + 256 * k:2 * D + 256 * (k + 1)] for k in range(3))
        f_h = [f_own[:, 2 * D + 256 * (3 + k):2 * D + 256 * (4 + k)] for k in range(3)]
        f_w1, f_par = f_own[:, 3584:3584 + HID], f_own[:, 3584 + 3 * HID:3584 + 3 * HID + 4]
        f_w2 = [f_own[:, 3584 + HID * (1 + k):3584 + HID * (2 + k)] for k in range(2)]
        f_hfb = B(1, 0, 4096).rearrange("p (t n) -> p t n", t=2)
        f_mag = B(4, 0, 4096).rearrange("p (t n) -> p t n", t=2)
        f_sd = B(2, 0, 4096).rearrange("p (k t n) -> p k t n", k=2, t=2)
        f_decay = B(3, 0, 2048).rearrange("p (t n) -> p t n", t=2)
        f_w3 = B(3, 2048, 2048)
        f_K = B(4, 0, 4096).rearrange("p (k n) -> p k n", k=4)
        N_FILT = 8
        x0T = B(1, 0, 4096).rearrange("p (m t) -> p m t", m=8)
        vgtok = B(2, 0, 4096).rearrange("p (t d) -> p t d", d=D)
        ip_u = B(3, 0, 1548).rearrange("p (o s t) -> p o s t", o=3, s=2)
        ip_t = B(3, 1548, 1536).rearrange("p (o s t) -> p o s t", o=3, s=2)
        ip_vgb = B(3, 3084, 512)
        cv_Y = B(0, 0, 4096).rearrange("p (k f n) -> p k f n", k=2, f=4)
        cv_t = B(3, 3072, 1024).rearrange("p (k n) -> p k n", k=2)
        op_rows = B(3, 0, 3072).rearrange("p (k n) -> p k n", k=3)
        op_t = dft_t[:, 1024:2048].rearrange("p (k n) -> p k n", k=2)
        moe_S = B(1, 0, 4096).rearrange("p (t d) -> p t d", d=D)
        moe_xg = [B(2, b * D, D) for b in range(2)]
        moe_xT = [B(2, (2 + b) * D, D).rearrange("p (c n) -> p c n", c=DC) for b in range(2)]
        moe_hid = [B(3, b * FF, FF) for b in range(2)]
        moe_hidT = [B(3, (2 + b) * FF, FF).rearrange("p (c n) -> p c n", c=FC) for b in range(2)]
        moe_y = B(3, 2048, D)
        moe_rw = B(3, 3072, 128).rearrange("p (c e) -> p c e", c=DC)
        moe_aff = B(3, 3200, 64)
        moe_sel = B(3, 3264, 64).rearrange("p (t e) -> p t e", e=E)
        moe_g2 = B(4, 0, 2048).rearrange("p (s d) -> p s d", s=2)
        moe_hot = B(4, 2048, 1024).rearrange("p (q n) -> p q n", q=2 * TILES)
        moe_hit = B(4, 3072, 2 * TILES * (T_MAX + 1)).rearrange("p (q t) -> p q t", t=T_MAX + 1)
        moe_cmp = B(4, 3272, 384)
        moe_r = [B(4, 3656 + 64 * k, 64) for k in range(3)]
        moe_pair = B(4, 3848, 96).rearrange("p (g s) -> p g s", s=6)
        moe_g4 = [B(4, 3944 + 16 * k, 16) for k in range(3)]
        moe_slot = B(4, 3992, 4 * TILES)
        moe_gat = blk[:, 0:8 * D].rearrange("p (t k d) -> p t k d", t=TILES, k=2)
        a_V = B(1, 0, 4096).rearrange("p (t d) -> p t d", d=D)
        kTn = B(2, 0, 4096).rearrange("p (h t) -> p h t", h=H)
        kTr = B(3, 0, 2048).rearrange("p (h t) -> p h t", h=H // 2)
        qTn = B(3, 2048, 2048).rearrange("p (h t) -> p h t", h=H)
        qTr = B(4, 0, 1024).rearrange("p (h t) -> p h t", h=H // 2)
        mla_hn = B(4, 1024, H * NOPE).rearrange("p (h d) -> p h d", h=H)
        mla_hr = B(4, 2048, H * ROPE).rearrange("p (h d) -> p h d", h=H)
        mla_t, mla_sq = B(4, 2560, 1024), B(4, 3584, 384)
        mla_lat, mla_latT = dft_t[:, 0:384], dft_t[:, 384:768].rearrange("p (c n) -> p c n", c=3)
        mla_g = dft_t[:, 768:768 + 2 * QK]
        mla_pe = [dft_t[:, 1152 + k * ROPE:1152 + (k + 1) * ROPE] for k in range(2)]
        o_gate = dft_t[:, 768:1792]
        hssq, hvar, hstd, hrstd = (dft_t[:, 1792 + 8 * k:1800 + 8 * k] for k in range(4))
        a_nm, a_sum = dft_t[:, 1824:1828], dft_t[:, 1828:1832]
        OT = Xt[:, 2 * D:4 * D].rearrange("p (h t) -> p h t", h=H)
        a_PT = B(0, 2048, 2048).rearrange("p (b k t) -> p b k t", b=2, k=4)
        a_P = B(4, 1024, 2048).rearrange("p (u n) -> p u n", u=4)
        o_t = B(4, 3072, 1024).rearrange("p (k n) -> p k n", k=2)

        def mod_row(l, stream, k):
            return mod_d[l, stream:stream + 1, k * D:(k + 1) * D].partition_broadcast(P)

        def row(ap):
            return ap.rearrange("(o n) -> o n", o=1).partition_broadcast(P)

        block = ctx.enter_context(nc.Block())

        ended = {}

        def end_phase(eng, name):
            ended.setdefault(name, len(ended) + 1)
            eng.drain().then_inc(S["phase"], 1)
            eng.wait_ge(S["phase"], 3 * ended[name])

        def mod_stored(eng, pieces):
            for b in range(2):
                eng.wait_ge(S[f"ad_st{b}"], 8 * pieces)

        def load_cols(eng, l):
            for s in range(2):
                for k, which in enumerate((SCALE1, SHIFT1)):
                    eng.dma_start(mod_cols[:, k, s, :], mod_d[l, s, which * D:(which + 1) * D]
                                  .rearrange("(p c) -> p c", c=DC)).then_inc(S["ld_cols"], 16)
            eng.dma_start(gain_col, a["norm_mix_g"][l].rearrange("(p c) -> p c", c=DC)).then_inc(S["ld_cols"], 16)

        @block.sync
        def _(sp):
            def load(name, dst_words, src, i=0, shape=None, free=None):
                s, n = W[name]
                sp.wait_ge(*(free or (w_used[s], n + 1 + i)))
                dst = slot(s, dst_words)
                if shape:
                    dst = dst.rearrange(shape[0], **shape[1])
                sp.dma_start(dst, src).then_inc(w_loaded[s], 16)

            def ada(l, q):
                return a["ada_w"][l, :, bass.ds(q * 512, 512)].rearrange("(p c) n -> p c n", c=DC)

            k8 = ("p (c n) -> p c n", {"c": DC})
            sp.dma_start(cst[:, :], a["c_small"]).then_inc(S["ld_const"], 16)
            for s, v in enumerate((a["c"][0], a["c_ctx"])):
                sp.dma_start(cT[:, 8 * s:8 * s + 8], v.rearrange("(p c) -> p c", c=DC)).then_inc(S["ld_cond"], 16)
            dma = sp.dma_start
            dma(f_pos[0:EMB, :], a["c_pos"]).then_inc(S["ld_filt"], 16)
            dma(f_w1[0:EMB, :], a["hy_f_w1"][0]).then_inc(S["ld_filt"], 16)
            dma(f_par[0:HID, 0:1], a["hy_f_b1"][0].rearrange("(n o) -> n o", o=1)).then_inc(S["ld_filt"], 16)
            dma(f_par[0:HID, 3:4], a["hy_sin_freq"][0].rearrange("(n o) -> n o", o=1)).then_inc(S["ld_filt"], 16)
            for k in range(2):
                dma(f_w2[k][0:HID, :], a["hy_f_w2"][0, k]).then_inc(S["ld_filt"], 16)
                dma(f_par[0:HID, 1 + k:2 + k], a["hy_f_b2"][0, k].rearrange("(n o) -> n o", o=1)
                    ).then_inc(S["ld_filt"], 16)
            for q, (w, k) in enumerate((("hy_in_b", 24), ("hy_conv_w", 72), ("hy_conv_b", 24))):
                at = (0, 24, 96)[q]
                src = a[w][0].rearrange("(r n) -> r n", n=P) if w != "hy_conv_w" else \
                    a[w][0].rearrange("k (r n) -> (k r) n", n=P)
                dma(hy_rows[at:at + k, :], src).then_inc(S["ld_hy"], 16)
            for u in range(4):
                load(f"ada_first{u}", 4096, ada(0, u), 0, k8)
                if u == 0:
                    dma(f_w3[0:HID, :], a["hy_f_w3"][0]).then_inc(S["ld_taps"], 16)
                    dma(f_decay, a["c_decay"].rearrange("(t p) d -> p t d", p=P)).then_inc(S["ld_taps"], 16)
                if u == 2:
                    dma(X[:, 0:2, :], a["x"][0].rearrange("(t p) d -> p t d", p=P)).then_inc(S["ld_x"], 16)
                    dma(X[:, 2:4, :], a["ctx"][0].rearrange("(t p) d -> p t d", p=P)).then_inc(S["ld_x"], 16)
            dma(dft_t[:, :], a["c_dft"]).then_inc(S["ld_dft"], 16)
            dma(f_bias, row(a["hy_f_bias"][0])).then_inc(S["ld_dft"], 16)
            mod_stored(sp, 4)
            load_cols(sp, 0)
            with sp.Fori(0, 4) as i:
                for u in range(2):
                    s = W[f"hy_in_{u}"][0]
                    sp.wait_ge(S["ip_z"], 6 * i + 3 * u + 3)
                    src = a["hy_in_w"][0].rearrange("(p c) (q m n) -> p c q m n", c=DC, q=3, n=P)
                    dst = slot(s, 3072).rearrange("p (q c n) -> p q c n", q=3, c=DC)
                    for q in range(3):
                        sp.dma_start(dst[:, q], src[:, :, q, bass.ds(2 * i + u, 1), :].rearrange("p c o n -> p c (o n)")
                                     ).then_inc(w_loaded_in[u], 16)
                    load(f"ada0_{u}", 4096, ada(0, 4 + 2 * i + u), i, k8, (S["ad_done"], 4 * i + 2 * u + 1))
                    load(f"ada1_{u}", 4096, ada(1, 1 + 2 * i + u), i, k8)
            for k in range(4):
                if k >= 2:
                    sp.wait_ge(S["ad_done"], 19 + k)
                load(f"ada_last{k}", 4096, ada(1, (0, 9, 10, 11)[k]), 0, k8)
            sp.wait_ge(S["ad_done"], 23)
            for n in range(2):
                load(f"hy_out{n}", 4096, a["hy_out_w"][0, :, n * 512:(n + 1) * 512]
                     .rearrange("(m p) n -> p m n", p=P), 0, k8)

            def experts(l):
                up = "(p c) n -> p c n"
                load(f"sh1_{l}", 4096, a["sh_w1"][l].rearrange(up, c=DC), 0, k8)
                load(f"sh3_{l}", 4096, a["sh_w3"][l].rearrange(up, c=DC), 0, k8)
                load(f"sh2_{l}", 4096, a["sh_w2"][l].rearrange(up, c=FC), 0, ("p (c n) -> p c n", {"c": FC}))
                pairs = looped_pairs(sp, l)

                def tile_weights(j, b, i=None):
                    e = sp.value_load(eid_i[0:1, bass.ds(j, 1)], min_val=0, max_val=E - 1)
                    for k, (w, c) in enumerate(((1, DC), (3, DC), (2, FC))):
                        s = 3 * b + k
                        if i is None:
                            sp.wait_ge(w_used[s], before_experts[l][s])
                        else:
                            free, count = ((e_used[l][b], i + 1), (M[l]["h13"], TOKEN_TILES[l] + 2 * i + b + 1),
                                           (M[l]["y"], TOKEN_TILES[l] + 2 * i + b + 1))[k]
                            sp.wait_ge(free, count)
                        if i is None and b == 0 and k == 2:
                            sp.wait_ge(M[l]["xg0"], 16)
                        src = a[f"exp_w{w}"][l, bass.ds(e, 1), :, :].rearrange("o (p c) n -> p (o c) n", c=c)
                        sp.dma_start(slot(s).rearrange("p (c n) -> p c n", c=c), src).then_inc(e_loaded[l][s], 16)

                for j in range(2):
                    tile_weights(j, j)
                with sp.Fori(0, pairs) as i:
                    for b in range(2):
                        tile_weights(2 * i + 2 + b, b, i)
                return pairs

            pairs = experts(0)
            for name in ("h13", "y"):
                sp.wait_ge(M[0][name], TOKEN_TILES[0] + 2 * pairs + 2)
            for t in range(TILES):
                sp.wait_ge(M[0][f"ga{t}"], 32)
            load("wkvd", 2560, a["mla_wkv_down"][0].rearrange("(p c) n -> p c n", c=DC), 0, k8)
            load("wkvu", 4096, a["mla_wkv_up"][0].rearrange("(c p) n -> p c n", p=P), 0,
                 ("p (c n) -> p c n", {"c": 2}))
            load("wqd", 3072, a["mla_wq_down"][0].rearrange("(p c) n -> p c n", c=DC), 0, k8)
            for n in range(2):
                load(f"wqu{n}", 2304, a["mla_wq_up"][0, :, n * 768:(n + 1) * 768].rearrange("(c p) n -> p c n", p=P),
                     0, ("p (c n) -> p c n", {"c": 3}))
            for n in range(2):
                load(f"wo{n}", 4096, a["mla_wo"][0, :, n * 512:(n + 1) * 512].rearrange("(h p) n -> p h n", p=P), 0, k8)
            experts(1)

        @block.tensor
        def _(pe):
            mm = pe.matmul
            for s in range(SLOTS - 1):
                pe.sem_inc(w_used[s], 1)
            pe.sem_inc(S["ip_z"], 3)

            pe.wait_ge(S["ld_const"], 16)
            pe.wait_ge(S["ld_hy"], 48)
            pe.transpose(bank(7, 120), hy_rows[0:120, :], ident[0:120, 0:120]).then_inc(S["f_pre"], 1)
            def filter_layer(k):
                if k == 0:
                    pe.wait_ge(S["ld_filt"], 16 * N_FILT)
                    mm(bank(0, SEQ, HID), f_w1[0:EMB, :], f_pos[0:EMB, :], start=True, stop=True
                       ).then_inc(S["f_pre"], 1)
                else:
                    pe.wait_ge(S["f_sin"], k)
                    mm(bank(k, SEQ, HID), f_w2[k - 1][0:HID, :], f_h[k - 1][0:HID, :], start=True, stop=True
                       ).then_inc(S["f_pre"], 1)

            def filter_taps():
                pe.wait_ge(S["f_sin"], 3)
                pe.wait_ge(S["ld_taps"], 32)
                for j in range(8):
                    t, n = j % 2, j // 2
                    if j >= 4:
                        pe.wait_ge(S["f_h"], j - 3)
                    mm(bank(j % 4), f_h[2][0:HID, t * P:(t + 1) * P], f_w3[0:HID, n * 512:(n + 1) * 512],
                       start=True, stop=True).then_inc(S["f_w3"], 1)

            def filter_norm():
                pe.wait_ge(S["f_sin"], 4)
                for half in range(2):
                    for k in range(4):
                        t, side = k % 2, k // 2
                        m = mm(bank(4 + half), C(C_ONES, P),
                               f_mag[:, t, side * D + half * 512:side * D + half * 512 + 512],
                               start=(k == 0), stop=(k == 3))
                m.then_inc(S["f_w3"], 1)

            def filter_transform():
                pe.wait_ge(S["f_h"], 9)
                pe.wait_ge(S["ld_dft"], 32)
                for j in range(8):
                    comp, ft, half = j // 4, (j // 2) % 2, j % 2
                    if j >= 4:
                        pe.wait_ge(S["f_kdone"], j - 3)
                    for t in range(2):
                        m = mm(bank(j % 4), dft_fwd[:, t, comp * SEQ + ft * P:comp * SEQ + ft * P + P],
                               f_sd[:, comp, t, half * 512:half * 512 + 512], start=(t == 0), stop=(t == 1))
                    m.then_inc(S["f_k"], 1)

            def ada_piece(name, n, b, i=0, frees=True):
                if not isinstance(n, int) or n >= 2:
                    pe.wait_ge(S["ad_ready"], n - 1)
                wait_piece(pe, name, i)
                w = piece(name).rearrange("p (c n) -> p c n", c=DC)
                for c in range(DC):
                    m = mm(mod_psum[b], scT[:, c, :], w[:, c, :], start=(c == 0), stop=(c == DC - 1))
                m.then_inc(S["ad_done"], 1)
                if frees:
                    pe.drain().then_inc(w_used[W[name][0]], 1)

            def turn_tile(k, t):
                h, g = norm_places(k)[3], NORM_BASE[k] + t
                pe.wait_ge(S["n_h"], g + 1)
                if t >= 2:
                    pe.wait_ge(S["n_hT"], g - 1)
                for c in range(DC):
                    m = pe.transpose(banks(TURN_BANK[k] + 2 * (t % 2), 2)[:, c * P:(c + 1) * P],
                                     h[:, (t % 2) * D + c:(t % 2) * D + D:DC], ident)
                m.then_inc(S["n_T"], 1)

            def norm_turn(k):
                for t in range(NORM_TILES[k]):
                    turn_tile(k, t)

            filter_layer(0)
            pe.wait_ge(S["silu_c"], 1)
            for n in range(4):
                ada_piece(f"ada_first{n}", n, n % 2)
                if n < 2:
                    filter_layer(n + 1)
            filter_taps()
            pe.wait_ge(S["f_h"], 7)
            norm_turn(0)
            filter_norm()
            pe.wait_ge(S["n_hT"], NORM_TILES[0])
            filter_transform()
            end_phase(pe, "start")
            pe.sem_inc(w_used[5], 1)
            pe.sem_inc(S["ip_z"], 3)

            with pe.Fori(0, 4) as i:
                for u in range(2):
                    m_ = 2 * i + u
                    name = f"hy_in_{u}"
                    w = piece(name, 3072).rearrange("p (q c n) -> p q c n", q=3, c=DC)
                    pe.wait_ge(w_loaded_in[u], 48 * i + 48)
                    for o, part in enumerate((1, 2, 0)):
                        pe.wait_ge(S["ip_u"], 3 * m_ + o + 1)
                        for c in range(DC):
                            m = mm(bank(3 * u + o), w[:, part, c, :], hT[:, c, :], start=(c == 0), stop=(c == DC - 1))
                        m.then_inc(S["ip_z"], 1)
                    ada_piece(f"ada0_{u}", 4 * i + 2 * u + 4, 0, i, False)
                    pe.wait_ge(S["ip_vg"], m_ + 1)
                    pe.wait_ge(S["ip_ve"], m_ + 1)
                    for t in range(TILES):
                        m = pe.transpose(bank(7)[:, t * P:(t + 1) * P], ip_vgb[:, t * P:(t + 1) * P], ident)
                    m.then_inc(S["ip_vt"], 1)
                    pe.wait_ge(S["ad_ready"], 4 * i + 2 * u + 4)
                    pe.wait_ge(S["ip_pm"], 2 * m_ + 2)
                    for s in range(2):
                        m = mm(mod_psum[1], C(C_PICK + 2 * s, 2), ada_sums[u][:, s, :], start=(s == 0), stop=(s == 1))
                    m.then_inc(S["ad_done"], 1)
            pe.drain()
            for u in range(2):
                pe.sem_inc(w_used[W[f"ada0_{u}"][0]], 4)
                pe.sem_inc(w_used[W[f"hy_in_{u}"][0]], 4)
            end_phase(pe, 3)

            def conv_back(k, quarters):
                pe.wait_ge(S["cv_y"], k + 1)
                for m4 in quarters:
                    n = 4 * k + m4
                    if n >= 2:
                        pe.wait_ge(S["cv_yt"], n - 1)
                    for f in range(4):
                        m = mm(bank(4 + m4 % 2, SEQ), cv_Y[:, k % 2, f, m4 * P:(m4 + 1) * P], dft_inv[:, f, :],
                               start=(f == 0), stop=(f == 3))
                    m.then_inc(S["cv_inv"], 1)

            for k in range(4):
                s, half = k % 2, k // 2
                if k >= 1:
                    pe.wait_ge(S["cv_xfree"], k)
                for f in range(4):
                    for t in range(2):
                        m = mm(bank(f), dft_fwd[:, t, f * P:(f + 1) * P], vgtok[:, 2 * s + t, half * 512:half * 512 + 512],
                               start=(t == 0), stop=(t == 1))
                m.then_inc(S["cv_x"], 1)
                if k >= 1:
                    conv_back(k - 1, (0, 1))
                ada_piece(f"ada_last{k}", 20 + k, k % 2)
                if k >= 1:
                    conv_back(k - 1, (2, 3))
            conv_back(3, range(4))
            end_phase(pe, 4)

            def project(names, lhs, k, before):
                w = [piece(name).rearrange("p (c n) -> p c n", c=DC) for name in names]
                for t in range(NORM_TILES[k]):
                    for n in range(2):
                        j = 2 * t + n
                        if t == 0:
                            wait_piece(pe, names[n])
                        if j >= 4:
                            pe.wait_ge(S["op_x"], before + j - 3)
                        for c in range(DC):
                            m = mm(bank(j % 4), lhs[:, c, t * P:(t + 1) * P], w[n][:, c, :], start=(c == 0), stop=(c == 7))
                        m.then_inc(S["op_y"], 1)
                    if t == NORM_TILES[k] - 1:
                        pe.drain().then_inc(w_used[W[names[0]][0]], 1)
                        pe.sem_inc(w_used[W[names[1]][0]], 1)
                    if t >= 1:
                        turn_tile(k, t - 1)
                turn_tile(k, t)
                pe.wait_ge(S["op_x"], before + 2 * NORM_TILES[k])

            project(("hy_out0", "hy_out1"), x0T, 1, 0)
            end_phase(pe, 6)

            def moe(l):
                m_, nt, nx = M[l], TOKEN_TILES[l], EXPERT_TILES[l]
                xT = moe_xT
                pe.wait_ge(m_["rw"], 16 * l + 16)
                for t in range(nt):
                    for c in range(DC):
                        m = mm(bank(7)[:, t * E:(t + 1) * E], hT[:, c, t * P:(t + 1) * P], moe_rw[:, c, :],
                               start=(c == 0), stop=(c == DC - 1))
                m.then_inc(m_["routing"], 1)

                def shared_piece(w, last):
                    name = f"sh{w}_{l}"
                    return W[name][0], w_loaded[W[name][0]], 16 * (LANDED[name] + 1), w_used[W[name][0]] if last else None

                def expert_piece(w, b, i):
                    s = 3 * b + (1, 3, 2).index(w)
                    return s, e_loaded[l][s], 16 * i + 16, e_used[l][b] if w == 1 else None

                def up(pieces, lhs):
                    for k, (s, loaded, count, used) in enumerate(pieces):
                        pe.wait_ge(loaded, count)
                        w = slot(s).rearrange("p (c n) -> p c n", c=DC)
                        for c in range(DC):
                            m = mm(bank(k), lhs(c), w[:, c, :], start=(c == 0), stop=(c == DC - 1))
                        if used and k == 0:
                            m.then_inc(used, 1)
                    m.then_inc(m_["h13"], 1)
                    if used:
                        pe.drain().then_inc(used, 1)

                def down(g, b, piece_, first=False):
                    s, loaded, count, used = piece_
                    pe.wait_ge(m_["hidT"], g + 1)
                    if not first:
                        pe.wait_ge(m_["yev"], g)
                    pe.wait_ge(loaded, count)
                    w = slot(s).rearrange("p (c n) -> p c n", c=FC)
                    for n in range(2):
                        for c in range(FC):
                            m = mm(bank(5 + n), moe_hidT[b][:, c, :], w[:, c, n * 512:(n + 1) * 512],
                                   start=(c == 0), stop=(c == FC - 1))
                    m.then_inc(m_["y"], 1)
                    if used:
                        pe.drain().then_inc(used, 1)

                def turn_hidden(g, b):
                    pe.wait_ge(m_["hid"], g + 1)
                    for c in range(FC):
                        m = pe.transpose(bank(4)[:, c * P:(c + 1) * P], moe_hid[b][:, c::FC], ident)
                    m.then_inc(m_["hT"], 1)

                def turn_tokens(j, b, count):
                    pe.wait_ge(m_[f"xg{b}"], count)
                    for c in range(DC):
                        m = pe.transpose(banks(2, 2)[:, c * P:(c + 1) * P], moe_xg[b][:, c::DC], ident)
                    m.then_inc(m_["xT"], 1)

                def ranks():
                    pe.wait_ge(m_["sel"], l + 1)
                    for q in range(nt + 1):
                        for r in range(min(q, nt - 1) + 1):
                            lhs = C(C_UPPER, P) if r == q else C(C_ONES, P)
                            m = mm(bank(7)[:, 64 + q * E:64 + (q + 1) * E], lhs, moe_sel[:, r, :],
                                   start=(r == 0), stop=(r == min(q, nt - 1)))
                    m.then_inc(m_["routing"], 1)

                for t in range(nt):
                    up([shared_piece(w, t == nt - 1) for w in (1, 3)], lambda c, t=t: hT[:, c, t * P:(t + 1) * P])
                    if t == 0:
                        ranks()
                    if t == 1:
                        pe.wait_ge(m_["hot"], l + 1)
                        for q in range(2 * nt):
                            m = mm(bank(7)[:, 192:192 + nx], moe_hot[:, q, :], moe_hit[:, q, 0:nx],
                                   start=(q == 0), stop=(q == 2 * nt - 1))
                        m.then_inc(m_["routing"], 1)
                    if t >= 1:
                        down(t - 1, (t - 1) % 2, shared_piece(2, False), t == 1)
                    turn_hidden(t, t % 2)
                turn_tokens(0, 0, 16)

                def step(j, b, i, count):
                    pe.wait_ge(m_["xTe"], j + 1)
                    up([expert_piece(w, b, i) for w in (1, 3)], lambda c: xT[b][:, c, :])
                    turn_tokens(j + 1, 1 - b, count)

                step(0, 0, 0, 16)
                down(nt - 1, 1, shared_piece(2, True))
                turn_hidden(nt, 0)
                step(1, 1, 0, 32)
                down(nt, 0, expert_piece(2, 0, 0))
                turn_hidden(nt + 1, 1)
                pairs = looped_pairs(pe, l)
                with pe.Fori(0, pairs) as i:
                    step(2 * i + 2, 0, i + 1, 16 * i + 32)
                    down(2 * i + nt + 1, 1, expert_piece(2, 1, i))
                    turn_hidden(2 * i + nt + 2, 0)
                    step(2 * i + 3, 1, i + 1, 16 * i + 48)
                    down(2 * i + nt + 2, 0, expert_piece(2, 0, i + 1))
                    turn_hidden(2 * i + nt + 3, 1)
                down(2 * pairs + nt + 1, 1, expert_piece(2, 1, pairs))

            moe(0)
            norm_turn(2)
            end_phase(pe, 8)

            def latent_down(n):
                is_q, tile = n >= 4, n % 4
                name, width = ("wqd", Q_LORA) if is_q else ("wkvd", KV_LORA + ROPE)
                w = piece(name, DC * width).rearrange("p (c n) -> p c n", c=DC)
                wait_piece(pe, name)
                if n:
                    pe.wait_ge(S["l_lat"], n)
                for c in range(DC):
                    m = mm(bank(0, width), hT[:, c, tile * P:(tile + 1) * P], w[:, c, :],
                           start=(c == 0), stop=(c == DC - 1))
                m.then_inc(S["l_down"], 1)

            def latent_turn(n):
                if n >= 2:
                    pe.wait_ge(S["l_hevac"], n - 1)
                pe.wait_ge(S["l_lat"], n + 1)
                for c in range(3 if n >= 4 else 2):
                    m = pe.transpose(bank(1)[:, c * P:(c + 1) * P], mla_lat[:, c * P:(c + 1) * P], ident)
                m.then_inc(S["l_T"], 1)

            def heads_up(n):
                is_q = n >= 4
                chunks = 3 if is_q else 2
                pe.wait_ge(S["l_TT"], n + 1)
                if n:
                    pe.wait_ge(S["l_hn"], n)
                for q in range(4):
                    if is_q:
                        name, width = f"wqu{q // 2}", 384
                        w = piece(name, 2304).rearrange("p (c n) -> p c n", c=3)[:, :, (q % 2) * 384:(q % 2) * 384 + 384]
                    else:
                        name, width = "wkvu", 512
                        w = piece(name).rearrange("p (c n) -> p c n", c=2)[:, :, q * 512:(q + 1) * 512]
                    wait_piece(pe, name)
                    for c in range(chunks):
                        m = mm(bank(2 + q, width), mla_latT[:, c, :], w[:, c, :], start=(c == 0), stop=(c == chunks - 1))
                m.then_inc(S["l_up"], 1)

            def heads_turn(n):
                pe.wait_ge(S["l_hr"], n + 1)
                for h in range(H):
                    pe.transpose(banks(6, 2)[:, h * P:(h + 1) * P], mla_hn[:, h, :], ident)
                for h in range(H // 2):
                    m = pe.transpose(bank(1)[:, h * P:(h + 1) * P], B(4, 2048 + h * P, P), ident)
                m.then_inc(S["l_HT"], 1)

            latent_down(0)
            latent_turn(0)
            latent_down(1)
            for n in range(6):
                heads_up(n)
                if n >= 1:
                    heads_turn(n - 1)
                if n + 2 < 6:
                    latent_down(n + 2)
                if n + 1 < 6:
                    latent_turn(n + 1)
            heads_turn(5)
            pe.drain().then_inc(w_used[W["wqd"][0]], 1)
            for name in ("wkvd", "wkvu", "wqu0", "wqu1"):
                pe.sem_inc(w_used[W[name][0]], 1)
            end_phase(pe, 9)

            units = [(h, t) for h in range(H) for t in range(LAT_TILES)]

            def scores(u):
                h, t = units[u]
                r = 64 * (h % 2)
                if u >= 4:
                    pe.wait_ge(S["a_p"], u - 3)
                bk = (0, 1, 6, 7)[u % 4]
                mm(bank(bk), qTn[:, h, t * P:(t + 1) * P], kTn[:, h, :], start=True, stop=False)
                mm(bank(bk), qTr[r:r + 64, h // 2, t * P:(t + 1) * P], kTr[r:r + 64, h // 2, :],
                   start=False, stop=True).then_inc(S["a_s"], 1)

            def turn_probs(u):
                pe.wait_ge(S["a_pn"], u + 1)
                if u >= 2:
                    pe.wait_ge(S["a_PT"], u - 1)
                for k in range(4):
                    m = pe.transpose(bank(2 + u % 2)[:, k * P:(k + 1) * P], a_P[:, u % 4, k * P:(k + 1) * P], ident)
                m.then_inc(S["a_pT"], 1)

            def values(h):
                pe.wait_ge(S["a_PT"], 2 * h + 2)
                if h >= 2:
                    pe.wait_ge(S["a_ot"], h - 1)
                for k in range(4):
                    m = mm(bank(4 + h % 2, SEQ), a_V[:, k, h * P:(h + 1) * P], a_PT[:, h % 2, k, :],
                           start=(k == 0), stop=(k == 3))
                m.then_inc(S["a_o"], 1)

            for u in range(2):
                scores(u)
            for u in range(16):
                if u + 2 < 16:
                    scores(u + 2)
                turn_probs(u)
                if u >= 2 and u % 2 == 0:
                    values(u // 2 - 1)
            values(7)
            end_phase(pe, 10)
            project(("wo0", "wo1"), OT, 3, 2 * TILES)
            end_phase(pe, 12)
            moe(1)

        @block.scalar
        def _(act):
            A = nc.scalar.activation
            link = Link(act, S["link_act"])
            dma = act.dma_start

            dma(router_b, row(a["router_bias"])).then_inc(S["ld_lat"], 16)
            for k, (w, c) in enumerate([("mla_q_norm_g", c) for c in range(3)] + [("mla_kv_norm_g", c) for c in range(2)]):
                dma(lat_g[:, k:k + 1], a[w][0, c * P:(c + 1) * P].rearrange("(p o) -> p o", o=1)
                    ).then_inc(S["ld_lat"], 16)

            act.wait_ge(S["ld_cond"], 32)
            A(scT, cT.rearrange("p (s c) -> p c s", s=2), ACT.Silu).then_inc(S["silu_c"], 1)

            def load_rows(k):
                l = k // 2
                rows, gain = norm_places(k)[:2]
                for s in range(2 if l == 0 else 1):
                    dma(rows[:, 2 * s * D:(2 * s + 1) * D], mod_row(l, s, SCALE2)).then_inc(S["ld_rows"], 16)
                    dma(rows[:, (2 * s + 1) * D:(2 * s + 2) * D], mod_row(l, s, SHIFT2)).then_inc(S["ld_rows"], 16)
                dma(gain, row(a["norm_ffn_g"][l])).then_inc(S["ld_rows"], 16)

            def square(k, t):
                if k:
                    done, before = {1: (S["x_done"], 0), 2: (M[0]["comb"], 0), 3: (S["x_done"], TILES)}[k]
                    act.wait_ge(done, before + t + 1)
                link(A(norm_places(k)[2], X[:, t, :], ACT.Square, accum_out=ssq[:, t:t + 1]))

            def root(k, tiles, n):
                act.drain().then_inc(S["n_ssq"], 1)
                act.wait_ge(S["n_var"], ROOT_BASE[k] + n + 1)
                A(std[:, tiles], var[:, tiles], ACT.Sqrt).then_inc(S["n_std"], 1)

            def turned(k, t):
                h, g = norm_places(k)[3], NORM_BASE[k] + t
                if k % 2 == 1:
                    act.wait_ge(S["n_h"], g + 1)
                    dma(h2_d[k // 2][t * P:(t + 1) * P, :], h[:, (t % 2) * D:(t % 2 + 1) * D]).then_inc(S[f"n_st{t % 2}"], 16)
                act.wait_ge(S["n_T"], g + 1)
                A(hT[:, :, t * P:(t + 1) * P], banks(TURN_BANK[k] + 2 * (t % 2), 2).rearrange("p (c n) -> p c n", n=P),
                  ACT.Copy).then_inc(S["n_hT"], 1)

            def norm_by_tile(k):
                for t in range(NORM_TILES[k]):
                    square(k, t)
                    root(k, slice(t, t + 1), t)
                    if t >= 1:
                        turned(k, t - 1)
                turned(k, t)

            def load_router(l):
                dma(moe_rw, a["router_w"].rearrange("(p c) e -> p c e", c=DC)).then_inc(M[l]["rw"], 16)

            for k in range(3):
                act.wait_ge(S["f_arg"], k + 1)
                A(f_h[k][0:HID, :], f_arg[0:HID, :], ACT.Sin).then_inc(S["f_sin"], 1)
            act.wait_ge(S["ld_x"], 32)
            for t in range(TILES):
                square(0, t)
            root(0, slice(0, TILES), 0)
            act.wait_ge(S["f_h"], 8)
            A(f_mag.rearrange("p t n -> p (t n)"), f_hfb.rearrange("p t n -> p (t n)"), ACT.Abs).then_inc(S["f_sin"], 1)
            for t in range(TILES):
                turned(0, t)
            end_phase(act, "start")

            act.sem_inc(S["ip_u"], 6)
            with act.Fori(0, 4) as i:
                for u in range(2):
                    m_ = 2 * i + u
                    act.wait_ge(S["ip_pm"], 2 * m_ + 1)
                    for o, part in enumerate((1, 2, 0)):
                        act.wait_ge(S["ip_z"], 6 + 3 * m_ + o + 1)
                        act.wait_ge(S["ip_c"], 3 * m_ + o + 1)
                        A(ip_u[:, o, :, 1:SEQ + 1], bank(3 * u + o).rearrange("p (s t) -> p s t", s=2), ACT.Identity,
                          bias=pm[u][:, part:part + 1]).then_inc(S["ip_u"], 1)
            end_phase(act, 3)

            mod_stored(act, 20)
            dma(op_rows[:, 0, :], row(a["hy_out_b"][0])).then_inc(S["ld_rows2"], 16)
            for s in range(2):
                dma(op_rows[:, 1 + s, :], mod_row(0, s, GATE1)).then_inc(S["ld_rows2"], 16)
            end_phase(act, 4)
            load_rows(1)
            load_router(0)
            norm_by_tile(1)

            def moe_loads(l):
                dma(moe_g2[:, 0, :], mod_row(l, 0, GATE2)).then_inc(M[l]["ld"], 16)
                if l == 0:
                    dma(moe_g2[:, 1, :], mod_row(l, 1, GATE2)).then_inc(M[l]["ld"], 16)

            end_phase(act, 6)
            moe_loads(0)
            mod_stored(act, 24)
            load_cols(act, 1)
            act.wait_ge(S["pool_st"], 16)
            dma(mla_g[:, 0:QK], row(a["mla_q_head_g"][0])).then_inc(S["ld_rows2"], 16)
            dma(mla_g[:, QK:2 * QK], row(a["mla_k_head_g"][0])).then_inc(S["ld_rows2"], 16)

            def moe(l):
                m_, nt, nx = M[l], TOKEN_TILES[l], EXPERT_TILES[l]
                act.wait_ge(m_["routing"], 3 * l + 1)
                A(moe_aff[:, 0:nt * E], bank(7)[:, 0:nt * E], ACT.Sigmoid).then_inc(m_["aff"], 1)

                def silu(g, b):
                    act.wait_ge(m_["h13"], g + 1)
                    A(moe_hid[b], bank(0), ACT.Silu).then_inc(m_["silu"], 1)

                def hidden_t(g, b):
                    act.wait_ge(m_["hT"], g + 1)
                    A(moe_hidT[b].rearrange("p c n -> p (c n)"), bank(4), ACT.Copy).then_inc(m_["hidT"], 1)

                def result(g, dst):
                    act.wait_ge(m_["y"], g + 1)
                    A(dst, banks(5, 2), ACT.Copy).then_inc(m_["yev"], 1)

                def expert_result(j, first=False):
                    if not first:
                        act.wait_ge(m_["yst"], 16 * j)
                    result(nt + j, moe_y)
                    act.wait_ge(m_["yev"], nt + j + 1)
                    act.dma_start(y_d.rearrange("(t p) d -> p t d", p=P)[:, bass.ds(j, 1), :]
                                  .rearrange("p o d -> p (o d)"), moe_y).then_inc(m_["yst"], 16)

                for t in range(nt):
                    silu(t, t % 2)
                    if t >= 1:
                        result(t - 1, moe_S[:, t - 1, :])
                    hidden_t(t, t % 2)
                silu(nt, 0)
                result(nt - 1, moe_S[:, nt - 1, :])
                hidden_t(nt, 0)
                silu(nt + 1, 1)
                expert_result(0, True)
                hidden_t(nt + 1, 1)
                pairs = looped_pairs(act, l)
                with act.Fori(0, pairs) as i:
                    for u in range(2):
                        silu(2 * i + nt + 2 + u, u)
                        expert_result(2 * i + 1 + u)
                        hidden_t(2 * i + nt + 2 + u, u)
                expert_result(2 * pairs + 1)
                for t in range(nt):
                    act.wait_ge(m_[f"ga{t}"], 32 * l + 32)
                    A(moe_gat[:, t, 0, :], moe_gat[:, t, 0, :], ACT.Copy, scale=gates[:, t:t + 1]
                      ).then_inc(m_["yev"], 1)
                    if l == 0 and t >= 1:
                        square(2, t - 1)
                if l == 0:
                    square(2, nt - 1)

            moe(0)
            root(2, slice(0, TILES), 0)
            for t in range(TILES):
                turned(2, t)
            end_phase(act, 8)

            def latent(n):
                is_q, k = n >= 4, 2 * (n % 2)
                width = Q_LORA if is_q else KV_LORA
                act.wait_ge(S["l_down"], n + 1)
                m = A(mla_sq[:, 0:width], bank(0, width), ACT.Square, accum_out=ssq[:, k:k + 1])
                if not is_q:
                    link(m)
                    m = A(mla_sq[:, 0:ROPE], psum[:, 0, KV_LORA:KV_LORA + ROPE], ACT.Square,
                          accum_out=ssq[:, k + 1:k + 2])
                link(m)
                act.drain().then_inc(S["l_ssq"], 1)
                act.wait_ge(S["l_var"], n + 1)
                A(std[:, 0:1], var[:, 0:1], ACT.Sqrt).then_inc(S["l_std"], 1)

            latent(0)
            latent(1)
            for n in range(6):
                act.wait_ge(S["l_up"], n + 1)
                if n < 4:
                    act.wait_ge(S["l_v"], n + 1)
                for h in range(H):
                    src = psum[:, 2 + h // 2, (h % 2) * QK:(h % 2) * QK + QK] if n >= 4 else \
                        psum[:, 2 + h // 2, (h % 2) * 256:(h % 2) * 256 + NOPE]
                    link(A(mla_sq[:, 0:src.shape[1]], src, ACT.Square, accum_out=hssq[:, h:h + 1]))
                act.drain().then_inc(S["l_hssq"], 1)
                act.wait_ge(S["l_hvar"], n + 1)
                A(hstd, hvar, ACT.Sqrt).then_inc(S["l_hstd"], 1)
                if n + 2 < 6:
                    latent(n + 2)
            end_phase(act, 9)

            dma(o_gate, mod_row(1, 0, GATE1)).then_inc(S["ld_rows2"], 16)
            for u in range(16):
                h, t = u // 2, u % 2
                act.wait_ge(S["a_m"], u + 1)
                A(a_P[:, u % 4, :], bank((0, 1, 6, 7)[u % 4]), ACT.Exp, bias=a_nm[:, u % 4:u % 4 + 1], scale=SM_SCALE,
                  accum_out=a_sum[:, u % 4:u % 4 + 1])
                act.drain().then_inc(S["a_p"], 1)
                if u >= 1:
                    v, hv, tv = u - 1, (u - 1) // 2, (u - 1) % 2
                    act.wait_ge(S["a_pT"], v + 1)
                    if hv >= 2:
                        act.wait_ge(S["a_o"], hv - 1)
                    A(a_PT[:, hv % 2, :, tv * P:(tv + 1) * P], bank(2 + v % 2).rearrange("p (k n) -> p k n", n=P),
                      ACT.Copy).then_inc(S["a_PT"], 1)
            act.wait_ge(S["a_pT"], 16)
            act.wait_ge(S["a_o"], 6)
            A(a_PT[:, 1, :, P:2 * P], bank(3).rearrange("p (k n) -> p k n", n=P), ACT.Copy).then_inc(S["a_PT"], 1)
            end_phase(act, 10)
            load_rows(3)
            load_router(1)
            norm_by_tile(3)
            end_phase(act, 12)
            moe_loads(1)
            moe(1)

        @block.vector
        def _(dve):
            link = Link(dve, S["link_dve"])
            tt, ts, stt, cp = dve.tensor_tensor, dve.tensor_scalar, dve.scalar_tensor_tensor, dve.tensor_copy
            red = dve.tensor_reduce

            dve.wait_ge(S["f_pre"], 1)
            link(cp(hy_par, bank(7, 120)))

            def sine_argument(k):
                if k == 0:
                    dve.wait_ge(S["ld_filt"], 16 * N_FILT)
                dve.wait_ge(S["f_pre"], k + 2)
                if k:
                    dve.wait_ge(S["f_sin"], k)
                link(ts(f_arg[0:HID, :], bank(k, SEQ, HID), f_par[0:HID, k:k + 1], f_par[0:HID, 3:4], ALU.add, ALU.mult))
                link(ts(f_n[0:HID, :], f_arg[0:HID, :], 1.0 / (2.0 * np.pi), ROUND, ALU.mult, ALU.add))
                link(ts(f_n[0:HID, :], f_n[0:HID, :], -ROUND, None, ALU.add))
                link(stt(f_arg[0:HID, :], f_n[0:HID, :], -TWO_PI_HI, f_arg[0:HID, :], ALU.mult, ALU.add))
                link(stt(f_arg[0:HID, :], f_n[0:HID, :], -TWO_PI_LO, f_arg[0:HID, :], ALU.mult, ALU.add))
                ts(f_arg[0:HID, :], f_arg[0:HID, :], 3.1415925, -3.1415925, ALU.min, ALU.max).then_inc(S["f_arg"], 1)

            def taps():
                dve.wait_ge(S["ld_taps"], 32)
                for j in range(8):
                    t, n = j % 2, j // 2
                    dve.wait_ge(S["f_w3"], j + 1)
                    m = tt(f_hfb[:, t, n * 512:(n + 1) * 512], bank(j % 4),
                           f_decay[:, t, (n % 2) * 512:(n % 2) * 512 + 512], ALU.mult)
                    if j < 7:
                        m.then_inc(S["f_h"], 1)
                    else:
                        link(m)
                dve.wait_ge(S["f_h"], 7)
                dve.memset(f_hfb[0:1, 0, D:2 * D], 0.0).then_inc(S["f_h"], 1)

            def even_odd():
                dve.wait_ge(S["f_h"], 8)
                link(tt(f_sd[:, 0], f_hfb[:, :, 0:D], f_hfb[:, :, D:2 * D], ALU.add))
                tt(f_sd[:, 1], f_hfb[:, :, 0:D], f_hfb[:, :, D:2 * D], ALU.subtract).then_inc(S["f_h"], 1)

            def transform():
                dve.wait_ge(S["ld_dft"], 32)
                dve.wait_ge(S["f_w3"], 9)
                link(dve.reciprocal(f_rn, banks(4, 2)))
                for j in range(8):
                    comp, ft, half = j // 4, (j // 2) % 2, j % 2
                    dve.wait_ge(S["f_k"], j + 1)
                    cols = slice(half * 512, half * 512 + 512)
                    tt(f_K[:, 2 * comp + ft, cols], bank(j % 4), f_rn[:, cols], ALU.mult).then_inc(S["f_kdone"], 1)
                    if comp == 0:
                        dve.wait_ge(S["f_kdone"], j + 1)
                        link(tt(f_K[:, ft, cols], f_K[:, ft, cols], f_bias[:, cols], ALU.add))

            def ada_bias(n, b, count):
                dve.wait_ge(S[f"ad_ld{b}"], count)
                dve.wait_ge(S["ad_done"], n + 1)
                dst = mod_first[n] if isinstance(n, int) and n < 4 else mod_piece[b]
                tt(dst, mod_psum[b], dst, ALU.add).then_inc(S["ad_ready"], 1)

            def norm_cols(k):
                norm_var(k)
                norm_scale(k)
                norm_modulate(k)

            def norm_var(k):
                dve.wait_ge(S["n_ssq"], ROOT_BASE[k] + 1)
                ts(var[:, 0:TILES], ssq[:, 0:TILES], 1.0 / D, EPS, ALU.mult, ALU.add).then_inc(S["n_var"], 1)

            def norm_scale(k):
                h = norm_places(k)[3]
                dve.wait_ge(S["n_std"], ROOT_BASE[k] + 1)
                link(dve.reciprocal(rstd[:, 0:TILES], std[:, 0:TILES]))
                for t in range(TILES):
                    g = NORM_BASE[k] + t
                    if t >= 2:
                        dve.wait_ge(S["n_T"], g - 1)
                    ts(h[:, (t % 2) * D:(t % 2 + 1) * D], X[:, t, :], rstd[:, t:t + 1], None, ALU.mult
                       ).then_inc(S["n_h"], 1)

            def norm_modulate(k):
                dve.wait_ge(S["ld_cols"], 80 * (k // 2 + 1))
                link(stt(mod_cols[:, 0], mod_cols[:, 0], 1.0, bc(gain_col, 1, 2), ALU.add, ALU.mult))
                for s in range(2):
                    dve.wait_ge(S["n_hT"], NORM_BASE[k] + LAT_TILES * (s + 1))
                    for c in range(DC):
                        part = hT[:, c, s * SEQ:(s + 1) * SEQ]
                        ts(part, part, mod_cols[:, 0, s, c:c + 1], mod_cols[:, 1, s, c:c + 1], ALU.mult, ALU.add)

            sine_argument(0)
            for n in range(4):
                ada_bias(n, n % 2, 16)
                if n < 2:
                    sine_argument(n + 1)
            norm_var(0)
            taps()
            norm_scale(0)
            even_odd()
            transform()
            norm_modulate(0)
            end_phase(dve, "start")

            def norm_rows(k):
                rows, gain = norm_places(k)[:2]
                dve.wait_ge(S["ld_rows"], {1: 80, 3: 80 + 48}[k])
                for s in range(NORM_TILES[k] // 2):
                    r = rows[:, 2 * s * D:(2 * s + 1) * D]
                    link(stt(r, r, 1.0, gain, ALU.add, ALU.mult))

            def norm_tile(k, t):
                rows, gain, junk, h = norm_places(k)
                g, s, n = NORM_BASE[k] + t, t // 2, ROOT_BASE[k] + t + 1
                hb = h[:, (t % 2) * D:(t % 2 + 1) * D]
                dve.wait_ge(S["n_ssq"], n)
                ts(var[:, t:t + 1], ssq[:, t:t + 1], 1.0 / D, EPS, ALU.mult, ALU.add).then_inc(S["n_var"], 1)
                dve.wait_ge(S["n_std"], n)
                link(dve.reciprocal(rstd[:, t:t + 1], std[:, t:t + 1]))
                if t >= 2:
                    dve.wait_ge(S["n_T"], g - 1)
                    dve.wait_ge(S[f"n_st{t % 2}"], 16)
                link(stt(hb, X[:, t, :], rstd[:, t:t + 1], rows[:, 2 * s * D:(2 * s + 1) * D], ALU.mult, ALU.mult))
                tt(hb, hb, rows[:, (2 * s + 1) * D:(2 * s + 2) * D], ALU.add).then_inc(S["n_h"], 1)

            dve.memset(B(3, 0, 3 * 516), 0.0).then_inc(S["ip_c"], 3)
            dve.sem_inc(S["ip_ve"], 1)
            par = hy_par.rearrange("p (v m) -> p v m", m=8)
            with dve.Fori(0, 4) as i:
                link.enter(i, 2 * (6 + DC - 1))
                for u in range(2):
                    m_ = 2 * i + u
                    cp(pm[u], par[:, :, bass.ds(m_, 1)].rearrange("p v o -> p (v o)")).then_inc(S["ip_pm"], 1)
                    dve.wait_ge(w_loaded[W[f"ada1_{u}"][0]], 16 * (LANDED[f"ada1_{u}"] + 1) + 16 * i)
                    w = piece(f"ada1_{u}").rearrange("p (c n) -> p c n", c=DC)
                    for c in range(DC):
                        for s in range(2):
                            acc = ada_sums[u][:, s, :]
                            m = ts(acc, w[:, c, :], scT[:, c, s:s + 1], None, ALU.mult) if c == 0 else \
                                stt(acc, w[:, c, :], scT[:, c, s:s + 1], acc, ALU.mult, ALU.add)
                        if c < DC - 1:
                            link(m)
                    m.then_inc(S["ip_pm"], 1)
                    dve.wait_ge(S["ip_pm"], 2 * m_ + 2)
                    dve.sem_inc(w_used[W[f"ada1_{u}"][0]], 1)
                    for o, part in enumerate((1, 2, 0)):
                        k = [pm[u][:, (1 + j) * 3 + part:(1 + j) * 3 + part + 1] for j in range(4)]
                        src, tmp = ip_u[:, o], ip_t[:, o]
                        dve.wait_ge(S["ip_u"], 6 + 3 * m_ + o + 1)
                        link(ts(tmp, src[:, :, 1:SEQ + 1], k[1], k[3], ALU.mult, ALU.add))
                        link(stt(tmp, src[:, :, 0:SEQ], k[0], tmp, ALU.mult, ALU.add))
                        dst = tmp if o < 2 else x0T[:, bass.ds(m_, 1), :].rearrange("p o (s t) -> p (o s) t", s=2)
                        stt(dst, src[:, :, 2:SEQ + 2], k[2], tmp, ALU.mult, ALU.add).then_inc(S["ip_c"], 1)
                        if o == 1:
                            dve.wait_ge(S["ip_c"], 3 + 3 * m_ + 2)
                            tt(ip_vgb.rearrange("p (s t) -> p s t", s=2), ip_t[:, 0], ip_t[:, 1], ALU.mult
                               ).then_inc(S["ip_vg"], 1)
                    ada_bias(4 * i + 2 * u + 4, 0, 32 * i + 16 * u + 32)
                    dve.wait_ge(S["ip_vt"], m_ + 1)
                    ts(vgtok[:, :, bass.ds(m_ * P, P)], bank(7).rearrange("p (t n) -> p t n", n=P), 1.0, None, ALU.mult
                       ).then_inc(S["ip_ve"], 1)
                    ada_bias(4 * i + 2 * u + 5, 1, 32 * i + 16 * u + 32)
                link.leave(4)
            end_phase(dve, 3)

            def back(k, quarters):
                s, half = k % 2, k // 2
                for m4 in quarters:
                    dve.wait_ge(S["cv_inv"], 4 * k + m4 + 1)
                    dst = x0T[:, 4 * half + m4, s * SEQ:(s + 1) * SEQ]
                    tt(dst, bank(4 + m4 % 2, SEQ), dst, ALU.mult).then_inc(S["cv_yt"], 1)

            for k in range(4):
                half = k // 2
                cols = slice(half * 512, half * 512 + 512)
                dve.wait_ge(S["cv_x"], k + 1)
                if k >= 1:
                    dve.wait_ge(S["cv_y"], k)
                if k >= 2:
                    dve.wait_ge(S["cv_inv"], 4 * (k - 1))
                Y = cv_Y[:, k % 2]
                for f in range(2):
                    Kr, Ki, t0, t1 = f_K[:, f, cols], f_K[:, 2 + f, cols], cv_t[:, 0], cv_t[:, 1]
                    tt(Y[:, f], bank(f), Kr, ALU.mult)
                    tt(t0, bank(2 + f), Ki, ALU.mult)
                    tt(Y[:, 2 + f], bank(f), Ki, ALU.mult)
                    link(tt(t1, bank(2 + f), Kr, ALU.mult))
                    if f == 1:
                        dve.sem_inc(S["cv_xfree"], 1)
                    tt(Y[:, f], Y[:, f], t0, ALU.subtract)
                    m = tt(Y[:, 2 + f], Y[:, 2 + f], t1, ALU.add)
                    if f == 0:
                        link(m)
                m.then_inc(S["cv_y"], 1)
                if k >= 1:
                    back(k - 1, (0, 1))
                ada_bias(20 + k, k % 2, 16 * (10 + k // 2))
                if k >= 1:
                    back(k - 1, (2, 3))
            back(3, range(4))
            end_phase(dve, 4)

            dve.wait_ge(S["ld_rows2"], 48)
            for t in range(TILES):
                for n in range(2):
                    j = 2 * t + n
                    cols = slice(n * 512, n * 512 + 512)
                    dve.wait_ge(S["op_y"], j + 1)
                    tmp = op_t[:, j % 2]
                    tt(tmp, bank(j % 4), op_rows[:, 0, cols], ALU.add).then_inc(S["op_x"], 1)
                    dve.wait_ge(S["op_x"], j + 1)
                    link(tt(tmp, tmp, op_rows[:, 1 + t // 2, cols], ALU.mult))
                    m = tt(X[:, t, cols], X[:, t, cols], tmp, ALU.add)
                m.then_inc(S["x_done"], 1)
                if t == 0:
                    norm_rows(1)
                norm_tile(1, t)
            end_phase(dve, 6)

            def moe(l):
                m_, nt, nx = M[l], TOKEN_TILES[l], EXPERT_TILES[l]
                nte = nt * E
                dve.wait_ge(S["ld_lat"], 96)
                v3 = lambda ap: ap.rearrange("p (t e) -> p t e", e=E)
                aff, sb_, w0, w1 = moe_aff[:, 0:nte], moe_r[0][:, 0:nte], moe_r[1][:, 0:nte], moe_r[2][:, 0:nte]
                pair, gs, g1, g2 = moe_pair[:, 0:nt * G, :], moe_g4[0][:, 0:nt * G], moe_g4[1][:, 0:nt * G], moe_g4[2][:, 0:nt]

                dve.wait_ge(m_["aff"], l + 1)
                link(tt(v3(sb_), v3(aff), bc(router_b, 1, nt), ALU.add))
                q = sb_.rearrange("p (g e) -> p g e", e=PER_G)
                tt(pair[:, :, 0:3], q[:, :, 0:3], q[:, :, 1:4], ALU.add)
                tt(pair[:, :, 3:5], q[:, :, 0:2], q[:, :, 2:4], ALU.add)
                link(tt(pair[:, :, 5:6], q[:, :, 0:1], q[:, :, 3:4], ALU.add))
                link(red(gs, pair, AX.X, ALU.max))
                gs3, g13 = (x.rearrange("p (t g) -> p t g", g=G) for x in (gs, g1))

                def first_max(dst3, val3, best, desc, n):
                    link(red(best, val3, AX.X, ALU.max))
                    link(tt(dst3, val3, bc(best, 2, n), ALU.is_equal))
                    link(tt(dst3, dst3, bc(desc, 1, nt), ALU.mult))
                    link(red(best, dst3, AX.X, ALU.max))
                    link(tt(dst3, dst3, bc(best, 2, n), ALU.is_equal))

                first_max(g13, gs3, g2, C(C_DESC4, G), G)
                gm = bc(g1, 2, PER_G)
                qw = w0.rearrange("p (g e) -> p g e", e=PER_G)
                link(tt(qw, q, gm, ALU.mult))
                link(ts(g1, g1, -1.0, BIG, ALU.add, ALU.mult))
                link(tt(qw, qw, gm, ALU.add))
                best = moe_g4[2][:, 0:nt]
                desc = C(C_DESC, E)
                sa, sb2 = sel_a[:, 0:nte], sel_b[:, 0:nte]
                first_max(v3(sa), v3(w0), best, desc, E)
                link(stt(w0, sa, -2.0 * BIG, w0, ALU.mult, ALU.add))
                first_max(v3(sb2), v3(w0), best, desc, E)
                tt(moe_sel[:, 0:nt, :].rearrange("p t e -> p (t e)"), sa, sb2, ALU.add).then_inc(m_["sel"], 1)
                for k, s_ in enumerate((sa, sb2)):
                    link(tt(w1, s_, aff, ALU.mult))
                    link(red(gates[:, k * TILES:k * TILES + nt], v3(w1), AX.X, ALU.add))
                link(tt(best, gates[:, 0:nt], gates[:, TILES:TILES + nt], ALU.add))
                link(dve.reciprocal(best, best))
                for k in range(2):
                    gk = gates[:, k * TILES:k * TILES + nt]
                    link(tt(gk, gk, best, ALU.mult))

                def hidden(g, b):
                    dve.wait_ge(m_["silu"], g + 1)
                    tt(moe_hid[b], moe_hid[b], bank(1), ALU.mult).then_inc(m_["hid"], 1)

                def tokens_t(j, b):
                    dve.wait_ge(m_["xT"], j + 1)
                    cp(moe_xT[b].rearrange("p c n -> p (c n)"), banks(2, 2)).then_inc(m_["xTe"], 1)

                hidden(0, 0)

                dve.wait_ge(m_["routing"], 3 * l + 2)
                cnt = bank(7)[:, 64 + nt * E:64 + (nt + 1) * E]
                link(ts(cnt16, cnt, 0.0, None, ALU.is_gt))
                for k in range(1, nt):
                    link(stt(cnt16, cnt, float(k * P), cnt16, ALU.is_gt, ALU.add))
                link(dve.memset(scan[0], 0.0))
                link(dve.memset(scan[1], 0.0))
                link(cp(scan[0][:, E:2 * E], cnt16))
                src = 0
                for d in (1, 2, 4, 8):
                    link(tt(scan[1 - src][:, E:2 * E], scan[src][:, E:2 * E], scan[src][:, E - d:2 * E - d], ALU.add))
                    src = 1 - src
                first = scan[src][:, E - 1:2 * E - 1]
                link(tt(moe_cmp[:, 0:nx * E].rearrange("p (t e) -> p t e", e=E), bc(C(C_TILE, nx), 2, E),
                        bc(first, 1, nx), ALU.is_ge))
                link(red(moe_r[2][:, 0:nx], moe_cmp[:, 0:nx * E].rearrange("p (t e) -> p t e", e=E), AX.X, ALU.add))
                ts(eid_i[:, 0:nx], moe_r[2][:, 0:nx], -1.0, None, ALU.add)
                ts(pairs_i, scan[src][:, 2 * E - 1:2 * E], 0.5, -0.75, ALU.mult, ALU.add).then_inc(m_["eid"], 1)
                link(stt(v3(w0), bc(first, 1, nt), float(P), v3(bank(7)[:, 64:64 + nte]), ALU.mult, ALU.add))
                for k, s_ in enumerate((sa, sb2)):
                    link(tt(w1, s_, w0, ALU.mult))
                    link(red(moe_slot[:, k * nt:(k + 1) * nt], v3(w1), AX.X, ALU.add))
                sl = moe_slot[:, 0:2 * nt]
                cp(slot_i[:, 0:2 * nt], sl)
                ge = moe_cmp[:, 0:2 * nt * (nx + 1)].rearrange("p (q t) -> p q t", t=nx + 1)
                link(tt(ge, bc(sl, 2, nx + 1), bc(C(C_GRID, nx + 1), 1, 2 * nt), ALU.is_ge))
                hi = moe_slot[:, 2 * nt:4 * nt]
                link(red(hi, ge, AX.X, ALU.add))
                link(stt(sl, hi, float(-P), sl, ALU.mult, ALU.add))
                link(ts(sl, sl, float(P), None, ALU.add))
                link(tt(moe_hot[:, 0:2 * nt, :], bc(C(C_IOTA, P), 1, 2 * nt), bc(sl, 2, P), ALU.is_equal))
                hit = moe_hit[:, 0:2 * nt, 0:nx]
                link(tt(hit, ge[:, :, 0:nx], ge[:, :, 1:nx + 1], ALU.subtract))
                for k in range(2):
                    h_ = moe_hit[:, k * nt:(k + 1) * nt, 0:nx]
                    m = tt(h_, h_, bc(C(C_TOK, nt), 2, nx), ALU.mult)
                m.then_inc(m_["hot"], 1)

                hidden(1, 1)
                dve.wait_ge(m_["routing"], 3 * l + 3)
                dve.memset(idx_i[:, nx:nx + 1], 0)
                cp(idx_i[:, 0:nx], bank(7)[:, 192:192 + nx]).then_inc(m_["idx"], 1)
                for t in range(2, nt):
                    hidden(t, t % 2)
                tokens_t(0, 0)
                hidden(nt, 0)
                tokens_t(1, 1)
                hidden(nt + 1, 1)
                tokens_t(2, 0)
                dve.wait_ge(m_["yev"], nt)
                dve.wait_ge(m_["ld"], 32 + 16 * l)
                for t in range(nt):
                    st = moe_S[:, t, :]
                    link(tt(st, st, moe_g2[:, t // 2, :], ALU.mult))
                    link(tt(X[:, t, :], X[:, t, :], st, ALU.add))
                pairs = looped_pairs(dve, l)
                with dve.Fori(0, pairs) as i:
                    for u in range(2):
                        hidden(2 * i + nt + 2 + u, u)
                        tokens_t(2 * i + 3 + u, 1 - u)

                for t in range(nt):
                    dve.wait_ge(m_[f"ga{t}"], 32 * l + 32)
                    ya, yb = (moe_gat[:, t, k, :] for k in range(2))
                    dve.wait_ge(m_["yev"], 2 * pairs + nt + 3 + t)
                    link(stt(yb, yb, gates[:, TILES + t:TILES + t + 1], ya, ALU.mult, ALU.add))
                    link(tt(yb, yb, moe_g2[:, t // 2, :], ALU.mult))
                    tt(X[:, t, :], X[:, t, :], yb, ALU.add).then_inc(m_["comb"], 1)

            moe(0)
            norm_cols(2)
            end_phase(dve, 8)

            dve.wait_ge(S["ld_rows2"], 80)
            up4 = psum[:, 2:6, :].rearrange("p b (h d) -> p (b h) d", d=256)

            def latent(n):
                is_q, k = n >= 4, 2 * (n % 2)
                width = Q_LORA if is_q else KV_LORA
                dve.wait_ge(S["l_ssq"], n + 1)
                ts(var[:, 0:1], ssq[:, k:k + 1], 1.0 / width, EPS, ALU.mult, ALU.add).then_inc(S["l_var"], 1)
                dve.wait_ge(S["l_std"], n + 1)
                link(dve.reciprocal(rstd[:, 0:1], std[:, 0:1]))
                if not is_q:
                    link(cp(mla_pe[n % 2], psum[:, 0, KV_LORA:KV_LORA + ROPE]))
                if n:
                    dve.wait_ge(S["l_T"], n)
                ts(mla_lat[:, 0:width], bank(0, width), rstd[:, 0:1], None, ALU.mult).then_inc(S["l_lat"], 1)

            def latent_turned(n):
                is_q, chunks = n >= 4, 3 if n >= 4 else 2
                dve.wait_ge(S["l_T"], n + 1)
                if n:
                    dve.wait_ge(S["l_up"], n)
                for c in range(chunks):
                    g = (0 if is_q else 3) + c
                    m = ts(mla_latT[:, c, :], bank(1)[:, c * P:(c + 1) * P], lat_g[:, g:g + 1], None, ALU.mult)
                m.then_inc(S["l_TT"], 1)

            def values_out(n):
                dve.wait_ge(S["l_up"], n + 1)
                cp(a_V[:, n, :].rearrange("p (h d) -> p h d", d=VD), up4[:, :, NOPE:256]).then_inc(S["l_v"], 1)

            def heads_out(n):
                dve.wait_ge(S["l_HT"], n + 1)
                nope, rope = (qTn, qTr) if n >= 4 else (kTn, kTr)
                cols = slice((n % 4) * P, (n % 4 + 1) * P)
                cp(nope[:, :, cols], banks(6, 2).rearrange("p (h n) -> p h n", n=P))
                cp(rope[:, :, cols], bank(1).rearrange("p (h n) -> p h n", n=P)).then_inc(S["l_hevac"], 1)

            latent(0)
            latent_turned(0)
            latent(1)
            for n in range(6):
                is_q, tile = n >= 4, n % 4
                if not is_q:
                    values_out(n)
                dve.wait_ge(S["l_hssq"], n + 1)
                if is_q:
                    ts(hvar, hssq, 1.0 / QK, EPS, ALU.mult, ALU.add).then_inc(S["l_hvar"], 1)
                else:
                    link(ts(hssq, hssq, ssq[:, 2 * (n % 2) + 1:2 * (n % 2) + 2], 1.0 / QK, ALU.add, ALU.mult))
                    ts(hvar, hssq, EPS, None, ALU.add).then_inc(S["l_hvar"], 1)
                dve.wait_ge(S["l_hstd"], n + 1)
                link(dve.reciprocal(hrstd, hstd))
                if n:
                    dve.wait_ge(S["l_HT"], n)
                if is_q:
                    for b in range(4):
                        src = psum[:, 2 + b, 0:384].rearrange("p (h d) -> p h d", d=QK)
                        pair_r = hrstd[:, 2 * b:2 * b + 2]
                        tt(mla_hn[:, 2 * b:2 * b + 2, :], src[:, :, 0:NOPE], bc(pair_r, 2, NOPE), ALU.mult)
                        m = tt(mla_hr[:, 2 * b:2 * b + 2, :], src[:, :, NOPE:QK], bc(pair_r, 2, ROPE), ALU.mult)
                else:
                    tt(mla_hr, bc(mla_pe[n % 2], 1, H), bc(hrstd, 2, ROPE), ALU.mult)
                    m = tt(mla_hn, up4[:, :, 0:NOPE], bc(hrstd, 2, NOPE), ALU.mult)
                m.then_inc(S["l_hn"], 1)
                if n:
                    heads_out(n - 1)
                if n + 1 < 6:
                    latent_turned(n + 1)
                if n + 2 < 6:
                    latent(n + 2)
                dve.wait_ge(S["l_hn"], n + 1)
                gain = mla_g[:, 0:QK] if is_q else mla_g[:, QK:2 * QK]
                link(tt(mla_hn, mla_hn, bc(gain[:, 0:NOPE], 1, H), ALU.mult))
                m = tt(mla_hr, mla_hr, bc(gain[:, NOPE:QK], 1, H), ALU.mult)
                if is_q or n < LAT_TILES:
                    link(m)
                    t0 = C_ROPE + 64 * tile
                    cos = bc(C(t0, 32).rearrange("p (a k) -> p a k", a=2), 1, H)
                    sin = bc(C(t0 + 32, 32).rearrange("p (a k) -> p a k", a=2), 1, H)
                    r = mla_hr.rearrange("p h (a b k) -> p h a b k", a=2, b=2)
                    t4 = [mla_t[:, k * 256:(k + 1) * 256].rearrange("p (h a k) -> p h a k", h=H, a=2) for k in range(4)]
                    x1, x2 = r[:, :, :, 0, :], r[:, :, :, 1, :]
                    tt(t4[0], x1, cos, ALU.mult)
                    tt(t4[1], x2, sin, ALU.mult)
                    tt(t4[2], x2, cos, ALU.mult)
                    link(tt(t4[3], x1, sin, ALU.mult))
                    tt(x1, t4[0], t4[1], ALU.subtract)
                    tt(x2, t4[2], t4[3], ALU.add).then_inc(S["l_hr"], 1)
                else:
                    m.then_inc(S["l_hr"], 1)
            heads_out(5)
            end_phase(dve, 9)

            def head_out(h):
                dve.wait_ge(S["a_o"], h + 1)
                cp(OT[:, h, :], bank(4 + h % 2, SEQ)).then_inc(S["a_ot"], 1)

            def probs(u):
                dve.wait_ge(S["a_p"], u + 1)
                s = a_sum[:, u % 4:u % 4 + 1]
                link(dve.reciprocal(s, s))
                ts(a_P[:, u % 4, :], a_P[:, u % 4, :], s, None, ALU.mult).then_inc(S["a_pn"], 1)

            for u in range(16):
                dve.wait_ge(S["a_s"], u + 1)
                if u >= 4:
                    dve.wait_ge(S["a_p"], u - 3)
                nm = a_nm[:, u % 4:u % 4 + 1]
                link(red(nm, bank((0, 1, 6, 7)[u % 4]), AX.X, ALU.max))
                ts(nm, nm, -SM_SCALE, None, ALU.mult).then_inc(S["a_m"], 1)
                if u >= 1:
                    probs(u - 1)
                if u >= 4 and u % 2 == 0:
                    head_out(u // 2 - 2)
            probs(15)
            head_out(6)
            head_out(7)
            end_phase(dve, 10)
            dve.wait_ge(S["ld_rows2"], 96)
            for t in range(LAT_TILES):
                for n in range(2):
                    j = 2 * t + n
                    cols = slice(n * 512, n * 512 + 512)
                    dve.wait_ge(S["op_y"], 2 * TILES + j + 1)
                    tmp = o_t[:, j % 2]
                    tt(tmp, bank(j), o_gate[:, cols], ALU.mult).then_inc(S["op_x"], 1)
                    dve.wait_ge(S["op_x"], 2 * TILES + j + 1)
                    m = tt(X[:, t, cols], X[:, t, cols], tmp, ALU.add)
                m.then_inc(S["x_done"], 1)
                if t == 0:
                    norm_rows(3)
                norm_tile(3, t)
            end_phase(dve, 12)
            moe(1)

        @block.gpsimd
        def _(pool):
            def moe(l):
                m_, nt, nx = M[l], TOKEN_TILES[l], EXPERT_TILES[l]
                pool.wait_ge(m_["idx"], l + 1)
                for b in range(2):
                    pool.wait_ge(S[f"n_st{b}"], 32 + 16 * l)

                def gather(j, b):
                    nc.gpsimd.tensor_copy(idx_cur[:, b:b + 1], idx_i[:, bass.ds(j, 1)]).then_inc(m_["cur"], 1)
                    pool.wait_ge(m_["cur"], j + 1)
                    pool.sem_inc(S["ordered"], 1)
                    nc.gpsimd.indirect_dma_start(
                        moe_xg[b], None, h2_d[l][:, :],
                        bass.IndirectOffsetOnAxis(ap=idx_cur[:, b:b + 1], axis=0)).then_inc(m_[f"xg{b}"], 16)

                gather(0, 0)
                gather(1, 1)
                pool.wait_ge(m_["xT"], 1)
                gather(2, 0)
                pairs = looped_pairs(pool, l)
                with pool.Fori(0, pairs) as i:
                    for u in range(2):
                        pool.wait_ge(m_["xT"], 2 * i + 2 + u)
                        gather(2 * i + 3 + u, 1 - u)
                pool.wait_ge(m_["yst"], 32 * pairs + 32)
                pool.sem_inc(S["ordered"], 1)
                for t in range(nt):
                    for k in range(2):
                        nc.gpsimd.indirect_dma_start(
                            moe_gat[:, t, k, :], None, y_d[:, :],
                            bass.IndirectOffsetOnAxis(ap=slot_i[:, k * nt + t:k * nt + t + 1], axis=0)
                        ).then_inc(m_[f"ga{t}"], 16)

            flat_bias = a["ada_b"].rearrange("l n -> (l n)")

            def bias_piece(q, b):
                pool.dma_start(mod_piece[b], flat_bias[bass.ds(q * 512, 512)].rearrange("(o n) -> o n", o=1)
                               .partition_broadcast(2)).then_inc(S[f"ad_ld{b}"], 16)

            def store_piece(n, l, q, b, count, then=None):
                pool.wait_ge(S["ad_ready"], n + 1)
                pool.sem_inc(S["ordered"], 1)
                pool.dma_start(mod_d[l, :, bass.ds(q * 512, 512)], mod_piece[b]).then_inc(S[f"ad_st{b}"], 16)
                if then is not None:
                    pool.wait_ge(S[f"ad_st{b}"], count)
                    pool.sem_inc(S["ordered"], 1)
                    bias_piece(then, b)

            for b in range(2):
                pool.dma_start(slot(4)[32 * b:32 * b + 2, 3072:4096].rearrange("p (k n) -> p k n", k=2),
                               flat_bias[0:2 * D].rearrange("(k two n) -> two k n", two=2, n=512)[b]
                               .partition_broadcast(2)).then_inc(S[f"ad_ld{b}"], 16)
            for n in range(4):
                pool.wait_ge(S["ad_ready"], n + 1)
                pool.dma_start(mod_d[0, :, n * 512:(n + 1) * 512], mod_first[n]).then_inc(S[f"ad_st{n % 2}"], 16)
                if n < 2:
                    bias_piece((4, 13)[n], n)
            with pool.Fori(0, 4) as i:
                for u in range(2):
                    n, count = 4 * i + 2 * u + 4, 32 * i + 16 * u + 48
                    store_piece(n, 0, 2 * i + u + 4, 0, count, 2 * i + u + 5)
                    store_piece(n + 1, 1, 2 * i + u + 1, 1, count, 2 * i + u + 14)
            store_piece(20, 1, 0, 0, 16 * 11, 22)
            store_piece(21, 1, 9, 1, 16 * 11, 23)
            store_piece(22, 1, 10, 0, 16 * 12)
            store_piece(23, 1, 11, 1, 16 * 12)
            pool.wait_ge(S["op_y"], 1)
            first_unsure = TOKEN_TILES[0] * TOP_K
            pool.dma_start(y_d[first_unsure * P:, :].rearrange("(t p) d -> p t d", p=P),
                           bc(dft_t[:, 0:D], 1, T_MAX - first_unsure)).then_inc(S["pool_st"], 16)
            moe(0)
            moe(1)
            pool.wait_ge(M[1]["comb"], TILES + LAT_TILES)
            pool.dma_start(out[0].rearrange("(t p) d -> p t d", p=P), X[:, 0:LAT_TILES, :]).then_inc(S["pool_st"], 16)
            pool.wait_ge(S["pool_st"], 32)


INPUTS = ["x", "c", "ctx", "c_ctx", "ada_w", "ada_b", "norm_mix_g", "norm_ffn_g", "hy_in_w", "hy_in_b", "hy_conv_w",
          "hy_conv_b", "hy_f_w1", "hy_f_b1", "hy_f_w2", "hy_f_b2", "hy_f_w3", "hy_sin_freq", "hy_f_bias", "hy_out_w",
          "hy_out_b", "mla_wq_down", "mla_q_norm_g", "mla_wq_up", "mla_wkv_down", "mla_kv_norm_g", "mla_wkv_up",
          "mla_q_head_g", "mla_k_head_g", "mla_wo", "router_w", "router_bias", "exp_w1", "exp_w3", "exp_w2", "sh_w1",
          "sh_w3", "sh_w2"]


def kernel(**inputs):
    import concourse.bacc as bacc
    from concourse.bass_utils import run_bass_kernel_spmd as run

    nc = bacc.Bacc("TRN2", target_bir_lowering=False, num_devices=1)
    arrays = {f"in_{n}": np.ascontiguousarray(inputs[n]) for n in INPUTS}
    arrays.update(shape_constants())
    aps = {n.removeprefix("in_"): nc.dram_tensor(n, v.shape, F32, kind="ExternalInput").ap() for n, v in arrays.items()}
    out = nc.dram_tensor("out", [1, SEQ, D], F32, kind="ExternalOutput").ap()
    build(nc, aps, out)
    return run(nc, [arrays], core_ids=[0]).results[0]["out"]
```
